# Optimizing a Trainium2 kernel written in Bass

```python
import math
import jax, jax.numpy as jnp
from jax import lax
import numpy as np

D_MODEL = 1024
BATCH = 1
SEQ = 2048
DEPTH = 1

CTX_LEN = 256
GRID_W = 64
D_INNER = 2 * D_MODEL
ATTN_WIDTH = D_INNER // 2
SSD_WIDTH = D_INNER - ATTN_WIDTH
HEAD_DIM = 64
N_Q_HEADS = ATTN_WIDTH // HEAD_DIM
N_KV_HEADS = 4
Q_PER_KV = N_Q_HEADS // N_KV_HEADS
KV_WIDTH = N_KV_HEADS * HEAD_DIM
SSD_HEAD_DIM = 64
SSD_HEADS = SSD_WIDTH // SSD_HEAD_DIM
SSD_GROUPS = 2
SSD_HEADS_PER_GROUP = SSD_HEADS // SSD_GROUPS
D_STATE = 128
GN = SSD_GROUPS * D_STATE
D_CONV = 5
CHUNK = 128
Q_BLOCK = 128
ROPE_THETA = 10000.0
ATTN_SCALE = HEAD_DIM ** -0.5
EPS = 1e-6
CONV_CH = SSD_WIDTH + 2 * GN
OFF_V = KV_WIDTH
OFF_XBC = 2 * KV_WIDTH
OFF_DT = OFF_XBC + CONV_CH
CTX_COLS = OFF_DT + 2 * SSD_HEADS
PROJ_COLS = CTX_COLS + 2 * ATTN_WIDTH + SSD_WIDTH

kernel_name = "hymba_ssd_gqa_axial_dit_layer"

def rms_norm(x, g):
    xf = x.astype(jnp.float32)
    y = xf * lax.rsqrt(jnp.mean(xf * xf, axis=-1, keepdims=True) + EPS)
    return (y * g.astype(jnp.float32)).astype(x.dtype)

def axial_rope(x):
    L = x.shape[1]
    rows = L // GRID_W
    row, col = jnp.meshgrid(jnp.arange(rows, dtype=jnp.float32),
                            jnp.arange(GRID_W, dtype=jnp.float32), indexing="ij")
    n_freq = HEAD_DIM // 4
    inv_freq = ROPE_THETA ** (-jnp.arange(n_freq, dtype=jnp.float32) / n_freq)
    ang = jnp.stack([row.reshape(-1)[:, None] * inv_freq,
                     col.reshape(-1)[:, None] * inv_freq], axis=1)
    cos = jnp.cos(ang)[:, None].astype(x.dtype)
    sin = jnp.sin(ang)[:, None].astype(x.dtype)
    xr = x.reshape(*x.shape[:3], 2, 2, n_freq)
    x1, x2 = xr[..., 0, :], xr[..., 1, :]
    out = jnp.stack([x1 * cos - x2 * sin, x2 * cos + x1 * sin], axis=-2)
    return out.reshape(x.shape)

def dwconv_centred(u, w, b):
    pad = D_CONV // 2
    y = lax.conv_general_dilated(u, w[:, None, :].astype(u.dtype), window_strides=(1,),
                                 padding=[(pad, pad)], dimension_numbers=("NWC", "WIO", "NWC"),
                                 feature_group_count=u.shape[-1])
    return y + b

def ssd_inputs(xbc_raw, dt_raw, conv_w, conv_b, dt_bias):
    bsz, L = xbc_raw.shape[:2]
    xbc = jax.nn.silu(dwconv_centred(xbc_raw, conv_w, conv_b))
    xs = xbc[..., :SSD_WIDTH].reshape(bsz, L, SSD_HEADS, SSD_HEAD_DIM)
    bm = xbc[..., SSD_WIDTH:SSD_WIDTH + GN].reshape(bsz, L, SSD_GROUPS, D_STATE)
    cm = xbc[..., SSD_WIDTH + GN:].reshape(bsz, L, SSD_GROUPS, D_STATE)
    dt = jax.nn.softplus(dt_raw.reshape(bsz, L, 2, SSD_HEADS).astype(jnp.float32) + dt_bias)
    return xs, bm, cm, dt

def ssd_scan(xs, dt, a_neg, b_in, c_in, init_state, want_y):
    bsz, L = xs.shape[:2]
    nc = L // CHUNK
    X = (xs * dt[..., None]).reshape(bsz, nc, CHUNK, SSD_GROUPS, SSD_HEADS_PER_GROUP, SSD_HEAD_DIM)
    a = (dt * a_neg).reshape(bsz, nc, CHUNK, SSD_GROUPS, SSD_HEADS_PER_GROUP)
    a_cs = jnp.cumsum(jnp.transpose(a, (0, 3, 4, 1, 2)), axis=-1)
    bc = b_in.reshape(bsz, nc, CHUNK, SSD_GROUPS, D_STATE)
    cc = c_in.reshape(bsz, nc, CHUNK, SSD_GROUPS, D_STATE)
    decay_to_end = jnp.exp(a_cs[..., -1:] - a_cs)
    chunk_states = jnp.einsum("bcsgn,bgrcs,bcsgrp->bcgrpn", bc, decay_to_end, X)
    chunk_decay = jnp.exp(a_cs[..., -1])

    def step(state, inp):
        st, dec = inp
        return state * dec[..., None, None] + st, state

    final, entering = lax.scan(step, init_state.astype(chunk_states.dtype),
                               (jnp.moveaxis(chunk_states, 1, 0), jnp.moveaxis(chunk_decay, -1, 0)))
    if not want_y:
        return None, final
    entering = jnp.moveaxis(entering, 0, 1)
    tril = jnp.tril(jnp.ones((CHUNK, CHUNK), dtype=bool))
    seg = a_cs[..., :, None] - a_cs[..., None, :]
    lmat = jnp.exp(jnp.where(tril, seg, -jnp.inf))
    cb = jnp.einsum("bclgn,bcsgn->bgcls", cc, bc)
    y_diag = jnp.einsum("bgrcls,bcsgrp->bclgrp", cb[:, :, None] * lmat, X)
    y_off = jnp.einsum("bclgn,bgrcl,bcgrpn->bclgrp", cc, jnp.exp(a_cs), entering)
    y = (y_diag + y_off).reshape(bsz, L, SSD_HEADS, SSD_HEAD_DIM)
    return y, final

def bidir_ssd(ssd_c, ssd_l, a_neg, want_ctx_y):
    xs_c, b_c, c_c, dt_c = ssd_c
    xs_l, b_l, c_l, dt_l = ssd_l
    bsz = xs_l.shape[0]
    zero = jnp.zeros((bsz, SSD_GROUPS, SSD_HEADS_PER_GROUP, SSD_HEAD_DIM, D_STATE), jnp.float32)
    y_l = 0.0
    y_c = 0.0 if want_ctx_y else None
    for d in range(2):
        fl = (lambda t: jnp.flip(t, axis=1)) if d == 1 else (lambda t: t)
        yc, s_ctx = ssd_scan(fl(xs_c), fl(dt_c[:, :, d]), a_neg[d], fl(b_c), fl(c_c), zero, want_ctx_y)
        yl, _ = ssd_scan(fl(xs_l), fl(dt_l[:, :, d]), a_neg[d], fl(b_l), fl(c_l), s_ctx, True)
        y_l = y_l + fl(yl)
        if want_ctx_y:
            y_c = y_c + fl(yc)
    return y_l, y_c

def gqa_dense(q, k, v):
    bsz, lq = q.shape[:2]
    qg = q.reshape(bsz, lq, N_KV_HEADS, Q_PER_KV, HEAD_DIM)
    s = jnp.einsum("bqkrd,bskd->bkrqs", qg, k, preferred_element_type=jnp.float32) * ATTN_SCALE
    p = jax.nn.softmax(s, axis=-1).astype(v.dtype)
    o = jnp.einsum("bkrqs,bskd->bqkrd", p, v)
    return o.reshape(bsz, lq, ATTN_WIDTH)

def blocked_attention(q, k, v):
    bsz, L = q.shape[:2]
    nb = L // Q_BLOCK
    qb = jnp.moveaxis(q.reshape(bsz, nb, Q_BLOCK, N_Q_HEADS, HEAD_DIM), 1, 0)
    o = lax.map(lambda qi: gqa_dense(qi, k, v), qb)
    return jnp.moveaxis(o, 0, 1).reshape(bsz, L, ATTN_WIDTH)

def split_ctx_cols(p):
    k = p[..., :OFF_V]
    v = p[..., OFF_V:OFF_XBC]
    xbc = p[..., OFF_XBC:OFF_DT]
    dt = p[..., OFF_DT:CTX_COLS]
    return k, v, xbc, dt

def split_query_cols(p):
    q = p[..., CTX_COLS:CTX_COLS + ATTN_WIDTH]
    g_attn = p[..., CTX_COLS + ATTN_WIDTH:CTX_COLS + 2 * ATTN_WIDTH]
    z = p[..., CTX_COLS + 2 * ATTN_WIDTH:]
    return q, g_attn, z

def merge_heads(o_attn, g_attn, y_ssd, z, ssd_norm_g, w_out):
    y_a = o_attn * jax.nn.silu(g_attn)
    y_s = rms_norm(y_ssd * jax.nn.silu(z), ssd_norm_g)
    return jnp.concatenate([y_a, y_s], axis=-1) @ w_out

def hybrid_layer(x_lat, x_ctx, c, c_ctx, ada_w, ada_b, norm_g, w_in, conv_w, conv_b, dt_bias,
                 a_log, d_skip, q_norm_g, k_norm_g, ssd_norm_g, w_out, ctx_out):
    bsz, L = x_lat.shape[:2]
    lc = x_ctx.shape[1]
    mod_l = jax.nn.silu(c) @ ada_w + ada_b
    mod_c = jax.nn.silu(c_ctx) @ ada_w + ada_b
    sh_l, sc_l, g_l = jnp.split(mod_l[:, None, :], 3, axis=-1)
    sh_c, sc_c, g_c = jnp.split(mod_c, 3, axis=-1)
    h_l = rms_norm(x_lat, norm_g) * (1 + sc_l) + sh_l
    h_c = rms_norm(x_ctx, norm_g) * (1 + sc_c) + sh_c
    p_l = h_l @ w_in
    p_c = h_c @ (w_in if ctx_out else w_in[:, :CTX_COLS])
    k_l, v_l, xbc_l, dt_l = split_ctx_cols(p_l)
    k_c, v_c, xbc_c, dt_c = split_ctx_cols(p_c)
    q_l, ga_l, z_l = split_query_cols(p_l)

    k_l = axial_rope(rms_norm(k_l.reshape(bsz, L, N_KV_HEADS, HEAD_DIM), k_norm_g))
    k_c = rms_norm(k_c.reshape(bsz, lc, N_KV_HEADS, HEAD_DIM), k_norm_g)
    v_l = v_l.reshape(bsz, L, N_KV_HEADS, HEAD_DIM)
    v_c = v_c.reshape(bsz, lc, N_KV_HEADS, HEAD_DIM)
    q_l = axial_rope(rms_norm(q_l.reshape(bsz, L, N_Q_HEADS, HEAD_DIM), q_norm_g))
    o_l = blocked_attention(q_l, jnp.concatenate([k_l, k_c], axis=1), jnp.concatenate([v_l, v_c], axis=1))

    ssd_c = ssd_inputs(xbc_c, dt_c, conv_w, conv_b, dt_bias)
    ssd_l = ssd_inputs(xbc_l, dt_l, conv_w, conv_b, dt_bias)
    a_neg = -jnp.exp(a_log.astype(jnp.float32))
    y_l, y_c = bidir_ssd(ssd_c, ssd_l, a_neg, ctx_out)
    y_l = y_l + d_skip[:, None] * ssd_l[0]

    out_l = merge_heads(o_l, ga_l, y_l.reshape(bsz, L, SSD_WIDTH).astype(x_lat.dtype), z_l, ssd_norm_g, w_out)
    new_lat = x_lat + g_l * out_l

    new_ctx = x_ctx
    if ctx_out:
        q_c, ga_c, z_c = split_query_cols(p_c)
        q_c = rms_norm(q_c.reshape(bsz, lc, N_Q_HEADS, HEAD_DIM), q_norm_g)
        o_c = gqa_dense(q_c, k_c, v_c)
        y_c = y_c + d_skip[:, None] * ssd_c[0]
        out_c = merge_heads(o_c, ga_c, y_c.reshape(bsz, lc, SSD_WIDTH).astype(x_ctx.dtype), z_c, ssd_norm_g, w_out)
        new_ctx = x_ctx + g_c * out_c
    return new_lat, new_ctx

def setup_inputs(seed: int = 0) -> dict:
    key = jax.random.key(seed)
    ks = jax.random.split(key, 20)
    f32 = jnp.float32
    nrm = lambda k, shape, s: jax.random.normal(k, shape, f32) * s
    dt0 = jnp.exp(jax.random.uniform(ks[9], (DEPTH, 2, SSD_HEADS), f32, math.log(1e-3), math.log(1e-1)))
    return {
        "x": nrm(ks[0], (BATCH, SEQ, D_MODEL), 1.0),
        "c": nrm(ks[1], (BATCH, D_MODEL), 1.0),
        "ctx": nrm(ks[2], (BATCH, CTX_LEN, D_MODEL), 1.0),
        "c_ctx": nrm(ks[3], (D_MODEL,), 1.0),
        "ada_w": nrm(ks[4], (DEPTH, D_MODEL, 3 * D_MODEL), 0.5 * D_MODEL ** -0.5),
        "ada_b": nrm(ks[5], (DEPTH, 3 * D_MODEL), 0.01),
        "norm_g": 1.0 + nrm(ks[6], (DEPTH, D_MODEL), 0.05),
        "w_in": nrm(ks[7], (DEPTH, D_MODEL, PROJ_COLS), D_MODEL ** -0.5),
        "conv_w": nrm(ks[8], (DEPTH, D_CONV, CONV_CH), D_CONV ** -0.5),
        "conv_b": nrm(ks[10], (DEPTH, CONV_CH), 0.01),
        "dt_bias": dt0 + jnp.log(-jnp.expm1(-dt0)),
        "a_log": jnp.log(jax.random.uniform(ks[11], (DEPTH, 2, SSD_HEADS), f32, 1.0, 16.0)),
        "d_skip": 1.0 + nrm(ks[12], (DEPTH, SSD_HEADS), 0.05),
        "q_norm_g": 1.0 + nrm(ks[13], (DEPTH, HEAD_DIM), 0.05),
        "k_norm_g": 1.0 + nrm(ks[14], (DEPTH, HEAD_DIM), 0.05),
        "ssd_norm_g": 1.0 + nrm(ks[15], (DEPTH, SSD_WIDTH), 0.05),
        "w_out": nrm(ks[16], (DEPTH, D_INNER, D_MODEL), D_INNER ** -0.5),
        "final_g": 1.0 + nrm(ks[17], (D_MODEL,), 0.05),
    }

def reference(x, c, ctx, c_ctx, ada_w, ada_b, norm_g, w_in, conv_w, conv_b, dt_bias, a_log, d_skip,
              q_norm_g, k_norm_g, ssd_norm_g, w_out, final_g):
    x_lat, x_ctx = x, ctx
    for layer in range(DEPTH):
        ctx_out = layer < DEPTH - 1
        x_lat, x_ctx = hybrid_layer(x_lat, x_ctx, c, c_ctx, ada_w[layer], ada_b[layer], norm_g[layer],
                                    w_in[layer], conv_w[layer], conv_b[layer], dt_bias[layer],
                                    a_log[layer], d_skip[layer], q_norm_g[layer], k_norm_g[layer],
                                    ssd_norm_g[layer], w_out[layer], ctx_out)
    return rms_norm(x_lat, final_g)


_drawn_inputs = setup_inputs


def setup_inputs(seed=0):
    import zlib

    import numpy as np

    out = dict(_drawn_inputs(seed))
    spreads = {}
    factors = {'ctx': 8.0,
     'c_ctx': 8.0,
     'ada_b': 6.786,
     'norm_g': 3.672,
     'conv_b': 51.895,
     'd_skip': 64.0,
     'q_norm_g': 8.0,
     'k_norm_g': 8.0,
     'ssd_norm_g': 16.912}
    for name, (base, spread) in spreads.items():
        noise = np.random.default_rng([zlib.crc32(name.encode()), seed]).standard_normal(out[name].shape)
        drawn = base * np.exp(spread * noise) if base else spread * noise
        out[name] = __import__('jax').numpy.asarray(drawn.astype(out[name].dtype))
    for name, factor in factors.items():
        out[name] = (out[name] * factor).astype(out[name].dtype)
    return out
```

```python
from contextlib import ExitStack

import numpy as np

import concourse.bass as bass
from concourse import mybir

P = 128
D_MODEL = 1024
SEQ = 2048
CTX = 256
TOK = CTX + SEQ
GRID_W = 64
HEAD_DIM = 64
N_Q = 16
N_KV = 4
Q_PER_KV = N_Q // N_KV
SSD_HEADS = 16
GROUPS = 2
HEADS_PER_GROUP = SSD_HEADS // GROUPS
D_STATE = 128
D_CONV = 5
EPS = 1e-6
WIDTH = 1024
KD = D_MODEL // P
CTX_TILES = CTX // P
LAT_TILES = SEQ // P
TILES = TOK // P
XBC_TILES = (WIDTH + 2 * GROUPS * D_STATE) // P
OFF_XBC = 2 * N_KV * HEAD_DIM
OFF_Q = OFF_XBC + XBC_TILES * P + 2 * SSD_HEADS
OFF_G = OFF_Q + WIDTH
OFF_Z = OFF_G + WIDTH
PAD = D_CONV // 2
COLS_W = 256
HPB = COLS_W // HEAD_DIM
BLOCKS = [(0, CTX)] + [(CTX + 512 * i, 512) for i in range(SEQ // 512)]

F32 = mybir.dt.float32
F32R = mybir.dt.float32r
ALU = mybir.AluOpType
ACT = mybir.ActivationFunctionType
AX = mybir.AxisListType

ROW_C, ROW_CCTX, ROW_NORM, ROW_CONVW = 0, KD, 2 * KD, 3 * KD
ROW_CONVB = ROW_CONVW + D_CONV * XBC_TILES
ROW_ADAB = ROW_CONVB + XBC_TILES
ROW_SSDG = ROW_ADAB + 3 * KD


def bcast(ap, dims):
    return bass.AP(tensor=ap.tensor, offset=ap.offset, ap=[list(ap.ap[0])] + [list(d) for d in dims])


def stage_modulation(nc, sem, io, keep):
    with ExitStack() as ctx:
        def sb(name, shape, dt=F32):
            return ctx.enter_context(nc.sbuf_tensor(name, shape, dt))

        SLOTS, CW = 3, 512
        CHUNKS = 3 * D_MODEL // CW
        rows = sb("rows", [P, P])
        silu_c = sb("silu_c", [P, 2, KD])
        ada = sb("ada", [P, SLOTS, KD, CW])
        mod = sb("mod", [P, 3 * KD, 2])
        ps_cols = ctx.enter_context(nc.psum_tensor("ps_cols", [P, 512], F32))
        ps_mod = ctx.enter_context(nc.psum_tensor("ps_mod", [P, 512], F32))
        mod_psum = ps_mod[:, 0:2 * 3 * KD].rearrange("p (m j) -> p m j", j=2)
        rows_landed, ident_landed = sem("rows_landed"), sem("ident_landed")
        ada_landed = [sem(f"ada_landed{s}") for s in range(SLOTS)]
        ada_used, cols_turned, cols_ready = sem("ada_used"), sem("cols_turned"), sem("cols_ready")
        c_ready, mod_summed, mod_ready = sem("c_ready"), sem("mod_summed"), sem("mod_ready")
        vecs_ready, gate_stored = sem("vecs_ready"), sem("gate_stored")
        ada_w = io["ada_w"].rearrange("o (k p) (m c) -> p (o k) m c", p=P, c=CW)
        block = ctx.enter_context(nc.Block())

        @block.sync
        def _(sync):
            sync.dma_start(keep["ident"][:], io["ident"]).then_inc(ident_landed, 16)
            sync.dma_start(keep["pick"][:], io["pick"]).then_inc(ident_landed, 16)
            for row, name, view in ((ROW_C, "c", "o (r p) -> (o r) p"), (ROW_CCTX, "c_ctx", "(r p) -> r p"),
                                    (ROW_NORM, "norm_g", "o (r p) -> (o r) p"),
                                    (ROW_CONVW, "conv_w", "o k (r p) -> (o k r) p"),
                                    (ROW_CONVB, "conv_b", "o (r p) -> (o r) p"),
                                    (ROW_ADAB, "ada_b", "o (r p) -> (o r) p"),
                                    (ROW_SSDG, "ssd_norm_g", "o (r p) -> (o r) p")):
                src = io[name].rearrange(view, p=P)
                sync.dma_start(rows[row:row + src.shape[0], :], src).then_inc(rows_landed, 16)
            for n in range(CHUNKS):
                if n >= SLOTS:
                    sync.wait_ge(ada_used, n - SLOTS + 1)
                sync.dma_start(ada[:, n % SLOTS], ada_w[:, :, n]).then_inc(ada_landed[n % SLOTS], 16)
            sync.wait_ge(mod_ready, 1)
            sync.dma_start(keep["gate_dram"].rearrange("(k p) -> p k", p=P),
                           mod[:, 2 * KD:3 * KD, 0], allow_slow_non_contiguous=True).then_inc(gate_stored, 16)
            sync.wait_ge(gate_stored, 16)

        @block.tensor
        def _(pe):
            pe.wait_ge(rows_landed, 7 * 16)
            pe.wait_ge(ident_landed, 32)
            pe.transpose(ps_cols[:, 0:P], rows[:], keep["ident"][:]).then_inc(cols_turned, 1)
            pe.wait_ge(c_ready, 1)
            for n in range(CHUNKS):
                pe.wait_ge(ada_landed[n % SLOTS], 16 * (n // SLOTS + 1))
                for j in range(CW // P):
                    for k in range(KD):
                        last = pe.matmul(mod_psum[:, n * (CW // P) + j, :],
                                         ada[:, n % SLOTS, k, j * P:(j + 1) * P], silu_c[:, :, k],
                                         start=(k == 0), stop=(k == KD - 1))
                last.then_inc(ada_used, 1)

        @block.scalar
        def _(act):
            act.wait_ge(cols_ready, 1)
            act.activation(silu_c[:].rearrange("p j k -> p (j k)"), keep["cols"][:, 0:2 * KD],
                           ACT.Silu).then_inc(c_ready, 1)

        @block.vector
        def _(dve):
            dve.memset(keep["eps"][:], EPS).then_inc(vecs_ready, 1)
            dve.memset(keep["one"][:], 1.0).then_inc(vecs_ready, 1)
            dve.wait_ge(cols_turned, 1)
            dve.tensor_copy(keep["cols"][:], ps_cols[:, 0:P]).then_inc(cols_ready, 1)
            dve.wait_ge(cols_ready, 1)
            dve.wait_ge(ada_used, CHUNKS)
            bias = keep["cols"][:, ROW_ADAB:ROW_ADAB + 3 * KD]
            dve.tensor_tensor(mod[:], mod_psum, bcast(bias, [(1, 3 * KD), (0, 2)]), ALU.add).then_inc(mod_ready, 1)
            dve.wait_ge(mod_ready, 1)
            for j in range(2):
                dve.tensor_copy(keep["shift"][:, j], mod[:, 0:KD, j]).then_inc(vecs_ready, 1)
                dve.scalar_tensor_tensor(keep["scale"][:, j], mod[:, KD:2 * KD, j], 1.0,
                                         keep["cols"][:, ROW_NORM:ROW_NORM + KD], ALU.add,
                                         ALU.mult).then_inc(vecs_ready, 1)


def split(dve, w_raw, w_hi, w_lo, hi_done, count, lo_done):
    dve.tensor_copy(w_hi, w_raw).then_inc(hi_done, 1)
    dve.wait_ge(hi_done, count)
    dve.tensor_tensor(w_lo, w_raw, w_hi.bitcast(F32), ALU.subtract).then_inc(lo_done, 1)


def stage_hidden(nc, sem, io, keep, h_hi, h_lo):
    with ExitStack() as ctx:
        def sb(name, shape, dt=F32):
            return ctx.enter_context(nc.sbuf_tensor(name, shape, dt))

        GT = 4
        xin = sb("xin", [P, 2, GT, D_MODEL])
        junk = sb("junk", [P, D_MODEL])
        ss = sb("ss", [P, 2, GT])
        rms, rstd = sb("rms", [P, 2, GT]), sb("rstd", [P, 2, GT])
        h32 = sb("h32", [P, 2, 512])
        ps_x = [ctx.enter_context(nc.psum_tensor(f"ps_x{b}", [P, 512], F32)) for b in range(4)]
        x_landed = [sem(f"x_landed{s}") for s in range(2)]
        x_squared, x_rms, x_rstd, x_normed, x_turned = (sem("x_squared"), sem("x_rms"), sem("x_rstd"),
                                                        sem("x_normed"), sem("x_turned"))
        h_full, h_hi_done, h_lo_done, x_free = sem("h_full"), sem("h_hi_done"), sem("h_lo_done"), sem("x_free")
        x_lat = io["x"].rearrange("o (g t p) d -> p (o g) t d", p=P, t=GT)
        x_ctx = io["ctx"].rearrange("o (t p) d -> p (o t) d", p=P)
        groups = [(CTX_TILES, 0, 1)] + [(GT, CTX + 512 * g, 0) for g in range(SEQ // 512)]
        block = ctx.enter_context(nc.Block())

        @block.sync
        def _(sync):
            for g, (tiles, tok, which) in enumerate(groups):
                if g >= 2:
                    sync.wait_ge(x_turned, KD * (g - 1))
                src = x_ctx if g == 0 else x_lat[:, g - 1]
                sync.dma_start(xin[:, g % 2, 0:tiles], src).then_inc(x_landed[g % 2], 16)

        @block.scalar
        def _(act):
            def norms(g):
                tiles = groups[g][0]
                act.wait_ge(x_landed[g % 2], 16 * (g // 2 + 1))
                for t in range(tiles):
                    if g or t:
                        act.wait_ge(x_squared, sum(x[0] for x in groups[:g]) + t)
                    if g >= 2 and t == 0:
                        act.wait_ge(x_rms, g - 1)
                    act.activation(junk[:], xin[:, g % 2, t], ACT.Square,
                                   accum_out=ss[:, g % 2, t:t + 1]).then_inc(x_squared, 1)
                act.wait_ge(x_squared, sum(x[0] for x in groups[:g + 1]))
                if g >= 2:
                    act.wait_ge(x_normed, sum(x[0] for x in groups[:g - 1]))
                act.activation(rms[:, g % 2, 0:tiles], ss[:, g % 2, 0:tiles], ACT.Sqrt, scale=1.0 / D_MODEL,
                               bias=keep["eps"][:]).then_inc(x_rms, 1)

            norms(0)
            for g, (tiles, tok, which) in enumerate(groups):
                if g + 1 < len(groups):
                    norms(g + 1)
                for k in range(KD):
                    n = g * KD + k
                    act.wait_ge(x_turned, n + 1)
                    if n >= 2:
                        act.wait_ge(h_lo_done, n - 1)
                    act.activation(h32[:, n % 2, 0:tiles * P], ps_x[n % 4][:, 0:tiles * P], ACT.Identity,
                                   bias=keep["shift"][:, which, k:k + 1],
                                   scale=keep["scale"][:, which, k:k + 1]).then_inc(h_full, 1)

        @block.vector
        def _(dve):
            def normalise(g):
                dve.wait_ge(x_rms, g + 1)
                dve.reciprocal(rstd[:, g % 2, 0:groups[g][0]], rms[:, g % 2, 0:groups[g][0]]).then_inc(x_rstd, 1)
                dve.wait_ge(x_rstd, g + 1)
                for t in range(groups[g][0]):
                    dve.tensor_scalar(xin[:, g % 2, t], xin[:, g % 2, t], rstd[:, g % 2, t:t + 1], None,
                                      ALU.mult).then_inc(x_normed, 1)

            normalise(0)
            for g, (tiles, tok, which) in enumerate(groups):
                if g + 1 < len(groups):
                    normalise(g + 1)
                for k in range(KD):
                    n = g * KD + k
                    dve.wait_ge(h_full, n + 1)
                    split(dve, h32[:, n % 2, 0:tiles * P], h_hi[:, k, tok:tok + tiles * P],
                          h_lo[:, k, tok:tok + tiles * P], h_hi_done, n + 1, h_lo_done)

        @block.tensor
        def _(pe):
            for g, (tiles, tok, which) in enumerate(groups):
                pe.wait_ge(x_normed, sum(x[0] for x in groups[:g + 1]))
                for k in range(KD):
                    n = g * KD + k
                    if n >= 4:
                        pe.wait_ge(h_full, n - 3)
                    for t in range(tiles):
                        last = pe.transpose(ps_x[n % 4][:, t * P:(t + 1) * P], xin[:, g % 2, t, k * P:(k + 1) * P],
                                            keep["ident"][:])
                    last.then_inc(x_turned, 1)



RING = 2


class TokenMajor:

    def __init__(self, nc, sem, ctx, tag, src, count, tiles):
        self.src, self.count, self.tiles, self.n_tiles = src, count, tiles, len(tiles)

        def sb(name, shape, dt=F32):
            return ctx.enter_context(nc.sbuf_tensor(f"{tag}_{name}", shape, dt))

        self.w_raw = sb("w_raw", [P, KD, COLS_W])
        self.w_hi = sb("w_hi", [P, 2, KD, COLS_W], F32R)
        self.w_lo = sb("w_lo", [P, 2, KD, COLS_W], F32R)
        self.acc = [ctx.enter_context(nc.psum_tensor(f"{tag}_acc{b}", [P, 512], F32)) for b in range(4)]
        self.w_landed, self.w_hi_done, self.w_split = sem(tag + "w_landed"), sem(tag + "w_hi_done"), sem(tag + "w_split")
        self.w_used, self.acc_done, self.acc_free = sem(tag + "w_used"), sem(tag + "acc_done"), sem(tag + "acc_free")

    def blocks(self, eng, body):
        if self.count == 1:
            body(0, 0)
            return
        with eng.Fori(0, self.count - 1, 2) as i:
            for u in range(2):
                body(i + u, u)

    def load(self, sync, b):
        sync.wait_ge(self.w_split, b)
        sync.dma_start(self.w_raw[:], self.src(b)).then_inc(self.w_landed, 16)

    def split(self, dve, b, slot):
        dve.wait_ge(self.w_landed, (b + 1) * 16)
        dve.wait_ge(self.w_used, b + 1)
        split(dve, self.w_raw[:], self.w_hi[:, slot], self.w_lo[:, slot], self.w_hi_done, b + 1, self.w_split)

    def products(self, pe, h_hi, h_lo, b, slot, i):
        n, bank = b * self.n_tiles + i, self.acc[i % 4][:, 0:COLS_W]
        tok = slice(self.tiles[i] * P, (self.tiles[i] + 1) * P)
        if i == 0:
            pe.wait_ge(self.w_split, b + 1)
        pe.wait_ge(self.acc_free, n + 1)
        for k in range(KD):
            pe.matmul(bank, h_hi[:, k, tok], self.w_hi[:, slot, k], start=(k == 0), stop=False)
            pe.matmul(bank, h_hi[:, k, tok], self.w_lo[:, slot, k], start=False, stop=False)
            last = pe.matmul(bank, h_lo[:, k, tok], self.w_hi[:, slot, k], start=False, stop=(k == KD - 1))
        last.then_inc(self.acc_done, 1)

    def used(self, pe):
        pe.drain().then_inc(self.w_used, 1)


def stage_plain(nc, sem, h_hi, h_lo, tag, src, count, tiles, func, dst):
    with ExitStack() as ctx:
        tm = TokenMajor(nc, sem, ctx, tag, src, count, tiles)
        out = ctx.enter_context(nc.sbuf_tensor(f"{tag}_out", [P, RING, COLS_W], F32))
        stored = [sem(f"{tag}stored{s}") for s in range(RING)]
        block = ctx.enter_context(nc.Block())
        nt = len(tiles)

        @block.sync
        def _(sync):
            tm.load(sync, 0)

            def body(b, slot):
                if count > 1:
                    tm.load(sync, b + 1)
                for i in range(nt):
                    sync.wait_ge(tm.acc_free, b * nt + i + 5)
                    sync.dma_start(dst(b, i), out[:, i % RING]).then_inc(stored[i % RING], 16)

            tm.blocks(sync, body)
            for s in range(RING):
                sync.wait_ge(stored[s], 16 * count * nt // RING)

        @block.tensor
        def _(pe):
            def body(b, slot):
                for i in range(nt):
                    tm.products(pe, h_hi, h_lo, b, slot, i)
                tm.used(pe)

            tm.blocks(pe, body)

        @block.scalar
        def _(act):
            act.sem_inc(tm.acc_free, 4)

            def body(b, slot):
                for i in range(nt):
                    n, s = b * nt + i, i % RING
                    act.wait_ge(tm.acc_done, n + 1)
                    act.wait_ge(stored[s], 16 * (b * (nt // RING) + i // RING))
                    act.activation(out[:, s], tm.acc[i % 4][:, 0:COLS_W], func).then_inc(tm.acc_free, 1)

            tm.blocks(act, body)

        @block.vector
        def _(dve):
            dve.sem_inc(tm.w_used, RING)
            tm.split(dve, 0, 0)
            if count > 1:
                tm.blocks(dve, lambda b, slot: tm.split(dve, b + 1, 1 - slot))


def stage_heads(nc, sem, io, keep, h_hi, h_lo, tag, src, count, tiles, gain, gain_scale, dst):
    with ExitStack() as ctx:
        def sb(name, shape, dt=F32):
            return ctx.enter_context(nc.sbuf_tensor(f"{tag}_{name}", shape, dt))

        tm = TokenMajor(nc, sem, ctx, tag, src, count, tiles)
        turn = [ctx.enter_context(nc.psum_tensor(f"{tag}_turn{b}", [P, 512], F32)) for b in range(RING)]
        rope = sb("rope", [P, 2, TILES, HEAD_DIM])
        gains = sb("gains", [P, 2, HEAD_DIM])
        sq, raw = sb("sq", [P, RING, COLS_W]), sb("raw", [P, RING, COLS_W])
        r1, r2 = sb("r1", [P, RING, COLS_W]), sb("r2", [P, RING, COLS_W])
        t_hi, t_lo = sb("t_hi", [P, RING, COLS_W], F32R), sb("t_lo", [P, RING, COLS_W], F32R)
        hss, hrms, hrstd = sb("hss", [P, RING, HPB]), sb("hrms", [P, RING, HPB]), sb("hrstd", [P, RING, HPB])
        names = ("sq_done", "hss_done", "rms_done", "rstd_done", "n_done", "r1_done", "r2_done", "rot_done",
                 "turned", "hi_done", "lo_free", "raw_free", "sq_free", "tables_landed", "tables_scaled")
        (sq_done, hss_done, rms_done, rstd_done, n_done, r1_done, r2_done, rot_done, turned, hi_done, lo_free,
         raw_free, sq_free, tables_landed, tables_scaled) = [sem(f"{tag}{x}") for x in names]
        hi_stored, lo_stored = [sem(f"{tag}hi_st{s}") for s in range(RING)], [sem(f"{tag}lo_st{s}") for s in range(RING)]
        nt = len(tiles)
        QUARTER = HEAD_DIM // 4

        def heads(x):
            return x.rearrange("p (h d) -> p h d", d=HEAD_DIM)

        def quarters(x, half):
            return x.rearrange("p (a f d) -> p a f d", f=2, d=QUARTER)[:, :, half]

        block = ctx.enter_context(nc.Block())

        @block.sync
        def _(sync):
            tm.load(sync, 0)
            sync.dma_start(rope[:], io["rope"]).then_inc(tables_landed, 16)
            sync.dma_start(gains[:, 0], io[gain].broadcast_to([P, HEAD_DIM])).then_inc(tables_landed, 16)
            swap = io[gain].rearrange("o (a f d) -> o a f d", f=2, d=QUARTER)
            for half in range(2):
                sync.dma_start(quarters(gains[:, 1], half),
                               swap[:, :, 1 - half].broadcast_to([P, 2, QUARTER])).then_inc(tables_landed, 16)

            def body(b, slot):
                if count > 1:
                    tm.load(sync, b + 1)
                for i in range(nt):
                    n = b * nt + i
                    sync.wait_ge(hi_done, n + 1)
                    sync.dma_start(dst(0, b, i), t_hi[:, i % RING].bitcast(F32).rearrange(
                        "p (j t) -> p j t", t=P)).then_inc(hi_stored[i % RING], 16)
                    sync.wait_ge(lo_free, n + 1 + RING)
                    sync.dma_start(dst(1, b, i), t_lo[:, i % RING].bitcast(F32).rearrange(
                        "p (j t) -> p j t", t=P)).then_inc(lo_stored[i % RING], 16)

            tm.blocks(sync, body)
            for s in range(RING):
                sync.wait_ge(hi_stored[s], 16 * count * nt // RING)
                sync.wait_ge(lo_stored[s], 16 * count * nt // RING)

        @block.tensor
        def _(pe):
            pe.sem_inc(turned, RING)

            def turn_tile(b, i):
                n, s = b * nt + i, i % RING
                pe.wait_ge(rot_done, n + 1)
                pe.wait_ge(lo_free, n + 1)
                for j in range(COLS_W // P):
                    last = pe.transpose(turn[s][:, j * P:(j + 1) * P], r1[:, s, j * P:(j + 1) * P], keep["ident"][:])
                last.then_inc(turned, 1)

            def body(b, slot):
                for i in range(nt):
                    tm.products(pe, h_hi, h_lo, b, slot, i)
                    if i >= 2:
                        turn_tile(b, i - 2)
                tm.used(pe)
                turn_tile(b, nt - 2)
                turn_tile(b, nt - 1)

            tm.blocks(pe, body)

        @block.scalar
        def _(act):
            act.sem_inc(tm.acc_free, 4)

            def take(b, i):
                n, s = b * nt + i, i % RING
                act.wait_ge(tm.acc_done, n + 1)
                act.wait_ge(sq_free, n + 1)
                act.activation(sq[:, s], tm.acc[i % 4][:, 0:COLS_W], ACT.Square).then_inc(sq_done, 1)
                act.wait_ge(raw_free, n + 1)
                act.activation(raw[:, s], tm.acc[i % 4][:, 0:COLS_W], ACT.Copy).then_inc(tm.acc_free, 1)

            def rms(b, i):
                n, s = b * nt + i, i % RING
                act.wait_ge(hss_done, n + 1)
                act.activation(hrms[:, s], hss[:, s], ACT.Sqrt, scale=1.0 / HEAD_DIM, bias=keep["eps"][:]).then_inc(
                    rms_done, 1)

            def hi(b, i):
                n, s = b * nt + i, i % RING
                act.wait_ge(turned, n + 1 + RING)
                act.wait_ge(hi_stored[s], 16 * (b * (nt // RING) + i // RING))
                act.activation(t_hi[:, s], turn[s][:, 0:COLS_W], ACT.Copy).then_inc(hi_done, 1)

            def body(b, slot):
                for i in range(nt + 3):
                    if i < nt:
                        take(b, i)
                    if 1 <= i <= nt:
                        rms(b, i - 1)
                    if i >= 3:
                        hi(b, i - 3)

            tm.blocks(act, body)

        @block.gpsimd
        def _(pool):
            pool.wait_ge(tables_scaled, 3)

            def body(b, slot):
                for i in range(nt):
                    n, s = b * nt + i, i % RING
                    pool.wait_ge(n_done, n + 1)
                    pool.wait_ge(turned, n + 1)
                    pool.tensor_tensor(heads(r1[:, s]), heads(raw[:, s]),
                                       bcast(rope[:, 0, tiles[i]], [(0, HPB), (1, HEAD_DIM)]),
                                       ALU.mult).then_inc(r1_done, 1)

            tm.blocks(pool, body)

        @block.vector
        def _(dve):
            dve.sem_inc(tm.w_used, RING)
            dve.sem_inc(sq_free, RING)
            dve.sem_inc(raw_free, RING)
            dve.sem_inc(lo_free, RING)
            tm.split(dve, 0, 0)
            dve.wait_ge(tables_landed, 64)
            dve.tensor_scalar(gains[:], gains[:], gain_scale, None, ALU.mult).then_inc(tables_scaled, 1)
            dve.wait_ge(tables_scaled, 1)
            for which in range(2):
                dve.tensor_tensor(rope[:, which], rope[:, which],
                                  bcast(gains[:, which], [(0, TILES), (1, HEAD_DIM)]), ALU.mult).then_inc(
                                      tables_scaled, 1)
            dve.wait_ge(tables_scaled, 3)

            def total(b, i):
                n, s = b * nt + i, i % RING
                dve.wait_ge(sq_done, n + 1)
                dve.tensor_reduce(hss[:, s], heads(sq[:, s]), AX.X, ALU.add).then_inc(hss_done, 1)
                dve.wait_ge(hss_done, n + 1)
                dve.sem_inc(sq_free, 1)

            def rotate(b, i):
                n, s = b * nt + i, i % RING
                dve.wait_ge(rms_done, n + 1)
                dve.reciprocal(hrstd[:, s], hrms[:, s]).then_inc(rstd_done, 1)
                dve.wait_ge(rstd_done, n + 1)
                dve.wait_ge(tm.acc_free, n + 5)
                dve.tensor_tensor(heads(raw[:, s]), heads(raw[:, s]), bcast(hrstd[:, s], [(1, HPB), (0, HEAD_DIM)]),
                                  ALU.mult).then_inc(n_done, 1)
                dve.wait_ge(n_done, n + 1)
                dve.wait_ge(rot_done, n)
                for half in range(2):
                    t = rope[:, 1, tiles[i]].rearrange("p (a f d) -> p a f d", f=2, d=QUARTER)[:, :, half]
                    dve.tensor_tensor(
                        quarters(r2[:, s], half).rearrange("p (h a) d -> p h a d", a=2),
                        quarters(raw[:, s], 1 - half).rearrange("p (h a) d -> p h a d", a=2),
                        bcast(t, [(0, HPB), (2 * QUARTER, 2), (1, QUARTER)]), ALU.mult).then_inc(r2_done, 1)
                dve.wait_ge(r2_done, 2 * n + 2)
                dve.wait_ge(r1_done, n + 1)
                dve.sem_inc(raw_free, 1)
                dve.tensor_tensor(r1[:, s], r1[:, s], r2[:, s], ALU.add).then_inc(rot_done, 1)

            def lo(b, i):
                n, s = b * nt + i, i % RING
                dve.wait_ge(hi_done, n + 1)
                dve.wait_ge(lo_stored[s], 16 * (b * (nt // RING) + i // RING))
                dve.tensor_tensor(t_lo[:, s], turn[s][:, 0:COLS_W], t_hi[:, s].bitcast(F32),
                                  ALU.subtract).then_inc(lo_free, 1)

            def body(b, slot):
                for i in range(nt + 3):
                    if i < nt:
                        total(b, i)
                    if 1 <= i <= nt:
                        rotate(b, i - 1)
                    if i == 4 and count > 1:
                        tm.split(dve, b + 1, 1 - slot)
                    if i >= 3:
                        lo(b, i - 3)

            tm.blocks(dve, body)



def channel_products(pe, h_hi, h_lo, w_hi, w_lo, bank, tok, width):
    for k in range(KD):
        pe.matmul(bank, w_hi[:, k], h_hi[:, k, tok:tok + width], start=(k == 0), stop=False)
        pe.matmul(bank, w_hi[:, k], h_lo[:, k, tok:tok + width], start=False, stop=False)
        last = pe.matmul(bank, w_lo[:, k], h_hi[:, k, tok:tok + width], start=False, stop=(k == KD - 1))
    return last


def stage_channels(nc, sem, io, keep, h_hi, h_lo, dram):
    with ExitStack() as ctx:
        def sb(name, shape, dt=F32):
            return ctx.enter_context(nc.sbuf_tensor("cm_" + name, shape, dt))

        GATE_TILES = WIDTH // P
        CONV = TOK + PAD
        NB = len(BLOCKS)
        w_raw = sb("w_raw", [P, KD, P])
        w_hi, w_lo = sb("w_hi", [P, RING, KD, P], F32R), sb("w_lo", [P, RING, KD, P], F32R)
        line = sb("line", [P, RING, TOK + 3 * PAD])
        y = sb("y", [P, RING, CONV])
        acc = [ctx.enter_context(nc.psum_tensor(f"cm_acc{b}", [P, 512], F32)) for b in range(NB)]
        (w_landed, w_hi_done, w_split, w_used, acc_done, acc_free, line_zero, line_free, tap_done, y_done) = [
            sem("cm_" + x) for x in ("w_landed", "w_hi_done", "w_split", "w_used", "acc_done", "acc_free",
                                     "line_zero", "line_free", "tap_done", "y_done")]
        stored = [sem(f"cm_stored{s}") for s in range(RING)]
        w_in = io["w_in"].rearrange("o (k p) c -> p (o k) c", p=P)
        w_xbc = w_in[:, :, OFF_XBC:OFF_XBC + XBC_TILES * P].rearrange("p k (m c) -> p m k c", c=P)
        w_gate = w_in[:, :, OFF_G:OFF_G + WIDTH].rearrange("p k (m c) -> p m k c", c=P)
        block = ctx.enter_context(nc.Block())

        def loop(eng, count, body):
            with eng.Fori(0, count - 1, 2) as i:
                for u in range(2):
                    body(i + u, u)

        @block.sync
        def _(sync):
            def load(src, m):
                sync.wait_ge(w_split, m)
                sync.dma_start(w_raw[:], src).then_inc(w_landed, 16)

            loop(sync, XBC_TILES, lambda m, s: load(w_xbc[:, m], m))
            loop(sync, GATE_TILES, lambda m, s: load(w_gate[:, m], m + XBC_TILES))

        @block.tensor
        def _(pe):
            def xbc(m, s):
                pe.wait_ge(w_split, m + 1)
                for i, (tok, width) in enumerate(BLOCKS):
                    pe.wait_ge(acc_free, m * NB + i + 1)
                    channel_products(pe, h_hi, h_lo, w_hi[:, s], w_lo[:, s], acc[i][:, 0:width], tok,
                                     width).then_inc(acc_done, 1)
                pe.drain().then_inc(w_used, 1)

            def gate(m, s):
                pe.wait_ge(w_split, m + XBC_TILES + 1)
                for i in range(1, NB):
                    pe.wait_ge(acc_free, XBC_TILES * NB + m * (NB - 1) + i + 1)
                    channel_products(pe, h_hi, h_lo, w_hi[:, s], w_lo[:, s], acc[i][:], BLOCKS[i][0],
                                     512).then_inc(acc_done, 1)
                pe.drain().then_inc(w_used, 1)

            loop(pe, XBC_TILES, xbc)
            loop(pe, GATE_TILES, gate)

        @block.scalar
        def _(act):
            act.sem_inc(acc_free, NB)

            def xbc(m, s):
                act.wait_ge(line_zero, 1)
                act.wait_ge(line_free, m + 1)
                for i, (tok, width) in enumerate(BLOCKS):
                    act.wait_ge(acc_done, m * NB + i + 1)
                    at = PAD + tok + (PAD if i else 0)
                    act.activation(line[:, s, at:at + width], acc[i][:, 0:width], ACT.Copy).then_inc(acc_free, 1)
                act.wait_ge(tap_done, D_CONV * (m + 1))
                act.activation(y[:, s], y[:, s], ACT.Silu).then_inc(y_done, 1)
                act.wait_ge(y_done, m + 1)
                act.dma_start(dram["xbc"][m, :, 0:CTX], y[:, s, 0:CTX]).then_inc(stored[s], 16)
                act.dma_start(dram["xbc"][m, :, CTX:TOK], y[:, s, CTX + PAD:CONV]).then_inc(stored[s], 16)

            def gate(m, s):
                act.wait_ge(stored[s], 16 * (XBC_TILES + m // 2) if isinstance(m, int) else gate_stored(m, s))
                for i in range(1, NB):
                    act.wait_ge(acc_done, XBC_TILES * NB + m * (NB - 1) + i)
                    act.activation(y[:, s, (i - 1) * 512:i * 512], acc[i][:], ACT.Silu).then_inc(acc_free, 1)
                act.wait_ge(acc_free, NB + XBC_TILES * NB + (m + 1) * (NB - 1))
                act.dma_start(dram["gate"][m], y[:, s, 0:SEQ]).then_inc(stored[s], 16)

            def gate_stored(m, s):
                return 16 * XBC_TILES + 8 * (m - s)

            loop(act, XBC_TILES, xbc)
            loop(act, GATE_TILES, gate)
            for s in range(RING):
                act.wait_ge(stored[s], 16 * XBC_TILES + 8 * GATE_TILES)

        @block.vector
        def _(dve):
            def part(m, s):
                dve.wait_ge(w_landed, 16 * (m + 1))
                dve.wait_ge(w_used, m + 1)
                split(dve, w_raw[:], w_hi[:, s], w_lo[:, s], w_hi_done, m + 1, w_split)

            dve.sem_inc(w_used, RING)
            dve.sem_inc(line_free, RING)
            dve.memset(line[:], 0.0).then_inc(line_zero, 1)
            dve.wait_ge(line_zero, 1)
            part(0, 0)

            def conv(m, s):
                part(m + 1, 1 - s)
                dve.wait_ge(acc_free, NB + NB * (m + 1))
                dve.wait_ge(stored[s], 16 * (m - s))
                for k in range(D_CONV):
                    tap = keep["cols"][:, bass.ds(ROW_CONVW + k * XBC_TILES + m, 1)]
                    if k == 0:
                        dve.tensor_scalar(y[:, s], line[:, s, 0:CONV], tap,
                                          keep["cols"][:, bass.ds(ROW_CONVB + m, 1)], ALU.mult,
                                          ALU.add).then_inc(tap_done, 1)
                    else:
                        dve.wait_ge(tap_done, D_CONV * m + k)
                        dve.scalar_tensor_tensor(y[:, s], line[:, s, k:k + CONV], tap, y[:, s], ALU.mult,
                                                 ALU.add).then_inc(tap_done, 1)
                dve.wait_ge(tap_done, D_CONV * (m + 1))
                dve.sem_inc(line_free, 1)

            loop(dve, XBC_TILES, conv)
            with dve.Fori(0, GATE_TILES - 3, 2) as i:
                for u in range(2):
                    part(XBC_TILES + 1 + i + u, 1 - u)
            part(XBC_TILES + GATE_TILES - 1, 1)


def stage_dt(nc, sem, io, keep, h_hi, h_lo, dram):
    NH = 2 * SSD_HEADS
    with ExitStack() as ctx:
        def sb(name, shape, dt=F32):
            return ctx.enter_context(nc.sbuf_tensor("dt_" + name, shape, dt))

        w_raw, w_hi, w_lo = sb("w_raw", [P, KD, P]), sb("w_hi", [P, KD, P], F32R), sb("w_lo", [P, KD, P], F32R)
        head = sb("head", [NH, 4])
        raw, soft = sb("raw", [NH, TOK]), sb("soft", [NH, TOK])
        sums = sb("sums", [NH, 2, TOK])
        ones = sb("ones", [NH, P])
        cols = sb("cols", [P, 5, TILES, NH])
        total = cols[:, 3]
        ps = [ctx.enter_context(nc.psum_tensor(f"dt_ps{b}", [P, 512], F32)) for b in range(8)]
        names = ("w_landed", "head_landed", "w_hi_done", "w_split", "head_ready", "acc_done", "raw_done", "steps",
                 "dt_done", "a_done", "ones_done", "scanned", "turned", "cols_done", "total_done", "factors", "stored",
                 "total_copied", "weight_log", "weighted")
        (w_landed, head_landed, w_hi_done, w_split, head_ready, acc_done, raw_done, steps, dt_done, a_done, ones_done,
         scanned, turned, cols_done, total_done, factors, stored, total_copied, weight_log, weighted) = [sem("dt_" + x) for x in names]
        HALF = TILES // 2
        w_in = io["w_in"].rearrange("o (k p) c -> p (o k) c", p=P)
        off = OFF_XBC + XBC_TILES * P
        block = ctx.enter_context(nc.Block())

        @block.sync
        def _(sync):
            sync.dma_start(w_raw[:], w_in[:, :, off:off + P]).then_inc(w_landed, 16)
            sync.dma_start(head[:, 0:1], io["dt_bias"].rearrange("o d h -> (d h) o")).then_inc(head_landed, 16)
            sync.dma_start(head[:, 1:2], io["a_log"].rearrange("o d h -> (d h) o")).then_inc(head_landed, 16)
            sync.wait_ge(scanned, 2 * TILES)
            for d in range(2):
                rows = slice(d * SSD_HEADS, (d + 1) * SSD_HEADS)
                sync.dma_start(dram["cs"][rows], sums[rows, d]).then_inc(stored, 16)
            sync.wait_ge(weighted, 1)
            sync.dma_start(dram["dtcols"], cols[:].rearrange("p a c h -> p (a c h)")).then_inc(stored, 16)
            sync.wait_ge(stored, 48)

        @block.tensor
        def _(pe):
            pe.wait_ge(w_split, 1)
            for i, (tok, width) in enumerate(BLOCKS):
                channel_products(pe, h_hi, h_lo, w_hi, w_lo, ps[i][:, 0:width], tok, width).then_inc(acc_done, 1)
            pe.wait_ge(raw_done, len(BLOCKS))
            pe.wait_ge(scanned, 2 * TILES)
            pe.wait_ge(dt_done, 1)
            for what in range(3):
                for c in range(TILES):
                    src = soft if what == 0 else sums[:, what - 1]
                    at = (c % HALF) * NH
                    last = pe.transpose(ps[2 * what + c // HALF][:, at:at + NH],
                                        (src[:, c * P:(c + 1) * P]), keep["ident"][0:NH, 0:NH])
                last.then_inc(turned, 1)
            pe.wait_ge(cols_done, 6)
            for d in range(2):
                pe.matmul(ps[6 + d][:, 0:TILES * SSD_HEADS], keep["pick"][:, d],
                          cols[:, 1, :, d * SSD_HEADS:(d + 1) * SSD_HEADS], start=True, stop=True).then_inc(
                              total_done, 1)

        @block.scalar
        def _(act):
            act.wait_ge(head_landed, 32)
            act.activation(head[:, 2:3], head[:, 1:2], ACT.Exp).then_inc(head_ready, 1)
            for i, (tok, width) in enumerate(BLOCKS):
                act.wait_ge(acc_done, i + 1)
                act.activation(raw[:, tok:tok + width], ps[i][0:NH, 0:width], ACT.Identity,
                               bias=head[:, 0:1]).then_inc(raw_done, 1)
            act.wait_ge(raw_done, len(BLOCKS))
            act.activation(soft[:], raw[:], ACT.Abs).then_inc(steps, 1)
            act.wait_ge(steps, 1)
            act.activation(soft[:], soft[:], ACT.Exp, scale=-1.0).then_inc(steps, 1)
            act.wait_ge(steps, 2)
            act.activation(soft[:], soft[:], ACT.Ln, bias=keep["one"][0:NH]).then_inc(steps, 1)
            act.wait_ge(cols_done, 6)
            act.activation(cols[:, 2], cols[:, 1], ACT.Exp).then_inc(factors, 1)
            act.wait_ge(weight_log, 1)
            act.activation(cols[:, 3], cols[:, 3], ACT.Exp).then_inc(factors, 1)
            act.activation(cols[:, 4], cols[:, 4], ACT.Exp).then_inc(factors, 1)

        @block.vector
        def _(dve):
            dve.wait_ge(w_landed, 16)
            split(dve, w_raw[:], w_hi[:], w_lo[:], w_hi_done, 1, w_split)
            dve.memset(ones[:], 1.0).then_inc(ones_done, 1)
            dve.wait_ge(head_ready, 1)
            dve.wait_ge(steps, 3)
            dve.scalar_tensor_tensor(soft[:], raw[:], 0.0, soft[:], ALU.max, ALU.add).then_inc(dt_done, 1)
            dve.wait_ge(dt_done, 1)
            dve.tensor_scalar(raw[:], soft[:], head[:, 2:3], -1.0, ALU.mult, ALU.mult).then_inc(a_done, 1)
            dve.wait_ge(a_done, 1)
            dve.wait_ge(ones_done, 1)
            for c in range(TILES):
                for d in range(2):
                    def way(x):
                        return x[:, ::-1] if d else x
                    dve.tensor_tensor_scan(way(sums[:, d, c * P:(c + 1) * P]), way(ones[:]),
                                           way(raw[:, c * P:(c + 1) * P]), 0.0, ALU.mult, ALU.add).then_inc(scanned, 1)
            heads = [slice(0, NH), slice(0, SSD_HEADS), slice(SSD_HEADS, NH)]
            for what in range(3):
                dve.wait_ge(turned, what + 1)
                for half in range(2):
                    src = ps[2 * what + half][:, 0:HALF * NH].rearrange("p (c h) -> p c h", h=NH)
                    dve.tensor_copy(cols[:, min(what, 1), half * HALF:(half + 1) * HALF, heads[what]],
                                    src[:, :, heads[what]]).then_inc(cols_done, 1)
            for d in range(2):
                dve.wait_ge(total_done, 2)
                dve.tensor_copy(total[:, :, heads[1 + d]],
                                ps[6 + d][:, 0:TILES * SSD_HEADS].rearrange("p (c h) -> p c h", h=SSD_HEADS)).then_inc(
                                    total_copied, 1)
            dve.wait_ge(total_copied, 2)
            dve.tensor_tensor(cols[:, 4], total, cols[:, 1], ALU.subtract).then_inc(weight_log, 1)
            dve.wait_ge(factors, 3)
            dve.tensor_tensor(cols[:, 4], cols[:, 4], cols[:, 0], ALU.mult).then_inc(weighted, 1)




class Factors:

    def __init__(self, cols):
        self.dt, self.cs, self.e_cs, self.e_total, self.weight = [cols[:, a] for a in range(5)]


def spread(x, at, d, g=None):
    heads = SSD_HEADS if g is None else HEADS_PER_GROUP
    h0 = d * SSD_HEADS + (0 if g is None else g * HEADS_PER_GROUP)
    return bcast(x[:, at, h0:h0 + heads], [(1, heads), (0, HEAD_DIM)])


def by_head(x):
    return x.rearrange("p (h d) -> p h d", d=HEAD_DIM)


def stage_ssd_backward(nc, sem, io, keep, dram, cols):
    f = Factors(cols)
    GW = HEADS_PER_GROUP * HEAD_DIM
    X_T = WIDTH // P
    with ExitStack() as ctx:
        def sb(name, shape, dt=F32):
            return ctx.enter_context(nc.sbuf_tensor("sb_" + name, shape, dt))

        xbc = sb("xbc", [P, 2, XBC_TILES, P])
        rows = sb("rows", [P, 2, WIDTH + GROUPS * D_STATE])
        xw = sb("xw", [P, 2, WIDTH])
        yb = sb("yb", [P, 2, WIDTH])
        state, decayed = sb("state", [P, WIDTH]), sb("decayed", [P, WIDTH])
        ps_turn = ctx.enter_context(nc.psum_tensor("sb_ps_turn", [P, 3 * 512], F32))
        ps_state = ctx.enter_context(nc.psum_tensor("sb_ps_state", [P, 2 * 512], F32))
        ps_off = ctx.enter_context(nc.psum_tensor("sb_ps_off", [P, 2 * 512], F32))
        names = ("cols_landed", "turned", "rows_done", "xw_done", "state_sum", "off_done", "yb_done", "decay_done",
                 "state_done")
        (cols_landed, turned, rows_done, xw_done, state_sum, off_done, yb_done, decay_done, state_done) = [
            sem("sb_" + x) for x in names]
        landed = [sem(f"sb_landed{s}") for s in range(2)]
        stored = [sem(f"sb_stored{s}") for s in range(2)]
        yb_stored = [sem(f"sb_yb_stored{s}") for s in range(2)]
        src = dram["xbc"].rearrange("m p (c t) -> c p m t", t=P)
        ROWS = WIDTH + GROUPS * D_STATE
        block = ctx.enter_context(nc.Block())

        def steps(eng, body):
            for n in range(CTX_TILES):
                body(n, CTX_TILES - 1 - n, n % 2, False)
            with eng.Fori(0, LAT_TILES - 1, 2) as i:
                for u in range(2):
                    body(CTX_TILES + i + u, i * -1 + (TILES - 1 - u), u, True)

        @block.sync
        def _(sync):
            sync.dma_start(cols[:].rearrange("p a c h -> p (a c h)"), dram["dtcols"]).then_inc(cols_landed, 16)

            def body(n, c, s, latent):
                if latent:
                    sync.wait_ge(state_sum, n - 1)
                sync.dma_start(xbc[:, s], src[c]).then_inc(landed[s], 16)

            steps(sync, body)

        @block.scalar
        def _(act):
            def body(n, c, s, latent):
                act.wait_ge(turned, n + 1)
                act.wait_ge(stored[s], 16 * (n - s))
                if latent:
                    act.wait_ge(xw_done, n - 1)
                    act.wait_ge(state_sum, n - 1)
                act.activation(rows[:, s], ps_turn[:, 0:ROWS], ACT.Copy).then_inc(rows_done, 1)
                act.wait_ge(rows_done, n + 1)
                act.dma_start(dram["x"][c], rows[:, s, 0:WIDTH]).then_inc(stored[s], 16)
                act.dma_start(dram["b"][c], rows[:, s, WIDTH:ROWS]).then_inc(stored[s], 16)
                if latent:
                    act.wait_ge(yb_done, 2 * (n - CTX_TILES) + 2)
                    act.dma_start(dram["yb"][c - CTX_TILES], yb[:, s]).then_inc(yb_stored[s], 16)

            steps(act, body)
            for s in range(2):
                act.wait_ge(stored[s], 16 * TILES)
                act.wait_ge(yb_stored[s], 16 * LAT_TILES // 2)

        @block.tensor
        def _(pe):
            def body(n, c, s, latent):
                pe.wait_ge(landed[s], 8 * (n - s) + 16)
                pe.wait_ge(rows_done, n)
                for m in range(X_T + GROUPS):
                    last = pe.transpose(ps_turn[:, m * P:(m + 1) * P], xbc[:, s, m], keep["ident"][:])
                last.then_inc(turned, 1)
                if latent:
                    pe.wait_ge(state_done, n)
                    pe.wait_ge(yb_done, 2 * (n - CTX_TILES))
                    for g in range(GROUPS):
                        last = pe.matmul(ps_off[:, g * GW:(g + 1) * GW], xbc[:, s, X_T + GROUPS + g],
                                         state[:, g * GW:(g + 1) * GW], start=True, stop=True)
                    last.then_inc(off_done, 1)
                pe.wait_ge(xw_done, n + 1)
                pe.wait_ge(state_done, n)
                for g in range(GROUPS):
                    last = pe.matmul(ps_state[:, g * GW:(g + 1) * GW],
                                     rows[:, s, WIDTH + g * D_STATE:WIDTH + (g + 1) * D_STATE],
                                     xw[:, s, g * GW:(g + 1) * GW], start=True, stop=True)
                last.then_inc(state_sum, 1)

            steps(pe, body)

        @block.vector
        def _(dve):
            dve.wait_ge(cols_landed, 16)

            def body(n, c, s, latent):
                dve.wait_ge(rows_done, n + 1)
                if latent:
                    dve.wait_ge(state_sum, n - 1)
                dve.tensor_tensor(by_head(xw[:, s]), by_head(rows[:, s, 0:WIDTH]), spread(f.weight, c, 1),
                                  ALU.mult).then_inc(xw_done, 1)
                if isinstance(n, int) and n == 0:
                    dve.wait_ge(state_sum, 1)
                    dve.tensor_copy(state[:], ps_state[:]).then_inc(state_done, 1)
                    return
                dve.wait_ge(state_done, n)
                dve.tensor_tensor(by_head(decayed[:]), by_head(state[:]), spread(f.e_total, c, 1),
                                  ALU.mult).then_inc(decay_done, 1)
                if latent:
                    dve.wait_ge(off_done, n - CTX_TILES + 1)
                    dve.wait_ge(yb_stored[s], 8 * (n - s) - 8 * CTX_TILES)
                    for g in range(GROUPS):
                        cut = slice(g * GW, (g + 1) * GW)
                        dve.tensor_tensor(by_head(yb[:, s, cut]), by_head(ps_off[:, cut]),
                                          spread(f.e_cs, c, 1, g), ALU.mult).then_inc(yb_done, 1)
                dve.wait_ge(decay_done, n)
                dve.wait_ge(state_sum, n + 1)
                dve.tensor_tensor(state[:], decayed[:], ps_state[:], ALU.add).then_inc(state_done, 1)

            steps(dve, body)


def stage_ssd_forward(nc, sem, io, keep, dram, cols):
    f = Factors(cols)
    GW = HEADS_PER_GROUP * HEAD_DIM
    X_T = WIDTH // P
    HL = SSD_HEADS * P
    with ExitStack() as ctx:
        def sb(name, shape, dt=F32):
            return ctx.enter_context(nc.sbuf_tensor("sf_" + name, shape, dt))

        bc = sb("bc", [P, 2, 2 * GROUPS, P])
        rows = sb("rows", [P, 2, WIDTH + GROUPS * D_STATE])
        sums_f, sums_b = sb("sums_f", [P, 2, SSD_HEADS, P]), sb("sums_b", [P, 2, SSD_HEADS, P])
        yb, z = sb("yb", [P, 2, WIDTH]), sb("z", [P, 2, WIDTH])
        cb = sb("cb", [P, 2, GROUPS, P])
        w = sb("w", [P, 2, SSD_HEADS, P])
        xw, y, junk = sb("xw", [P, WIDTH]), sb("y", [P, WIDTH]), sb("junk", [P, WIDTH])
        skip_x = sb("skip_x", [P, WIDTH])
        state, decayed = sb("state", [P, WIDTH]), sb("decayed", [P, WIDTH])
        d_skip = sb("d_skip", [P, SSD_HEADS])
        masks = sb("masks", [P, 2, P])
        t_hi, t_lo = sb("t_hi", [P, WIDTH], F32R), sb("t_lo", [P, WIDTH], F32R)
        ps_cb = ctx.enter_context(nc.psum_tensor("sf_ps_cb", [P, 512], F32))
        ps_turn = ctx.enter_context(nc.psum_tensor("sf_ps_turn", [P, 512], F32))
        ps_y = ctx.enter_context(nc.psum_tensor("sf_ps_y", [P, 2 * 512], F32))
        ps_off = ctx.enter_context(nc.psum_tensor("sf_ps_off", [P, 2 * 512], F32))
        ps_state = ctx.enter_context(nc.psum_tensor("sf_ps_state", [P, 2 * 512], F32))
        names = ("consts", "cb_done", "cb_masked", "diff_f", "diff_b", "least", "w_exp", "w_b", "w_sum", "w_done",
                 "xw_done", "state_sum", "state_done", "decay_done", "y_diag", "y_off", "y_a", "y_b", "y_c", "y_gated",
                 "skip_a", "skip_done", "squared", "turned", "hi_done", "lo_done",
                 "stored_hi", "stored_lo")
        sems = {x: sem("sf_" + x) for x in names}
        landed = [sem(f"sf_landed{s}") for s in range(2)]
        diag_landed = [sem(f"sf_diag_landed{s}") for s in range(2)]
        S = sems
        ROWS = WIDTH + GROUPS * D_STATE
        bc_src = dram["xbc"][X_T:XBC_TILES].rearrange("m p (c t) -> c p m t", t=P)
        cs_src = dram["cs"].rearrange("(d h) (c t) -> c d h t", d=2, t=P)
        out_dst = dram["ys"].rearrange("s m p (c t) -> s c p m t", t=P)
        block = ctx.enter_context(nc.Block())

        def steps(eng, context, first, second):
            for c in range(CTX_TILES):
                context(c, c, c % 2)
            first(0, 0)
            with eng.Fori(0, LAT_TILES - 3, 2) as i:
                for u in range(2):
                    first(i + u + 1, 1 - u)
                    second(i + u, u)
            for c in (LAT_TILES - 2, LAT_TILES - 1):
                if c + 1 < LAT_TILES:
                    first(c + 1, (c + 1) % 2)
                second(c, c % 2)

        def nothing(*_):
            pass

        @block.sync
        def _(sync):
            sync.dma_start(d_skip[:], io["d_skip"].broadcast_to([P, SSD_HEADS])).then_inc(S["consts"], 16)
            sync.dma_start(masks[:], io["masks"]).then_inc(S["consts"], 16)

            def context(c, n, s):
                sync.dma_start(rows[:, s, 0:WIDTH], dram["x"][c]).then_inc(landed[s], 16)
                sync.dma_start(rows[:, s, WIDTH:ROWS], dram["b"][c]).then_inc(landed[s], 16)

            def first(c, s):
                known = isinstance(c, int)
                if not known or c >= 2:
                    sync.wait_ge(S["w_done"], c - 1)
                    sync.wait_ge(S["y_off"], c - 1)
                sync.dma_start(bc[:, s], bc_src[c + CTX_TILES]).then_inc(diag_landed[s], 16)
                for d, dst in ((0, sums_f), (1, sums_b)):
                    sync.dma_start(dst[:, s], cs_src[c + CTX_TILES, d].unsqueeze(0).broadcast_to(
                        [P, SSD_HEADS, P])).then_inc(diag_landed[s], 16)
                sync.wait_ge(S["state_sum"], c + 1)
                if not known or c >= 2:
                    sync.wait_ge(S["y_diag"], c - 1)
                    sync.wait_ge(S["skip_done"], c - 1)
                    sync.wait_ge(S["y_gated"], c - 1)
                sync.dma_start(rows[:, s, 0:WIDTH], dram["x"][c + CTX_TILES]).then_inc(landed[s], 16)
                sync.dma_start(rows[:, s, WIDTH:ROWS], dram["b"][c + CTX_TILES]).then_inc(landed[s], 16)
                sync.dma_start(yb[:, s], dram["yb"][c]).then_inc(landed[s], 16)
                sync.dma_start(z[:, s], dram["z"][c]).then_inc(landed[s], 16)

            steps(sync, context, first, nothing)

        def rows_here(eng, c, s):
            eng.wait_ge(landed[s], 32 + 32 * (c - s) + 64)

        @block.gpsimd
        def _(pool):
            pool.wait_ge(S["consts"], 32)

            def first(c, s):
                for d, x, name in ((0, sums_f, "diff_f"), (1, sums_b, "diff_b")):
                    pool.wait_ge(diag_landed[s], 24 * (c - s) + 48)
                    col = f.cs[:, c + CTX_TILES, d * SSD_HEADS:(d + 1) * SSD_HEADS]
                    pool.tensor_tensor(x[:, s], x[:, s], bcast(col, [(1, SSD_HEADS), (0, P)]),
                                       ALU.subtract).then_inc(S[name], 1)

            def second(c, s):
                rows_here(pool, c, s)
                pool.wait_ge(S["y_c"], c)
                pool.tensor_tensor(by_head(skip_x[:]), by_head(rows[:, s, 0:WIDTH]),
                                   bcast(d_skip[:], [(1, SSD_HEADS), (0, HEAD_DIM)]), ALU.mult).then_inc(S["skip_a"], 1)
                pool.wait_ge(S["skip_a"], c + 1)
                pool.tensor_tensor(skip_x[:], skip_x[:], yb[:, s], ALU.add).then_inc(S["skip_done"], 1)

            steps(pool, nothing, first, second)

        @block.tensor
        def _(pe):
            def add_state(n, s):
                pe.wait_ge(S["xw_done"], n + 1)
                pe.wait_ge(S["state_done"], n)
                for g in range(GROUPS):
                    last = pe.matmul(ps_state[:, g * GW:(g + 1) * GW],
                                     rows[:, s, WIDTH + g * D_STATE:WIDTH + (g + 1) * D_STATE],
                                     xw[:, g * GW:(g + 1) * GW], start=True, stop=True)
                last.then_inc(S["state_sum"], 1)

            def first(c, s):
                pe.wait_ge(diag_landed[s], 24 * (c - s) + 48)
                pe.wait_ge(S["cb_masked"], 2 * c)
                for g in range(GROUPS):
                    last = pe.matmul(ps_cb[:, g * P:(g + 1) * P], bc[:, s, g], bc[:, s, GROUPS + g], start=True,
                                     stop=True)
                last.then_inc(S["cb_done"], 1)

            def second(c, s):
                pe.wait_ge(S["state_done"], c + CTX_TILES)
                pe.wait_ge(S["y_a"], 2 * c)
                for g in range(GROUPS):
                    last = pe.matmul(ps_off[:, g * GW:(g + 1) * GW], bc[:, s, GROUPS + g],
                                     state[:, g * GW:(g + 1) * GW], start=True, stop=True)
                last.then_inc(S["y_off"], 1)
                add_state(c + CTX_TILES, s)
                pe.wait_ge(S["w_done"], c + 1)
                pe.wait_ge(S["y_b"], c)
                for g in range(GROUPS):
                    for h in range(HEADS_PER_GROUP - 1, -1, -1):
                        head = g * HEADS_PER_GROUP + h
                        lo = (head - (h > 0)) * HEAD_DIM
                        last = pe.matmul(ps_y[:, lo:(head + 1) * HEAD_DIM], w[:, s, head],
                                         rows[:, s, lo:(head + 1) * HEAD_DIM], start=True, stop=True)
                last.then_inc(S["y_diag"], 1)
                pe.wait_ge(S["y_gated"], c + 1)
                for part in range(2):
                    pe.wait_ge(S["lo_done"], 2 * c + part)
                    for m in range(4):
                        at = (4 * part + m) * P
                        last = pe.transpose(ps_turn[:, m * P:(m + 1) * P], y[:, at:at + P], keep["ident"][:])
                    last.then_inc(S["turned"], 1)

            steps(pe, lambda c, n, s: add_state(n, s), first, second)

        @block.scalar
        def _(act):
            def first(c, s):
                act.wait_ge(S["least"], c + 1)
                act.activation(sums_f[:, s], sums_f[:, s], ACT.Exp).then_inc(S["w_exp"], 1)
                act.wait_ge(S["cb_masked"], 2 * c + 2)
                if not isinstance(c, int) or c >= 2:
                    act.wait_ge(S["y_diag"], c - 1)
                for h in range(SSD_HEADS):
                    act.activation(w[:, s, h], cb[:, 1, h // HEADS_PER_GROUP], ACT.Copy,
                                   scale=f.dt[:, c + CTX_TILES, SSD_HEADS + h:SSD_HEADS + h + 1]).then_inc(
                                       S["w_b"], 1)

            def second(c, s):
                act.wait_ge(S["y_gated"], c + 1)
                act.wait_ge(S["squared"], c)
                act.activation(junk[:], y[:], ACT.Square,
                               accum_out=keep["ss_y"][:, bass.ds(c, 1)]).then_inc(S["squared"], 1)
                for part in range(2):
                    act.wait_ge(S["turned"], 2 * c + part + 1)
                    act.wait_ge(S["stored_hi"], 16 * c)
                    act.activation(t_hi[:, part * 512:(part + 1) * 512], ps_turn[:], ACT.Copy).then_inc(
                        S["hi_done"], 1)
                for part, done, stored, src in ((0, "hi_done", "stored_hi", t_hi), (1, "lo_done", "stored_lo", t_lo)):
                    act.wait_ge(S[done], 2 * c + 2)
                    act.dma_start(out_dst[part, c], src[:].bitcast(F32).rearrange("p (m t) -> p m t", t=P)).then_inc(
                        S[stored], 16)

            steps(act, nothing, first, second)
            act.wait_ge(S["stored_hi"], 16 * LAT_TILES)
            act.wait_ge(S["stored_lo"], 16 * LAT_TILES)

        @block.vector
        def _(dve):
            dve.wait_ge(S["consts"], 32)

            def weigh(n, s, chunk):
                if not isinstance(n, int) or n:
                    dve.wait_ge(S["state_sum"], n)
                dve.tensor_tensor(by_head(xw[:]), by_head(rows[:, s, 0:WIDTH]), spread(f.weight, chunk, 0),
                                  ALU.mult).then_inc(S["xw_done"], 1)

            def advance(n, chunk):
                dve.wait_ge(S["state_sum"], n + 1)
                if isinstance(n, int) and n == 0:
                    dve.tensor_copy(state[:], ps_state[:]).then_inc(S["state_done"], 1)
                    return
                dve.wait_ge(S["decay_done"], n)
                dve.tensor_tensor(state[:], decayed[:], ps_state[:], ALU.add).then_inc(S["state_done"], 1)

            def decay(n, chunk):
                dve.wait_ge(S["state_done"], n)
                dve.tensor_tensor(by_head(decayed[:]), by_head(state[:]), spread(f.e_total, chunk, 0),
                                  ALU.mult).then_inc(S["decay_done"], 1)

            def context(c, n, s):
                dve.wait_ge(landed[s], 32)
                weigh(n, s, c)
                if n:
                    decay(n, c)
                advance(n, c)

            def first(c, s):
                dve.wait_ge(S["cb_done"], c + 1)
                dve.wait_ge(S["w_done"], c)
                for d in range(2):
                    dve.tensor_tensor(cb[:, d], ps_cb[:, 0:GROUPS * P].rearrange("p (g t) -> p g t", t=P),
                                      bcast(masks[:, d], [(0, GROUPS), (1, P)]), ALU.mult).then_inc(S["cb_masked"], 1)
                dve.wait_ge(S["diff_f"], c + 1)
                dve.wait_ge(S["diff_b"], c + 1)
                dve.tensor_tensor(sums_f[:, s], sums_f[:, s], sums_b[:, s], ALU.min).then_inc(S["least"], 1)
                dve.wait_ge(S["cb_masked"], 2 * c + 2)
                for h in range(SSD_HEADS):
                    dve.wait_ge(S["w_b"], SSD_HEADS * c + h + 1)
                    dve.scalar_tensor_tensor(w[:, s, h], cb[:, 0, h // HEADS_PER_GROUP],
                                             f.dt[:, c + CTX_TILES, h:h + 1], w[:, s, h], ALU.mult,
                                             ALU.add).then_inc(S["w_sum"], 1)
                dve.wait_ge(S["w_exp"], c + 1)
                dve.wait_ge(S["w_sum"], SSD_HEADS * (c + 1))
                dve.tensor_tensor(w[:, s], w[:, s], sums_f[:, s], ALU.mult).then_inc(S["w_done"], 1)

            def second(c, s):
                n, chunk = c + CTX_TILES, c + CTX_TILES
                rows_here(dve, c, s)
                weigh(n, s, chunk)
                decay(n, chunk)
                dve.wait_ge(S["y_off"], c + 1)
                dve.wait_ge(S["squared"], c)
                dve.wait_ge(S["turned"], 2 * c)
                for g in range(GROUPS):
                    cut = slice(g * GW, (g + 1) * GW)
                    dve.tensor_tensor(by_head(y[:, cut]), by_head(ps_off[:, cut]), spread(f.e_cs, chunk, 0, g),
                                      ALU.mult).then_inc(S["y_a"], 1)
                advance(n, chunk)
                dve.wait_ge(S["y_diag"], c + 1)
                dve.wait_ge(S["y_a"], 2 * c + 2)
                dve.tensor_tensor(y[:], y[:], ps_y[:], ALU.add).then_inc(S["y_b"], 1)
                dve.wait_ge(S["skip_done"], c + 1)
                dve.wait_ge(S["y_b"], c + 1)
                dve.tensor_tensor(y[:], y[:], skip_x[:], ALU.add).then_inc(S["y_c"], 1)
                dve.wait_ge(S["y_c"], c + 1)
                dve.tensor_tensor(y[:], y[:], z[:, s], ALU.mult).then_inc(S["y_gated"], 1)
                for part in range(2):
                    dve.wait_ge(S["hi_done"], 2 * c + part + 1)
                    dve.wait_ge(S["stored_lo"], 16 * c)
                    cut = slice(part * 512, (part + 1) * 512)
                    dve.tensor_tensor(t_lo[:, cut], ps_turn[:], t_hi[:, cut].bitcast(F32),
                                      ALU.subtract).then_inc(S["lo_done"], 1)

            steps(dve, context, first, second)


def stage_attention(nc, sem, io, keep, dram):
    N_G, ODD = N_KV, HEAD_DIM
    CHUNKS = [(0, 1024), (1024, 1024), (2048, TOK - 2048)]
    UNITS = [(0, 4), (4, 4), (8, 4), (12, 4), (16, 2)]
    ON_ACT = (0, 2, 4)
    PAIRS = TILES // 2
    with ExitStack() as ctx:
        def sb(name, shape, dt=F32):
            return ctx.enter_context(nc.sbuf_tensor("at_" + name, shape, dt))

        k_hi, k_lo = sb("k_hi", [P, N_KV, TOK], F32R), sb("k_lo", [P, N_KV, TOK], F32R)
        v = sb("v", [P, TILES, N_KV * HEAD_DIM])
        q = sb("q", [P, 2, Q_PER_KV, P], F32R)
        gate = sb("gate", [P, 2, 2, P])
        prob = sb("prob", [P, 2, TOK])
        prob_t = sb("prob_t", [P, 2, TILES, Q_PER_KV * P])
        top, neg_top = sb("top", [P, 2, 3]), sb("neg_top", [P, 2])
        sums = sb("sums", [P, 2, Q_PER_KV, 3])
        total, recip = sb("total", [P, 2, Q_PER_KV]), sb("recip", [P, 2, Q_PER_KV])
        diag = sb("diag", [P, Q_PER_KV, P])
        halves = sb("halves", [P, Q_PER_KV * P])
        fold, ones = sb("fold", [P, HEAD_DIM]), sb("ones", [P, HEAD_DIM])
        gated, o32 = sb("gated", [P, 2 * P]), sb("o32", [P, 2 * P])
        o_hi, o_lo = sb("o_hi", [P, 2, 2 * P], F32R), sb("o_lo", [P, 2, 2 * P], F32R)
        scores = ctx.enter_context(nc.psum_tensor("at_scores", [P, 5 * 512], F32))
        turn = [ctx.enter_context(nc.psum_tensor(f"at_turn{b}", [P, 512], F32)) for b in range(2)]
        ps_o = ctx.enter_context(nc.psum_tensor("at_ps_o", [P, 512], F32))
        names = ("kv_landed", "consts", "scored", "chunk_top", "top_done", "exp_done", "turned", "act_read",
                 "dve_read", "pv_done", "halves_done", "total_done", "recip_done", "diag_done", "folded",
                 "gated_done", "o32_done", "hi_done", "lo_done", "q_used")
        (kv_landed, consts, scored, chunk_top, top_done, exp_done, turned, act_read, dve_read, pv_done, halves_done,
         total_done, recip_done, diag_done, folded, gated_done, o32_done, hi_done, lo_done, q_used) = [
             sem("at_" + x) for x in names]
        q_landed = [sem(f"at_q_landed{s}") for s in range(2)]
        gate_landed = [sem(f"at_gate_landed{s}") for s in range(2)]
        stored = [sem(f"at_stored{s}") for s in range(2)]
        q_src = dram["q"].rearrange("s (g r) d (n t) -> n g s d r t", r=Q_PER_KV, t=P)
        gate_src = dram["gate"].rearrange("(g j) p (n t) -> n g p j t", j=2, t=P)
        o_dst = dram["ya"].rearrange("s (g j) p (n t) -> s n g p j t", j=2, t=P)
        block = ctx.enter_context(nc.Block())

        class Step:

            def __init__(self, n, g, r):
                self.n, self.g, self.r, self.group, self.head = n, g, r, n * N_G + g, (n * N_G + g) * Q_PER_KV + r
                known = isinstance(n, int)
                heads = LAT_TILES * N_Q
                self.scores = not known or self.head < heads
                self.turn = not known or 1 <= self.head <= heads
                self.pv = not known or 1 <= self.group <= heads // Q_PER_KV
                self.fold = r == 0 and (not known or 2 <= self.group <= heads // Q_PER_KV + 1)
                self.s = r % 2
                self.gs = g % 2

        def steps(eng, body):
            def tile(n):
                for g in range(N_G):
                    for r in range(Q_PER_KV):
                        body(Step(n, g, r))
            tile(0)
            with eng.Fori(1, LAT_TILES) as n:
                tile(n)
            for g in range(2):
                for r in range(Q_PER_KV if g == 0 else 1):
                    body(Step(LAT_TILES, g, r))

        @block.sync
        def _(sync):
            for half in range(2):
                rows = slice(half * HEAD_DIM, (half + 1) * HEAD_DIM)
                for part, dst in ((0, k_hi), (1, k_lo)):
                    sync.dma_start(dst[rows].bitcast(F32), dram["k"][part].rearrange("g d t -> d g t")).then_inc(
                        kv_landed, 16)
            sync.dma_start(v[:], dram["v"].rearrange("t p c -> p t c")).then_inc(kv_landed, 16)

            def body(st):
                if st.scores and st.r == 0:
                    if not isinstance(st.n, int) or st.group >= 2:
                        sync.wait_ge(q_used, st.group - 1)
                    for part in range(2):
                        sync.dma_start(q[part * HEAD_DIM:(part + 1) * HEAD_DIM, st.gs].bitcast(F32),
                                       q_src[st.n, st.g, part]).then_inc(q_landed[st.gs], 16)
                if st.fold:
                    n, g = (st.n, st.g - 2) if st.g >= 2 else (st.n - 1, st.g + 2)
                    for part, done, src in ((0, hi_done, o_hi), (1, lo_done, o_lo)):
                        sync.wait_ge(done, st.group - 1)
                        sync.dma_start(o_dst[part, n, g], src[:, st.gs].bitcast(F32).rearrange(
                            "p (j t) -> p j t", t=P)).then_inc(stored[st.gs], 16)
                if st.scores and st.r == 0:
                    sync.dma_start(gate[:, st.gs], gate_src[st.n, st.g]).then_inc(gate_landed[st.gs], 16)

            steps(sync, body)
            for s in range(2):
                sync.wait_ge(stored[s], 16 * LAT_TILES * N_G)

        @block.tensor
        def _(pe):
            pe.wait_ge(kv_landed, 5 * 16)
            pe.wait_ge(consts, 2)

            def score(st):
                if st.r == 0:
                    pe.wait_ge(q_landed[st.gs], 32 * (st.n * 2 + st.g // 2 + 1))
                for x, (key, width) in enumerate(CHUNKS):
                    if not isinstance(st.n, int) or st.head > 0:
                        pe.wait_ge(exp_done, 3 * (st.head - 1) + x + 1)
                    for at in range(key, key + width, 512):
                        w = min(512, TOK - at)
                        pe.matmul(scores[:, at:at + w], q[:, st.gs, st.r], k_hi[:, st.g, at:at + w],
                                  start=True, stop=False)
                        last = pe.matmul(scores[:, at:at + w], q[:, st.gs, st.r], k_lo[:, st.g, at:at + w],
                                         start=False, stop=True)
                    last.then_inc(scored, 1)
                if st.r == Q_PER_KV - 1:
                    pe.wait_ge(scored, 3 * st.head + 3)
                    pe.sem_inc(q_used, 1)

            def turn_unit(st, u):
                j, (t0, count) = st.head - 1, UNITS[u]
                pe.wait_ge(exp_done, 3 * j + (t0 * P) // 1024 + 1)
                if u in (0, 3):
                    pe.wait_ge(dve_read, 2 * j + (u == 3))
                else:
                    pe.wait_ge(act_read, 3 * j + {1: 0, 2: 1, 4: 2}[u])
                bank, prev = turn[(5 * ((st.g * Q_PER_KV + st.r - 1) % N_Q) + u) % 2], 1 - st.s
                for t in range(t0, t0 + count):
                    last = pe.transpose(bank[:, (t - t0) * P:(t - t0 + 1) * P], prob[:, prev, t * P:(t + 1) * P],
                                        keep["ident"][:])
                last.then_inc(turned, 1)

            def pv_pair(st, pair):
                grp, prev = st.group - 1, 1 - st.gs
                g = (st.g - 1) % N_G
                if pair == 0:
                    pe.wait_ge(act_read, 3 * Q_PER_KV * (grp + 1))
                    pe.wait_ge(dve_read, 2 * Q_PER_KV * (grp + 1))
                    pe.wait_ge(o32_done, grp)
                for odd in range(2):
                    last = pe.matmul(ps_o[odd * ODD:odd * ODD + HEAD_DIM, :],
                                     v[:, 2 * pair + odd, g * HEAD_DIM:(g + 1) * HEAD_DIM],
                                     prob_t[:, prev, 2 * pair + odd], start=(pair == 0), stop=(pair == PAIRS - 1))
                if pair == PAIRS - 1:
                    last.then_inc(pv_done, 1)

            def fold_group(st):
                grp = st.group - 2
                pe.wait_ge(halves_done, grp + 1)
                pe.wait_ge(diag_done, Q_PER_KV * (grp + 1))
                for what, rhs in ((fold, halves), (ones, diag[:].rearrange("p h t -> p (h t)"))):
                    for h in range(Q_PER_KV):
                        rows = slice((h % 2) * ODD, (h % 2) * ODD + HEAD_DIM)
                        at = (what is ones) * 2 * P + (h // 2) * P
                        last = pe.matmul(ps_o[rows, at:at + P], what[:], rhs[:, h * P:(h + 1) * P],
                                         start=True, stop=True)
                last.then_inc(folded, 1)

            def body(st):
                if st.scores:
                    score(st)
                for u in range(len(UNITS)):
                    if st.turn:
                        turn_unit(st, u)
                    if st.pv and st.r >= 1 and u in (0, 2, 4):
                        pv_pair(st, 3 * (st.r - 1) + u // 2)
                if st.fold:
                    fold_group(st)

            steps(pe, body)

        def read_unit(eng, st, u, done):
            j, (t0, count) = st.head - 1, UNITS[u]
            gs = st.gs if st.r else 1 - st.gs
            r = (st.r - 1) % Q_PER_KV
            bank = turn[(5 * ((st.g * Q_PER_KV + st.r - 1) % N_Q) + u) % 2]
            eng.wait_ge(turned, 5 * j + u + 1)
            grp = st.group if st.r else st.group - 1
            if not isinstance(st.n, int) or grp >= 2:
                eng.wait_ge(pv_done, grp - 1)
            dst = prob_t[:, gs, t0:t0 + count, r * P:(r + 1) * P]
            src = bank[:, 0:count * P].rearrange("p (t q) -> p t q", q=P)
            if done is act_read:
                eng.activation(dst, src, ACT.Copy).then_inc(done, 1)
            else:
                eng.tensor_copy(dst, src).then_inc(done, 1)

        @block.scalar
        def _(act):
            def body(st):
                for x, (key, width) in enumerate(CHUNKS):
                    if st.turn:
                        read_unit(act, st, ON_ACT[x], act_read)
                    if st.scores:
                        act.wait_ge(top_done, st.head + 1)
                        act.activation(prob[:, st.s, key:key + width], scores[:, key:key + width], ACT.Exp,
                                       bias=neg_top[:, st.s:st.s + 1],
                                       accum_out=sums[:, st.gs, st.r, x:x + 1]).then_inc(exp_done, 1)

            steps(act, body)

        @block.vector
        def _(dve):
            dve.tensor_tensor(fold[:], keep["ident"][:, 0:HEAD_DIM], keep["ident"][:, HEAD_DIM:P],
                              ALU.add).then_inc(consts, 1)
            dve.memset(ones[:], 1.0).then_inc(consts, 1)

            def maximum(st):
                for x, (key, width) in enumerate(CHUNKS):
                    dve.wait_ge(scored, 3 * st.head + x + 1)
                    dve.tensor_reduce(top[:, st.s, x:x + 1], scores[:, key:key + width], AX.X,
                                      ALU.max).then_inc(chunk_top, 1)
                dve.wait_ge(chunk_top, 3 * st.head + 3)
                if not isinstance(st.n, int) or st.head >= 2:
                    dve.wait_ge(exp_done, 3 * (st.head - 1))
                dve.tensor_reduce(neg_top[:, st.s:st.s + 1], top[:, st.s], AX.X, ALU.max,
                                  negate=True).then_inc(top_done, 1)

            def reciprocals(st):
                grp, gs = st.group - 1, 1 - st.gs
                dve.wait_ge(exp_done, 3 * Q_PER_KV * (grp + 1))
                dve.tensor_reduce(total[:, gs], sums[:, gs], AX.X, ALU.add).then_inc(total_done, 1)
                dve.wait_ge(total_done, grp + 1)
                dve.reciprocal(recip[:, gs], total[:, gs]).then_inc(recip_done, 1)
                dve.wait_ge(recip_done, grp + 1)
                dve.wait_ge(folded, grp)
                for h in range(Q_PER_KV):
                    dve.tensor_scalar(diag[:, h], keep["ident"][:], recip[:, gs, h:h + 1], None,
                                      ALU.mult).then_inc(diag_done, 1)

            def take_halves(st):
                grp = st.group - 2
                dve.wait_ge(pv_done, grp + 1)
                dve.wait_ge(folded, grp)
                dve.tensor_copy(halves[:], ps_o[:]).then_inc(halves_done, 1)

            def finish(st):
                grp, gs = st.group - 2, st.gs
                uses = 16 * (st.n * 2 + st.g // 2)
                dve.wait_ge(folded, grp + 1)
                dve.wait_ge(gate_landed[gs], uses)
                dve.tensor_tensor(gated[:], ps_o[:, 0:2 * P], gate[:, gs].rearrange("p j t -> p (j t)"),
                                  ALU.mult).then_inc(gated_done, 1)
                dve.wait_ge(gated_done, grp + 1)
                dve.wait_ge(lo_done, grp)
                dve.tensor_tensor(o32[:], gated[:], ps_o[:, 2 * P:4 * P], ALU.mult).then_inc(o32_done, 1)
                dve.wait_ge(o32_done, grp + 1)
                dve.wait_ge(stored[gs], 2 * uses - 32)
                split(dve, o32[:], o_hi[:, gs], o_lo[:, gs], hi_done, grp + 1, lo_done)

            def body(st):
                if st.scores:
                    maximum(st)
                if st.fold:
                    take_halves(st)
                for u in (1, 3):
                    if st.turn:
                        read_unit(dve, st, u, dve_read)
                if st.r == 1 and st.pv:
                    reciprocals(st)
                if st.fold:
                    finish(st)

            steps(dve, body)



def stage_out(nc, sem, io, keep, dram, out):
    K2, HALF = 2 * WIDTH // P, 512
    with ExitStack() as ctx:
        def sb(name, shape, dt=F32):
            return ctx.enter_context(nc.sbuf_tensor("ou_" + name, shape, dt))

        w_raw = sb("w_raw", [P, 2, D_MODEL])
        w_hi, w_lo = sb("w_hi", [P, K2, D_MODEL], F32R), sb("w_lo", [P, K2, D_MODEL], F32R)
        gate, final = sb("gate", [P, D_MODEL]), sb("final", [P, D_MODEL])
        yt = sb("yt", [P, 2, 2, K2, P], F32R)
        x, junk = sb("x", [P, 2, D_MODEL]), sb("junk", [P, D_MODEL])
        part, part2 = sb("part", [P, D_MODEL]), sb("part2", [P, D_MODEL])
        rms_y, rstd_y = sb("rms_y", [P, LAT_TILES]), sb("rstd_y", [P, LAT_TILES])
        ss, rms, rstd = sb("ss", [P, 1]), sb("rms", [P, 1]), sb("rstd", [P, 1])
        ps = [[ctx.enter_context(nc.psum_tensor(f"ou_ps{s}{h}", [P, 2 * HALF], F32)) for h in range(2)]
              for s in range(2)]
        names = ("consts", "w_scaled", "w_hi_done", "w_split", "y_rms", "y_rstd", "attn_done", "ssd_done", "part_done",
                 "mixed", "added", "squared", "rms_done", "rstd_done", "normed")
        (consts, w_scaled, w_hi_done, w_split, y_rms, y_rstd, attn_done, ssd_done, part_done, mixed, added, squared,
         rms_done, rstd_done, normed) = [sem("ou_" + a) for a in names]
        w_landed = [sem(f"ou_w_landed{s}") for s in range(2)]
        landed = [sem(f"ou_landed{s}") for s in range(2)]
        stored = [sem(f"ou_stored{s}") for s in range(2)]
        w_src = io["w_out"].rearrange("o (k p) c -> (o k) p c", p=P)
        srcs = [dram[a].rearrange("s m p (n t) -> n s p m t", t=P) for a in ("ya", "ys")]
        x_src = io["x"].rearrange("o (n p) d -> (o n) p d", p=P)
        out_dst = out.rearrange("o (n p) d -> (o n) p d", p=P)
        block = ctx.enter_context(nc.Block())

        def tiles(eng, body):
            with eng.Fori(0, LAT_TILES - 1, 2) as i:
                for u in range(2):
                    body(i + u, u)

        @block.sync
        def _(sync):
            sync.dma_start(gate[:], keep["gate_dram"].unsqueeze(0).broadcast_to([P, D_MODEL])).then_inc(consts, 16)
            sync.dma_start(final[:], io["final_g"].unsqueeze(0).broadcast_to([P, D_MODEL])).then_inc(consts, 16)
            for k in range(K2):
                if k >= 2:
                    sync.wait_ge(w_split, k - 1)
                sync.dma_start(w_raw[:, k % 2], w_src[k]).then_inc(w_landed[k % 2], 16)

        @block.gpsimd
        def _(pool):
            def load(n, s):
                pool.wait_ge(ssd_done, n + 1)
                pool.wait_ge(stored[s], 8 * (n - s))
                for half, src in enumerate(srcs):
                    for a in range(2):
                        pool.dma_start(yt[:, s, a, half * KD:(half + 1) * KD].bitcast(F32), src[n, a]).then_inc(
                            landed[s], 16)
                pool.dma_start(x[:, s], x_src[n]).then_inc(landed[s], 16)

            tiles(pool, load)

        @block.tensor
        def _(pe):
            pe.sem_inc(ssd_done, 2)

            def body(n, s):
                pe.wait_ge(landed[s], 40 * (n - s) + 80)
                pe.wait_ge(mixed, n + 1)
                for half in range(2):
                    for k in range(half * KD, (half + 1) * KD):
                        pe.wait_ge(w_split, k + 1)
                        for a, w in ((0, w_hi), (0, w_lo), (1, w_hi)):
                            for c in range(2):
                                last = pe.matmul(ps[s][half][:, c * HALF:(c + 1) * HALF], yt[:, s, a, k],
                                                 w[:, k, c * HALF:(c + 1) * HALF],
                                                 start=(k % KD == 0 and a == 0 and w is w_hi),
                                                 stop=(k % KD == KD - 1 and a == 1))
                    last.then_inc((attn_done, ssd_done)[half], 1)

            tiles(pe, body)

        @block.scalar
        def _(act):
            act.activation(rms_y[:], keep["ss_y"][:], ACT.Sqrt, scale=1.0 / WIDTH, bias=keep["eps"][:]).then_inc(
                y_rms, 1)

            def body(n, s):
                act.wait_ge(attn_done, n + 1)
                act.wait_ge(mixed, n + 2)
                act.activation(part[:], ps[s][0][:], ACT.Copy).then_inc(part_done, 1)
                act.wait_ge(added, n + 3)
                act.wait_ge(squared, n)
                act.activation(junk[:], x[:, s], ACT.Square, accum_out=ss[:]).then_inc(squared, 1)
                act.wait_ge(squared, n + 1)
                act.wait_ge(rstd_done, n)
                act.activation(rms[:], ss[:], ACT.Sqrt, scale=1.0 / D_MODEL, bias=keep["eps"][:]).then_inc(
                    rms_done, 1)
                act.wait_ge(normed, n + 1)
                act.dma_start(out_dst[n], x[:, s]).then_inc(stored[s], 16)

            tiles(act, body)
            for s in range(2):
                act.wait_ge(stored[s], 16 * LAT_TILES // 2)

        @block.vector
        def _(dve):
            dve.sem_inc(mixed, 2)
            dve.sem_inc(added, 2)
            dve.wait_ge(consts, 32)
            for k in range(K2):
                dve.wait_ge(w_landed[k % 2], 16 * (k // 2 + 1))
                raw = w_raw[:, k % 2]
                if k < KD:
                    dve.tensor_tensor(raw, raw, gate[:], ALU.mult).then_inc(w_scaled, 1)
                else:
                    row = ROW_SSDG + k - KD
                    dve.scalar_tensor_tensor(raw, raw, keep["cols"][:, row:row + 1], gate[:], ALU.mult,
                                             ALU.mult).then_inc(w_scaled, 1)
                dve.wait_ge(w_scaled, k + 1)
                split(dve, raw, w_hi[:, k], w_lo[:, k], w_hi_done, k + 1, w_split)
            dve.wait_ge(y_rms, 1)
            dve.reciprocal(rstd_y[:], rms_y[:]).then_inc(y_rstd, 1)
            dve.wait_ge(y_rstd, 1)

            def body(n, s):
                dve.wait_ge(part_done, n + 1)
                dve.wait_ge(ssd_done, n + 3)
                dve.wait_ge(added, n + 2)
                dve.scalar_tensor_tensor(part2[:], ps[s][1][:], rstd_y[:, bass.ds(n, 1)], part[:], ALU.mult,
                                         ALU.add).then_inc(mixed, 1)
                dve.wait_ge(mixed, n + 3)
                dve.wait_ge(landed[s], 40 * (n - s) + 80)
                dve.tensor_tensor(x[:, s], x[:, s], part2[:], ALU.add).then_inc(added, 1)
                dve.wait_ge(rms_done, n + 1)
                dve.reciprocal(rstd[:], rms[:]).then_inc(rstd_done, 1)
                dve.wait_ge(rstd_done, n + 1)
                dve.scalar_tensor_tensor(x[:, s], x[:, s], rstd[:], final[:], ALU.mult, ALU.mult).then_inc(normed, 1)

            tiles(dve, body)


def build(nc, io, out):
    with ExitStack() as ctx:
        made = []

        def sem(name):
            made.append(nc.alloc_semaphore(name=name))
            return made[-1]

        def reuse_semaphores():
            nc.clear_and_free_semaphores(made)
            made.clear()
            nc.all_engine_barrier()

        def sb(name, shape, dt=F32):
            return ctx.enter_context(nc.sbuf_tensor(name, shape, dt))

        def scratch(name, shape):
            return nc.dram_tensor(name, shape, F32).ap()

        NH = 2 * SSD_HEADS
        dram = {
            "xbc": scratch("xbc_t", [XBC_TILES, P, TOK]), "gate": scratch("gate_t", [WIDTH // P, P, SEQ]),
            "z": scratch("z_rows", [LAT_TILES, P, WIDTH]), "v": scratch("v_rows", [TILES, P, N_KV * HEAD_DIM]),
            "k": scratch("k_t", [2, N_KV, HEAD_DIM, TOK]), "q": scratch("q_t", [2, N_Q, HEAD_DIM, SEQ]),
            "cs": scratch("cs_rows", [NH, TOK]), "dtcols": scratch("dt_factors", [P, 5 * TILES * NH]),
            "x": scratch("x_rows", [TILES, P, WIDTH]), "b": scratch("b_rows", [TILES, P, GROUPS * D_STATE]),
            "yb": scratch("yb_rows", [LAT_TILES, P, WIDTH]),
            "ys": scratch("ys_t", [2, WIDTH // P, P, SEQ]), "ya": scratch("ya_t", [2, WIDTH // P, P, SEQ]),
        }
        keep = {"ident": sb("ident", [P, P]), "cols": sb("cols", [P, P]), "shift": sb("shift", [P, 2, KD]),
                "scale": sb("scale", [P, 2, KD]), "eps": sb("eps", [P, 1]), "one": sb("one", [P, 1]),
                "pick": sb("pick", [P, 2, P]), "ss_y": sb("ss_y", [P, LAT_TILES]),
                "gate_dram": scratch("gate_vec", [D_MODEL])}
        stage_modulation(nc, sem, io, keep)
        with ExitStack() as hs:
            h_hi = hs.enter_context(nc.sbuf_tensor("h_hi", [P, KD, TOK], F32R))
            h_lo = hs.enter_context(nc.sbuf_tensor("h_lo", [P, KD, TOK], F32R))
            stage_hidden(nc, sem, io, keep, h_hi, h_lo)
            stage_dt(nc, sem, io, keep, h_hi, h_lo, dram)
            stage_channels(nc, sem, io, keep, h_hi, h_lo, dram)
            w_in = io["w_in"].rearrange("o (k p) c -> p (o k) c", p=P)
            lat, every = list(range(CTX_TILES, TILES)), list(range(TILES))
            n_blocks = WIDTH // COLS_W
            w_q = w_in[:, :, OFF_Q:OFF_Q + WIDTH + COLS_W].rearrange("p k (b c) -> p b k c", c=COLS_W)
            w_z = w_in[:, :, OFF_Z - COLS_W:OFF_Z + WIDTH].rearrange("p k (b c) -> p b k c", c=COLS_W)
            k_dst = dram["k"].rearrange("s (j g) d t -> s (g d) j t", g=2)
            q_dst = dram["q"].rearrange("s (b j g) d (n t) -> s b n (g d) j t", j=HPB // 2, g=2, t=P)
            z_dst = dram["z"].rearrange("n p (b c) -> n b p c", c=COLS_W)
            stage_heads(nc, sem, io, keep, h_hi, h_lo, "k_", lambda b: w_in[:, :, 0:COLS_W], 1, every,
                        "k_norm_g", 1.0, lambda s, b, i: k_dst[s, :, :, i * P:(i + 1) * P])
            stage_plain(nc, sem, h_hi, h_lo, "v_", lambda b: w_in[:, :, COLS_W:2 * COLS_W], 1, every,
                        ACT.Copy, lambda b, i: dram["v"][i])
            stage_heads(nc, sem, io, keep, h_hi, h_lo, "q_", lambda b: w_q[:, b], n_blocks, lat,
                        "q_norm_g", HEAD_DIM ** -0.5, lambda s, b, i: q_dst[s, b, i])
            stage_plain(nc, sem, h_hi, h_lo, "z_", lambda b: w_z[:, b * -1 + n_blocks], n_blocks, lat,
                        ACT.Silu, lambda b, i: z_dst[i, b * -1 + (n_blocks - 1)])
        reuse_semaphores()
        with ExitStack() as ss:
            cols = ss.enter_context(nc.sbuf_tensor("ssd_cols", [P, 5, TILES, NH], F32))
            stage_ssd_backward(nc, sem, io, keep, dram, cols)
            stage_ssd_forward(nc, sem, io, keep, dram, cols)
        reuse_semaphores()
        stage_attention(nc, sem, io, keep, dram)
        stage_out(nc, sem, io, keep, dram, out)


def constants():
    ident = np.eye(P, dtype=np.float32)
    s, l = np.arange(P)[:, None], np.arange(P)[None]
    pick = np.zeros((2, P, P), np.float32)
    pick[0, P - 1], pick[1, 0] = 1, 1
    masks = np.stack([s <= l, s >= l]).astype(np.float32)
    nf = HEAD_DIM // 4
    t = np.arange(SEQ)
    freq = (10000.0 ** (-np.arange(nf, dtype=np.float32) / np.float32(nf))).astype(np.float32)
    pos = np.stack([t // GRID_W, t % GRID_W], 1).astype(np.float32)
    ang = pos[:, :, None] * freq
    rope = np.zeros((2, TOK, 2, 2, nf), np.float32)
    rope[0] = 1
    rope[0, CTX:] = np.cos(ang)[:, :, None]
    rope[1, CTX:] = np.sin(ang)[:, :, None] * np.array([-1, 1], np.float32)[None, None, :, None]
    rope = rope.reshape(2, TILES, P, HEAD_DIM).transpose(2, 0, 1, 3)
    return {"ident": ident, "pick": pick.transpose(1, 0, 2), "masks": masks.transpose(1, 0, 2), "rope": rope}


_INPUTS = ["x", "c", "ctx", "c_ctx", "ada_w", "ada_b", "norm_g", "w_in", "conv_w", "conv_b", "dt_bias", "a_log",
           "d_skip", "q_norm_g", "k_norm_g", "ssd_norm_g", "w_out", "final_g"]


def kernel(**inputs):
    import numpy as _np
    import concourse.bacc as _bacc
    from concourse import mybir as _mybir
    from concourse.bass_utils import run_bass_kernel_spmd as _run

    nc = _bacc.Bacc("TRN2", target_bir_lowering=False, num_devices=1)
    given = {name: inputs[name] for name in _INPUTS}
    given.update(constants())
    arrays, io = {}, {}
    for name, value in given.items():
        a = _np.ascontiguousarray(value)
        arrays[f"in_{name}_dram"] = a
        io[name] = nc.dram_tensor(f"in_{name}_dram", a.shape, _mybir.dt.from_np(a.dtype), kind="ExternalInput").ap()
    out = nc.dram_tensor("out_0_dram", (1, SEQ, D_MODEL), F32, kind="ExternalOutput").ap()
    build(nc, io, out)
    r = _run(nc, [arrays], core_ids=[0])
    return r.results[0]["out_0_dram"]
```

```python
from contextlib import ExitStack

import numpy as np

import concourse.bass as bass
from concourse import mybir

P = 128
D_MODEL = 1024
SEQ = 2048
CTX = 256
TOK = CTX + SEQ
GRID_W = 64
HEAD_DIM = 64
N_Q = 16
N_KV = 4
Q_PER_KV = N_Q // N_KV
SSD_HEADS = 16
GROUPS = 2
HEADS_PER_GROUP = SSD_HEADS // GROUPS
D_STATE = 128
D_CONV = 5
EPS = 1e-6
WIDTH = 1024
KD = D_MODEL // P
CTX_TILES = CTX // P
LAT_TILES = SEQ // P
TILES = TOK // P
XBC_TILES = (WIDTH + 2 * GROUPS * D_STATE) // P
OFF_XBC = 2 * N_KV * HEAD_DIM
OFF_Q = OFF_XBC + XBC_TILES * P + 2 * SSD_HEADS
OFF_G = OFF_Q + WIDTH
OFF_Z = OFF_G + WIDTH
PAD = D_CONV // 2
COLS_W = 256
HPB = COLS_W // HEAD_DIM
BLOCKS = [(0, CTX)] + [(CTX + 512 * i, 512) for i in range(SEQ // 512)]

F32 = mybir.dt.float32
F32R = mybir.dt.float32r
ALU = mybir.AluOpType
ACT = mybir.ActivationFunctionType
AX = mybir.AxisListType

ROW_C, ROW_CCTX, ROW_NORM, ROW_CONVW = 0, KD, 2 * KD, 3 * KD
ROW_CONVB = ROW_CONVW + D_CONV * XBC_TILES
ROW_ADAB = ROW_CONVB + XBC_TILES
ROW_SSDG = ROW_ADAB + 3 * KD


def bcast(ap, dims):
    return bass.AP(tensor=ap.tensor, offset=ap.offset, ap=[list(ap.ap[0])] + [list(d) for d in dims])


def stage_modulation(nc, sem, io, keep):
    with ExitStack() as ctx:
        def sb(name, shape, dt=F32):
            return ctx.enter_context(nc.sbuf_tensor(name, shape, dt))

        SLOTS, CW = 3, 512
        CHUNKS = 3 * D_MODEL // CW
        rows = sb("rows", [P, P])
        silu_c = sb("silu_c", [P, 2, KD])
        ada = sb("ada", [P, SLOTS, KD, CW])
        mod = sb("mod", [P, 3 * KD, 2])
        ps_cols = ctx.enter_context(nc.psum_tensor("ps_cols", [P, 512], F32))
        ps_mod = ctx.enter_context(nc.psum_tensor("ps_mod", [P, 512], F32))
        mod_psum = ps_mod[:, 0:2 * 3 * KD].rearrange("p (m j) -> p m j", j=2)
        rows_landed, ident_landed = sem("rows_landed"), sem("ident_landed")
        ada_landed = [sem(f"ada_landed{s}") for s in range(SLOTS)]
        ada_used, cols_turned, cols_ready = sem("ada_used"), sem("cols_turned"), sem("cols_ready")
        c_ready, mod_summed, mod_ready = sem("c_ready"), sem("mod_summed"), sem("mod_ready")
        vecs_ready, gate_stored = sem("vecs_ready"), sem("gate_stored")
        ada_w = io["ada_w"].rearrange("o (k p) (m c) -> p (o k) m c", p=P, c=CW)
        block = ctx.enter_context(nc.Block())

        @block.sync
        def _(sync):
            sync.dma_start(keep["ident"][:], io["ident"]).then_inc(ident_landed, 16)
            sync.dma_start(keep["pick"][:], io["pick"]).then_inc(ident_landed, 16)
            for row, name, view in ((ROW_C, "c", "o (r p) -> (o r) p"), (ROW_CCTX, "c_ctx", "(r p) -> r p"),
                                    (ROW_NORM, "norm_g", "o (r p) -> (o r) p"),
                                    (ROW_CONVW, "conv_w", "o k (r p) -> (o k r) p"),
                                    (ROW_CONVB, "conv_b", "o (r p) -> (o r) p"),
                                    (ROW_ADAB, "ada_b", "o (r p) -> (o r) p"),
                                    (ROW_SSDG, "ssd_norm_g", "o (r p) -> (o r) p")):
                src = io[name].rearrange(view, p=P)
                sync.dma_start(rows[row:row + src.shape[0], :], src).then_inc(rows_landed, 16)
            for n in range(CHUNKS):
                if n >= SLOTS:
                    sync.wait_ge(ada_used, n - SLOTS + 1)
                sync.dma_start(ada[:, n % SLOTS], ada_w[:, :, n]).then_inc(ada_landed[n % SLOTS], 16)
            sync.wait_ge(mod_ready, 1)
            sync.dma_start(keep["gate_dram"].rearrange("(k p) -> p k", p=P),
                           mod[:, 2 * KD:3 * KD, 0], allow_slow_non_contiguous=True).then_inc(gate_stored, 16)
            sync.wait_ge(gate_stored, 16)

        @block.tensor
        def _(pe):
            pe.wait_ge(rows_landed, 7 * 16)
            pe.wait_ge(ident_landed, 32)
            pe.transpose(ps_cols[:, 0:P], rows[:], keep["ident"][:]).then_inc(cols_turned, 1)
            pe.wait_ge(c_ready, 1)
            for n in range(CHUNKS):
                pe.wait_ge(ada_landed[n % SLOTS], 16 * (n // SLOTS + 1))
                for j in range(CW // P):
                    for k in range(KD):
                        last = pe.matmul(mod_psum[:, n * (CW // P) + j, :],
                                         ada[:, n % SLOTS, k, j * P:(j + 1) * P], silu_c[:, :, k],
                                         start=(k == 0), stop=(k == KD - 1))
                last.then_inc(ada_used, 1)

        @block.scalar
        def _(act):
            act.wait_ge(cols_ready, 1)
            act.activation(silu_c[:].rearrange("p j k -> p (j k)"), keep["cols"][:, 0:2 * KD],
                           ACT.Silu).then_inc(c_ready, 1)

        @block.vector
        def _(dve):
            dve.memset(keep["eps"][:], EPS).then_inc(vecs_ready, 1)
            dve.memset(keep["one"][:], 1.0).then_inc(vecs_ready, 1)
            dve.wait_ge(cols_turned, 1)
            dve.tensor_copy(keep["cols"][:], ps_cols[:, 0:P]).then_inc(cols_ready, 1)
            dve.wait_ge(cols_ready, 1)
            dve.wait_ge(ada_used, CHUNKS)
            bias = keep["cols"][:, ROW_ADAB:ROW_ADAB + 3 * KD]
            dve.tensor_tensor(mod[:], mod_psum, bcast(bias, [(1, 3 * KD), (0, 2)]), ALU.add).then_inc(mod_ready, 1)
            dve.wait_ge(mod_ready, 1)
            for j in range(2):
                dve.tensor_copy(keep["shift"][:, j], mod[:, 0:KD, j]).then_inc(vecs_ready, 1)
                dve.scalar_tensor_tensor(keep["scale"][:, j], mod[:, KD:2 * KD, j], 1.0,
                                         keep["cols"][:, ROW_NORM:ROW_NORM + KD], ALU.add,
                                         ALU.mult).then_inc(vecs_ready, 1)


def split(dve, w_raw, w_hi, w_lo, hi_done, count, lo_done):
    dve.tensor_copy(w_hi, w_raw).then_inc(hi_done, 1)
    dve.wait_ge(hi_done, count)
    dve.tensor_tensor(w_lo, w_raw, w_hi.bitcast(F32), ALU.subtract).then_inc(lo_done, 1)


def stage_hidden(nc, sem, io, keep, h_hi, h_lo):
    with ExitStack() as ctx:
        def sb(name, shape, dt=F32):
            return ctx.enter_context(nc.sbuf_tensor(name, shape, dt))

        GT = 4
        xin = sb("xin", [P, 2, GT, D_MODEL])
        junk = sb("junk", [P, D_MODEL])
        ss = sb("ss", [P, 2, GT])
        rms, rstd = sb("rms", [P, 2, GT]), sb("rstd", [P, 2, GT])
        h32 = sb("h32", [P, 2, 512])
        ps_x = [ctx.enter_context(nc.psum_tensor(f"ps_x{b}", [P, 512], F32)) for b in range(4)]
        x_landed = [sem(f"x_landed{s}") for s in range(2)]
        x_squared, x_rms, x_rstd, x_normed, x_turned = (sem("x_squared"), sem("x_rms"), sem("x_rstd"),
                                                        sem("x_normed"), sem("x_turned"))
        h_full, h_hi_done, h_lo_done, x_free = sem("h_full"), sem("h_hi_done"), sem("h_lo_done"), sem("x_free")
        x_lat = io["x"].rearrange("o (g t p) d -> p (o g) t d", p=P, t=GT)
        x_ctx = io["ctx"].rearrange("o (t p) d -> p (o t) d", p=P)
        groups = [(CTX_TILES, 0, 1)] + [(GT, CTX + 512 * g, 0) for g in range(SEQ // 512)]
        block = ctx.enter_context(nc.Block())

        @block.sync
        def _(sync):
            for g, (tiles, tok, which) in enumerate(groups):
                if g >= 2:
                    sync.wait_ge(x_turned, KD * (g - 1))
                src = x_ctx if g == 0 else x_lat[:, g - 1]
                sync.dma_start(xin[:, g % 2, 0:tiles], src).then_inc(x_landed[g % 2], 16)

        @block.scalar
        def _(act):
            def norms(g):
                tiles = groups[g][0]
                act.wait_ge(x_landed[g % 2], 16 * (g // 2 + 1))
                for t in range(tiles):
                    if g or t:
                        act.wait_ge(x_squared, sum(x[0] for x in groups[:g]) + t)
                    if g >= 2 and t == 0:
                        act.wait_ge(x_rms, g - 1)
                    act.activation(junk[:], xin[:, g % 2, t], ACT.Square,
                                   accum_out=ss[:, g % 2, t:t + 1]).then_inc(x_squared, 1)
                act.wait_ge(x_squared, sum(x[0] for x in groups[:g + 1]))
                if g >= 2:
                    act.wait_ge(x_normed, sum(x[0] for x in groups[:g - 1]))
                act.activation(rms[:, g % 2, 0:tiles], ss[:, g % 2, 0:tiles], ACT.Sqrt, scale=1.0 / D_MODEL,
                               bias=keep["eps"][:]).then_inc(x_rms, 1)

            norms(0)
            for g, (tiles, tok, which) in enumerate(groups):
                if g + 1 < len(groups):
                    norms(g + 1)
                for k in range(KD):
                    n = g * KD + k
                    act.wait_ge(x_turned, n + 1)
                    if n >= 2:
                        act.wait_ge(h_lo_done, n - 1)
                    act.activation(h32[:, n % 2, 0:tiles * P], ps_x[n % 4][:, 0:tiles * P], ACT.Identity,
                                   bias=keep["shift"][:, which, k:k + 1],
                                   scale=keep["scale"][:, which, k:k + 1]).then_inc(h_full, 1)

        @block.vector
        def _(dve):
            def normalise(g):
                dve.wait_ge(x_rms, g + 1)
                dve.reciprocal(rstd[:, g % 2, 0:groups[g][0]], rms[:, g % 2, 0:groups[g][0]]).then_inc(x_rstd, 1)
                dve.wait_ge(x_rstd, g + 1)
                for t in range(groups[g][0]):
                    dve.tensor_scalar(xin[:, g % 2, t], xin[:, g % 2, t], rstd[:, g % 2, t:t + 1], None,
                                      ALU.mult).then_inc(x_normed, 1)

            normalise(0)
            for g, (tiles, tok, which) in enumerate(groups):
                if g + 1 < len(groups):
                    normalise(g + 1)
                for k in range(KD):
                    n = g * KD + k
                    dve.wait_ge(h_full, n + 1)
                    split(dve, h32[:, n % 2, 0:tiles * P], h_hi[:, k, tok:tok + tiles * P],
                          h_lo[:, k, tok:tok + tiles * P], h_hi_done, n + 1, h_lo_done)

        @block.tensor
        def _(pe):
            for g, (tiles, tok, which) in enumerate(groups):
                pe.wait_ge(x_normed, sum(x[0] for x in groups[:g + 1]))
                for k in range(KD):
                    n = g * KD + k
                    if n >= 4:
                        pe.wait_ge(h_full, n - 3)
                    for t in range(tiles):
                        last = pe.transpose(ps_x[n % 4][:, t * P:(t + 1) * P], xin[:, g % 2, t, k * P:(k + 1) * P],
                                            keep["ident"][:])
                    last.then_inc(x_turned, 1)



RING = 2


class TokenMajor:

    def __init__(self, nc, sem, ctx, tag, src, count, tiles):
        self.src, self.count, self.tiles, self.n_tiles = src, count, tiles, len(tiles)

        def sb(name, shape, dt=F32):
            return ctx.enter_context(nc.sbuf_tensor(f"{tag}_{name}", shape, dt))

        self.w_raw = sb("w_raw", [P, KD, COLS_W])
        self.w_hi = sb("w_hi", [P, 2, KD, COLS_W], F32R)
        self.w_lo = sb("w_lo", [P, 2, KD, COLS_W], F32R)
        self.acc = [ctx.enter_context(nc.psum_tensor(f"{tag}_acc{b}", [P, 512], F32)) for b in range(4)]
        self.w_landed, self.w_hi_done, self.w_split = sem(tag + "w_landed"), sem(tag + "w_hi_done"), sem(tag + "w_split")
        self.w_used, self.acc_done, self.acc_free = sem(tag + "w_used"), sem(tag + "acc_done"), sem(tag + "acc_free")

    def blocks(self, eng, body):
        if self.count == 1:
            body(0, 0)
            return
        with eng.Fori(0, self.count - 1, 2) as i:
            for u in range(2):
                body(i + u, u)

    def load(self, sync, b):
        sync.wait_ge(self.w_split, b)
        sync.dma_start(self.w_raw[:], self.src(b)).then_inc(self.w_landed, 16)

    def split(self, dve, b, slot):
        dve.wait_ge(self.w_landed, (b + 1) * 16)
        dve.wait_ge(self.w_used, b + 1)
        split(dve, self.w_raw[:], self.w_hi[:, slot], self.w_lo[:, slot], self.w_hi_done, b + 1, self.w_split)

    def products(self, pe, h_hi, h_lo, b, slot, i):
        n, bank = b * self.n_tiles + i, self.acc[i % 4][:, 0:COLS_W]
        tok = slice(self.tiles[i] * P, (self.tiles[i] + 1) * P)
        if i == 0:
            pe.wait_ge(self.w_split, b + 1)
        pe.wait_ge(self.acc_free, n + 1)
        for k in range(KD):
            pe.matmul(bank, h_hi[:, k, tok], self.w_hi[:, slot, k], start=(k == 0), stop=False)
            pe.matmul(bank, h_hi[:, k, tok], self.w_lo[:, slot, k], start=False, stop=False)
            last = pe.matmul(bank, h_lo[:, k, tok], self.w_hi[:, slot, k], start=False, stop=(k == KD - 1))
        last.then_inc(self.acc_done, 1)

    def used(self, pe):
        pe.drain().then_inc(self.w_used, 1)


def stage_plain(nc, sem, h_hi, h_lo, tag, src, count, tiles, func, dst):
    with ExitStack() as ctx:
        tm = TokenMajor(nc, sem, ctx, tag, src, count, tiles)
        out = ctx.enter_context(nc.sbuf_tensor(f"{tag}_out", [P, RING, COLS_W], F32))
        stored = [sem(f"{tag}stored{s}") for s in range(RING)]
        block = ctx.enter_context(nc.Block())
        nt = len(tiles)

        @block.sync
        def _(sync):
            tm.load(sync, 0)

            def body(b, slot):
                if count > 1:
                    tm.load(sync, b + 1)
                for i in range(nt):
                    sync.wait_ge(tm.acc_free, b * nt + i + 5)
                    sync.dma_start(dst(b, i), out[:, i % RING]).then_inc(stored[i % RING], 16)

            tm.blocks(sync, body)
            for s in range(RING):
                sync.wait_ge(stored[s], 16 * count * nt // RING)

        @block.tensor
        def _(pe):
            def body(b, slot):
                for i in range(nt):
                    tm.products(pe, h_hi, h_lo, b, slot, i)
                tm.used(pe)

            tm.blocks(pe, body)

        @block.scalar
        def _(act):
            act.sem_inc(tm.acc_free, 4)

            def body(b, slot):
                for i in range(nt):
                    n, s = b * nt + i, i % RING
                    act.wait_ge(tm.acc_done, n + 1)
                    act.wait_ge(stored[s], 16 * (b * (nt // RING) + i // RING))
                    act.activation(out[:, s], tm.acc[i % 4][:, 0:COLS_W], func).then_inc(tm.acc_free, 1)

            tm.blocks(act, body)

        @block.vector
        def _(dve):
            dve.sem_inc(tm.w_used, RING)
            tm.split(dve, 0, 0)
            if count > 1:
                tm.blocks(dve, lambda b, slot: tm.split(dve, b + 1, 1 - slot))


def stage_heads(nc, sem, io, keep, h_hi, h_lo, tag, src, count, tiles, gain, gain_scale, dst):
    with ExitStack() as ctx:
        def sb(name, shape, dt=F32):
            return ctx.enter_context(nc.sbuf_tensor(f"{tag}_{name}", shape, dt))

        tm = TokenMajor(nc, sem, ctx, tag, src, count, tiles)
        turn = [ctx.enter_context(nc.psum_tensor(f"{tag}_turn{b}", [P, 512], F32)) for b in range(RING)]
        rope = sb("rope", [P, 2, TILES, HEAD_DIM])
        gains = sb("gains", [P, 2, HEAD_DIM])
        sq, raw = sb("sq", [P, RING, COLS_W]), sb("raw", [P, RING, COLS_W])
        r1, r2 = sb("r1", [P, RING, COLS_W]), sb("r2", [P, RING, COLS_W])
        t_hi, t_lo = sb("t_hi", [P, RING, COLS_W], F32R), sb("t_lo", [P, RING, COLS_W], F32R)
        hss, hrms, hrstd = sb("hss", [P, RING, HPB]), sb("hrms", [P, RING, HPB]), sb("hrstd", [P, RING, HPB])
        names = ("sq_done", "hss_done", "rms_done", "rstd_done", "n_done", "r1_done", "r2_done", "rot_done",
                 "turned", "hi_done", "lo_free", "raw_free", "sq_free", "tables_landed", "tables_scaled")
        (sq_done, hss_done, rms_done, rstd_done, n_done, r1_done, r2_done, rot_done, turned, hi_done, lo_free,
         raw_free, sq_free, tables_landed, tables_scaled) = [sem(f"{tag}{x}") for x in names]
        hi_stored, lo_stored = [sem(f"{tag}hi_st{s}") for s in range(RING)], [sem(f"{tag}lo_st{s}") for s in range(RING)]
        nt = len(tiles)
        QUARTER = HEAD_DIM // 4

        def heads(x):
            return x.rearrange("p (h d) -> p h d", d=HEAD_DIM)

        def quarters(x, half):
            return x.rearrange("p (a f d) -> p a f d", f=2, d=QUARTER)[:, :, half]

        block = ctx.enter_context(nc.Block())

        @block.sync
        def _(sync):
            tm.load(sync, 0)
            sync.dma_start(rope[:], io["rope"]).then_inc(tables_landed, 16)
            sync.dma_start(gains[:, 0], io[gain].broadcast_to([P, HEAD_DIM])).then_inc(tables_landed, 16)
            swap = io[gain].rearrange("o (a f d) -> o a f d", f=2, d=QUARTER)
            for half in range(2):
                sync.dma_start(quarters(gains[:, 1], half),
                               swap[:, :, 1 - half].broadcast_to([P, 2, QUARTER])).then_inc(tables_landed, 16)

            def body(b, slot):
                if count > 1:
                    tm.load(sync, b + 1)
                for i in range(nt):
                    n = b * nt + i
                    sync.wait_ge(hi_done, n + 1)
                    sync.dma_start(dst(0, b, i), t_hi[:, i % RING].bitcast(F32).rearrange(
                        "p (j t) -> p j t", t=P)).then_inc(hi_stored[i % RING], 16)
                    sync.wait_ge(lo_free, n + 1 + RING)
                    sync.dma_start(dst(1, b, i), t_lo[:, i % RING].bitcast(F32).rearrange(
                        "p (j t) -> p j t", t=P)).then_inc(lo_stored[i % RING], 16)

            tm.blocks(sync, body)
            for s in range(RING):
                sync.wait_ge(hi_stored[s], 16 * count * nt // RING)
                sync.wait_ge(lo_stored[s], 16 * count * nt // RING)

        @block.tensor
        def _(pe):
            pe.sem_inc(turned, RING)

            def turn_tile(b, i):
                n, s = b * nt + i, i % RING
                pe.wait_ge(rot_done, n + 1)
                pe.wait_ge(lo_free, n + 1)
                for j in range(COLS_W // P):
                    last = pe.transpose(turn[s][:, j * P:(j + 1) * P], r1[:, s, j * P:(j + 1) * P], keep["ident"][:])
                last.then_inc(turned, 1)

            def body(b, slot):
                for i in range(nt):
                    tm.products(pe, h_hi, h_lo, b, slot, i)
                    if i >= 2:
                        turn_tile(b, i - 2)
                tm.used(pe)
                turn_tile(b, nt - 2)
                turn_tile(b, nt - 1)

            tm.blocks(pe, body)

        @block.scalar
        def _(act):
            act.sem_inc(tm.acc_free, 4)

            def take(b, i):
                n, s = b * nt + i, i % RING
                act.wait_ge(tm.acc_done, n + 1)
                act.wait_ge(sq_free, n + 1)
                act.activation(sq[:, s], tm.acc[i % 4][:, 0:COLS_W], ACT.Square).then_inc(sq_done, 1)
                act.wait_ge(raw_free, n + 1)
                act.activation(raw[:, s], tm.acc[i % 4][:, 0:COLS_W], ACT.Copy).then_inc(tm.acc_free, 1)

            def rms(b, i):
                n, s = b * nt + i, i % RING
                act.wait_ge(hss_done, n + 1)
                act.activation(hrms[:, s], hss[:, s], ACT.Sqrt, scale=1.0 / HEAD_DIM, bias=keep["eps"][:]).then_inc(
                    rms_done, 1)

            def hi(b, i):
                n, s = b * nt + i, i % RING
                act.wait_ge(turned, n + 1 + RING)
                act.wait_ge(hi_stored[s], 16 * (b * (nt // RING) + i // RING))
                act.activation(t_hi[:, s], turn[s][:, 0:COLS_W], ACT.Copy).then_inc(hi_done, 1)

            def body(b, slot):
                for i in range(nt + 3):
                    if i < nt:
                        take(b, i)
                    if 1 <= i <= nt:
                        rms(b, i - 1)
                    if i >= 3:
                        hi(b, i - 3)

            tm.blocks(act, body)

        @block.gpsimd
        def _(pool):
            pool.wait_ge(tables_scaled, 3)

            def body(b, slot):
                for i in range(nt):
                    n, s = b * nt + i, i % RING
                    pool.wait_ge(n_done, n + 1)
                    pool.wait_ge(turned, n + 1)
                    pool.tensor_tensor(heads(r1[:, s]), heads(raw[:, s]),
                                       bcast(rope[:, 0, tiles[i]], [(0, HPB), (1, HEAD_DIM)]),
                                       ALU.mult).then_inc(r1_done, 1)

            tm.blocks(pool, body)

        @block.vector
        def _(dve):
            dve.sem_inc(tm.w_used, RING)
            dve.sem_inc(sq_free, RING)
            dve.sem_inc(raw_free, RING)
            dve.sem_inc(lo_free, RING)
            tm.split(dve, 0, 0)
            dve.wait_ge(tables_landed, 64)
            dve.tensor_scalar(gains[:], gains[:], gain_scale, None, ALU.mult).then_inc(tables_scaled, 1)
            dve.wait_ge(tables_scaled, 1)
            for which in range(2):
                dve.tensor_tensor(rope[:, which], rope[:, which],
                                  bcast(gains[:, which], [(0, TILES), (1, HEAD_DIM)]), ALU.mult).then_inc(
                                      tables_scaled, 1)
            dve.wait_ge(tables_scaled, 3)

            def total(b, i):
                n, s = b * nt + i, i % RING
                dve.wait_ge(sq_done, n + 1)
                dve.tensor_reduce(hss[:, s], heads(sq[:, s]), AX.X, ALU.add).then_inc(hss_done, 1)
                dve.wait_ge(hss_done, n + 1)
                dve.sem_inc(sq_free, 1)

            def rotate(b, i):
                n, s = b * nt + i, i % RING
                dve.wait_ge(rms_done, n + 1)
                dve.reciprocal(hrstd[:, s], hrms[:, s]).then_inc(rstd_done, 1)
                dve.wait_ge(rstd_done, n + 1)
                dve.wait_ge(tm.acc_free, n + 5)
                dve.tensor_tensor(heads(raw[:, s]), heads(raw[:, s]), bcast(hrstd[:, s], [(1, HPB), (0, HEAD_DIM)]),
                                  ALU.mult).then_inc(n_done, 1)
                dve.wait_ge(n_done, n + 1)
                dve.wait_ge(rot_done, n)
                for half in range(2):
                    t = rope[:, 1, tiles[i]].rearrange("p (a f d) -> p a f d", f=2, d=QUARTER)[:, :, half]
                    dve.tensor_tensor(
                        quarters(r2[:, s], half).rearrange("p (h a) d -> p h a d", a=2),
                        quarters(raw[:, s], 1 - half).rearrange("p (h a) d -> p h a d", a=2),
                        bcast(t, [(0, HPB), (2 * QUARTER, 2), (1, QUARTER)]), ALU.mult).then_inc(r2_done, 1)
                dve.wait_ge(r2_done, 2 * n + 2)
                dve.wait_ge(r1_done, n + 1)
                dve.sem_inc(raw_free, 1)
                dve.tensor_tensor(r1[:, s], r1[:, s], r2[:, s], ALU.add).then_inc(rot_done, 1)

            def lo(b, i):
                n, s = b * nt + i, i % RING
                dve.wait_ge(hi_done, n + 1)
                dve.wait_ge(lo_stored[s], 16 * (b * (nt // RING) + i // RING))
                dve.tensor_tensor(t_lo[:, s], turn[s][:, 0:COLS_W], t_hi[:, s].bitcast(F32),
                                  ALU.subtract).then_inc(lo_free, 1)

            def body(b, slot):
                for i in range(nt + 3):
                    if i < nt:
                        total(b, i)
                    if 1 <= i <= nt:
                        rotate(b, i - 1)
                    if i == 4 and count > 1:
                        tm.split(dve, b + 1, 1 - slot)
                    if i >= 3:
                        lo(b, i - 3)

            tm.blocks(dve, body)



def channel_products(pe, h_hi, h_lo, w_hi, w_lo, bank, tok, width):
    for k in range(KD):
        pe.matmul(bank, w_hi[:, k], h_hi[:, k, tok:tok + width], start=(k == 0), stop=False)
        pe.matmul(bank, w_hi[:, k], h_lo[:, k, tok:tok + width], start=False, stop=False)
        last = pe.matmul(bank, w_lo[:, k], h_hi[:, k, tok:tok + width], start=False, stop=(k == KD - 1))
    return last


def stage_channels(nc, sem, io, keep, h_hi, h_lo, dram):
    with ExitStack() as ctx:
        def sb(name, shape, dt=F32):
            return ctx.enter_context(nc.sbuf_tensor("cm_" + name, shape, dt))

        GATE_TILES = WIDTH // P
        CONV = TOK + PAD
        NB = len(BLOCKS)
        w_raw = sb("w_raw", [P, KD, P])
        w_hi, w_lo = sb("w_hi", [P, RING, KD, P], F32R), sb("w_lo", [P, RING, KD, P], F32R)
        line = sb("line", [P, RING, TOK + 3 * PAD])
        y = sb("y", [P, RING, CONV])
        acc = [ctx.enter_context(nc.psum_tensor(f"cm_acc{b}", [P, 512], F32)) for b in range(NB)]
        (w_landed, w_hi_done, w_split, w_used, acc_done, acc_free, line_zero, line_free, tap_done, y_done) = [
            sem("cm_" + x) for x in ("w_landed", "w_hi_done", "w_split", "w_used", "acc_done", "acc_free",
                                     "line_zero", "line_free", "tap_done", "y_done")]
        stored = [sem(f"cm_stored{s}") for s in range(RING)]
        w_in = io["w_in"].rearrange("o (k p) c -> p (o k) c", p=P)
        w_xbc = w_in[:, :, OFF_XBC:OFF_XBC + XBC_TILES * P].rearrange("p k (m c) -> p m k c", c=P)
        w_gate = w_in[:, :, OFF_G:OFF_G + WIDTH].rearrange("p k (m c) -> p m k c", c=P)
        block = ctx.enter_context(nc.Block())

        def loop(eng, count, body):
            with eng.Fori(0, count - 1, 2) as i:
                for u in range(2):
                    body(i + u, u)

        @block.sync
        def _(sync):
            def load(src, m):
                sync.wait_ge(w_split, m)
                sync.dma_start(w_raw[:], src).then_inc(w_landed, 16)

            loop(sync, XBC_TILES, lambda m, s: load(w_xbc[:, m], m))
            loop(sync, GATE_TILES, lambda m, s: load(w_gate[:, m], m + XBC_TILES))

        @block.tensor
        def _(pe):
            def xbc(m, s):
                pe.wait_ge(w_split, m + 1)
                for i, (tok, width) in enumerate(BLOCKS):
                    pe.wait_ge(acc_free, m * NB + i + 1)
                    channel_products(pe, h_hi, h_lo, w_hi[:, s], w_lo[:, s], acc[i][:, 0:width], tok,
                                     width).then_inc(acc_done, 1)
                pe.drain().then_inc(w_used, 1)

            def gate(m, s):
                pe.wait_ge(w_split, m + XBC_TILES + 1)
                for i in range(1, NB):
                    pe.wait_ge(acc_free, XBC_TILES * NB + m * (NB - 1) + i + 1)
                    channel_products(pe, h_hi, h_lo, w_hi[:, s], w_lo[:, s], acc[i][:], BLOCKS[i][0],
                                     512).then_inc(acc_done, 1)
                pe.drain().then_inc(w_used, 1)

            loop(pe, XBC_TILES, xbc)
            loop(pe, GATE_TILES, gate)

        @block.scalar
        def _(act):
            act.sem_inc(acc_free, NB)

            def xbc(m, s):
                act.wait_ge(line_zero, 1)
                act.wait_ge(line_free, m + 1)
                for i, (tok, width) in enumerate(BLOCKS):
                    act.wait_ge(acc_done, m * NB + i + 1)
                    at = PAD + tok + (PAD if i else 0)
                    act.activation(line[:, s, at:at + width], acc[i][:, 0:width], ACT.Copy).then_inc(acc_free, 1)
                act.wait_ge(tap_done, D_CONV * (m + 1))
                act.activation(y[:, s], y[:, s], ACT.Silu).then_inc(y_done, 1)
                act.wait_ge(y_done, m + 1)
                act.dma_start(dram["xbc"][m, :, 0:CTX], y[:, s, 0:CTX]).then_inc(stored[s], 16)
                act.dma_start(dram["xbc"][m, :, CTX:TOK], y[:, s, CTX + PAD:CONV]).then_inc(stored[s], 16)

            def gate(m, s):
                act.wait_ge(stored[s], 16 * (XBC_TILES + m // 2) if isinstance(m, int) else gate_stored(m, s))
                for i in range(1, NB):
                    act.wait_ge(acc_done, XBC_TILES * NB + m * (NB - 1) + i)
                    act.activation(y[:, s, (i - 1) * 512:i * 512], acc[i][:], ACT.Silu).then_inc(acc_free, 1)
                act.wait_ge(acc_free, NB + XBC_TILES * NB + (m + 1) * (NB - 1))
                act.dma_start(dram["gate"][m], y[:, s, 0:SEQ]).then_inc(stored[s], 16)

            def gate_stored(m, s):
                return 16 * XBC_TILES + 8 * (m - s)

            loop(act, XBC_TILES, xbc)
            loop(act, GATE_TILES, gate)
            for s in range(RING):
                act.wait_ge(stored[s], 16 * XBC_TILES + 8 * GATE_TILES)

        @block.vector
        def _(dve):
            def part(m, s):
                dve.wait_ge(w_landed, 16 * (m + 1))
                dve.wait_ge(w_used, m + 1)
                split(dve, w_raw[:], w_hi[:, s], w_lo[:, s], w_hi_done, m + 1, w_split)

            dve.sem_inc(w_used, RING)
            dve.sem_inc(line_free, RING)
            dve.memset(line[:], 0.0).then_inc(line_zero, 1)
            dve.wait_ge(line_zero, 1)
            part(0, 0)

            def conv(m, s):
                part(m + 1, 1 - s)
                dve.wait_ge(acc_free, NB + NB * (m + 1))
                dve.wait_ge(stored[s], 16 * (m - s))
                for k in range(D_CONV):
                    tap = keep["cols"][:, bass.ds(ROW_CONVW + k * XBC_TILES + m, 1)]
                    if k == 0:
                        dve.tensor_scalar(y[:, s], line[:, s, 0:CONV], tap,
                                          keep["cols"][:, bass.ds(ROW_CONVB + m, 1)], ALU.mult,
                                          ALU.add).then_inc(tap_done, 1)
                    else:
                        dve.wait_ge(tap_done, D_CONV * m + k)
                        dve.scalar_tensor_tensor(y[:, s], line[:, s, k:k + CONV], tap, y[:, s], ALU.mult,
                                                 ALU.add).then_inc(tap_done, 1)
                dve.wait_ge(tap_done, D_CONV * (m + 1))
                dve.sem_inc(line_free, 1)

            loop(dve, XBC_TILES, conv)
            with dve.Fori(0, GATE_TILES - 3, 2) as i:
                for u in range(2):
                    part(XBC_TILES + 1 + i + u, 1 - u)
            part(XBC_TILES + GATE_TILES - 1, 1)


def stage_dt(nc, sem, io, keep, h_hi, h_lo, dram):
    NH = 2 * SSD_HEADS
    with ExitStack() as ctx:
        def sb(name, shape, dt=F32):
            return ctx.enter_context(nc.sbuf_tensor("dt_" + name, shape, dt))

        w_raw, w_hi, w_lo = sb("w_raw", [P, KD, P]), sb("w_hi", [P, KD, P], F32R), sb("w_lo", [P, KD, P], F32R)
        head = sb("head", [NH, 4])
        raw, soft = sb("raw", [NH, TOK]), sb("soft", [NH, TOK])
        sums = sb("sums", [NH, 2, TOK])
        ones = sb("ones", [NH, P])
        cols = sb("cols", [P, 5, TILES, NH])
        total = cols[:, 3]
        ps = [ctx.enter_context(nc.psum_tensor(f"dt_ps{b}", [P, 512], F32)) for b in range(8)]
        names = ("w_landed", "head_landed", "w_hi_done", "w_split", "head_ready", "acc_done", "raw_done", "steps",
                 "dt_done", "a_done", "ones_done", "scanned", "turned", "cols_done", "total_done", "factors", "stored",
                 "total_copied", "weight_log", "weighted")
        (w_landed, head_landed, w_hi_done, w_split, head_ready, acc_done, raw_done, steps, dt_done, a_done, ones_done,
         scanned, turned, cols_done, total_done, factors, stored, total_copied, weight_log, weighted) = [sem("dt_" + x) for x in names]
        HALF = TILES // 2
        w_in = io["w_in"].rearrange("o (k p) c -> p (o k) c", p=P)
        off = OFF_XBC + XBC_TILES * P
        block = ctx.enter_context(nc.Block())

        @block.sync
        def _(sync):
            sync.dma_start(w_raw[:], w_in[:, :, off:off + P]).then_inc(w_landed, 16)
            sync.dma_start(head[:, 0:1], io["dt_bias"].rearrange("o d h -> (d h) o")).then_inc(head_landed, 16)
            sync.dma_start(head[:, 1:2], io["a_log"].rearrange("o d h -> (d h) o")).then_inc(head_landed, 16)
            sync.wait_ge(scanned, 2 * TILES)
            for d in range(2):
                rows = slice(d * SSD_HEADS, (d + 1) * SSD_HEADS)
                sync.dma_start(dram["cs"][rows], sums[rows, d]).then_inc(stored, 16)
            sync.wait_ge(weighted, 1)
            sync.dma_start(dram["dtcols"], cols[:].rearrange("p a c h -> p (a c h)")).then_inc(stored, 16)
            sync.wait_ge(stored, 48)

        @block.tensor
        def _(pe):
            pe.wait_ge(w_split, 1)
            for i, (tok, width) in enumerate(BLOCKS):
                channel_products(pe, h_hi, h_lo, w_hi, w_lo, ps[i][:, 0:width], tok, width).then_inc(acc_done, 1)
            pe.wait_ge(raw_done, len(BLOCKS))
            pe.wait_ge(scanned, 2 * TILES)
            pe.wait_ge(dt_done, 1)
            for what in range(3):
                for c in range(TILES):
                    src = soft if what == 0 else sums[:, what - 1]
                    at = (c % HALF) * NH
                    last = pe.transpose(ps[2 * what + c // HALF][:, at:at + NH],
                                        (src[:, c * P:(c + 1) * P]), keep["ident"][0:NH, 0:NH])
                last.then_inc(turned, 1)
            pe.wait_ge(cols_done, 6)
            for d in range(2):
                pe.matmul(ps[6 + d][:, 0:TILES * SSD_HEADS], keep["pick"][:, d],
                          cols[:, 1, :, d * SSD_HEADS:(d + 1) * SSD_HEADS], start=True, stop=True).then_inc(
                              total_done, 1)

        @block.scalar
        def _(act):
            act.wait_ge(head_landed, 32)
            act.activation(head[:, 2:3], head[:, 1:2], ACT.Exp).then_inc(head_ready, 1)
            for i, (tok, width) in enumerate(BLOCKS):
                act.wait_ge(acc_done, i + 1)
                act.activation(raw[:, tok:tok + width], ps[i][0:NH, 0:width], ACT.Identity,
                               bias=head[:, 0:1]).then_inc(raw_done, 1)
            act.wait_ge(raw_done, len(BLOCKS))
            act.activation(soft[:], raw[:], ACT.Abs).then_inc(steps, 1)
            act.wait_ge(steps, 1)
            act.activation(soft[:], soft[:], ACT.Exp, scale=-1.0).then_inc(steps, 1)
            act.wait_ge(steps, 2)
            act.activation(soft[:], soft[:], ACT.Ln, bias=keep["one"][0:NH]).then_inc(steps, 1)
            act.wait_ge(cols_done, 6)
            act.activation(cols[:, 2], cols[:, 1], ACT.Exp).then_inc(factors, 1)
            act.wait_ge(weight_log, 1)
            act.activation(cols[:, 3], cols[:, 3], ACT.Exp).then_inc(factors, 1)
            act.activation(cols[:, 4], cols[:, 4], ACT.Exp).then_inc(factors, 1)

        @block.vector
        def _(dve):
            dve.wait_ge(w_landed, 16)
            split(dve, w_raw[:], w_hi[:], w_lo[:], w_hi_done, 1, w_split)
            dve.memset(ones[:], 1.0).then_inc(ones_done, 1)
            dve.wait_ge(head_ready, 1)
            dve.wait_ge(steps, 3)
            dve.scalar_tensor_tensor(soft[:], raw[:], 0.0, soft[:], ALU.max, ALU.add).then_inc(dt_done, 1)
            dve.wait_ge(dt_done, 1)
            dve.tensor_scalar(raw[:], soft[:], head[:, 2:3], -1.0, ALU.mult, ALU.mult).then_inc(a_done, 1)
            dve.wait_ge(a_done, 1)
            dve.wait_ge(ones_done, 1)
            for c in range(TILES):
                for d in range(2):
                    def way(x):
                        return x[:, ::-1] if d else x
                    dve.tensor_tensor_scan(way(sums[:, d, c * P:(c + 1) * P]), way(ones[:]),
                                           way(raw[:, c * P:(c + 1) * P]), 0.0, ALU.mult, ALU.add).then_inc(scanned, 1)
            heads = [slice(0, NH), slice(0, SSD_HEADS), slice(SSD_HEADS, NH)]
            for what in range(3):
                dve.wait_ge(turned, what + 1)
                for half in range(2):
                    src = ps[2 * what + half][:, 0:HALF * NH].rearrange("p (c h) -> p c h", h=NH)
                    dve.tensor_copy(cols[:, min(what, 1), half * HALF:(half + 1) * HALF, heads[what]],
                                    src[:, :, heads[what]]).then_inc(cols_done, 1)
            for d in range(2):
                dve.wait_ge(total_done, 2)
                dve.tensor_copy(total[:, :, heads[1 + d]],
                                ps[6 + d][:, 0:TILES * SSD_HEADS].rearrange("p (c h) -> p c h", h=SSD_HEADS)).then_inc(
                                    total_copied, 1)
            dve.wait_ge(total_copied, 2)
            dve.tensor_tensor(cols[:, 4], total, cols[:, 1], ALU.subtract).then_inc(weight_log, 1)
            dve.wait_ge(factors, 3)
            dve.tensor_tensor(cols[:, 4], cols[:, 4], cols[:, 0], ALU.mult).then_inc(weighted, 1)




class Factors:

    def __init__(self, cols):
        self.dt, self.cs, self.e_cs, self.e_total, self.weight = [cols[:, a] for a in range(5)]


def spread(x, at, d, g=None):
    heads = SSD_HEADS if g is None else HEADS_PER_GROUP
    h0 = d * SSD_HEADS + (0 if g is None else g * HEADS_PER_GROUP)
    return bcast(x[:, at, h0:h0 + heads], [(1, heads), (0, HEAD_DIM)])


def by_head(x):
    return x.rearrange("p (h d) -> p h d", d=HEAD_DIM)


def stage_ssd_backward(nc, sem, io, keep, dram, cols):
    f = Factors(cols)
    GW = HEADS_PER_GROUP * HEAD_DIM
    X_T = WIDTH // P
    with ExitStack() as ctx:
        def sb(name, shape, dt=F32):
            return ctx.enter_context(nc.sbuf_tensor("sb_" + name, shape, dt))

        xbc = sb("xbc", [P, 2, XBC_TILES, P])
        rows = sb("rows", [P, 2, WIDTH + GROUPS * D_STATE])
        xw = sb("xw", [P, 2, WIDTH])
        yb = sb("yb", [P, 2, WIDTH])
        state, decayed = sb("state", [P, WIDTH]), sb("decayed", [P, WIDTH])
        ps_turn = ctx.enter_context(nc.psum_tensor("sb_ps_turn", [P, 3 * 512], F32))
        ps_state = ctx.enter_context(nc.psum_tensor("sb_ps_state", [P, 2 * 512], F32))
        ps_off = ctx.enter_context(nc.psum_tensor("sb_ps_off", [P, 2 * 512], F32))
        names = ("cols_landed", "turned", "rows_done", "xw_done", "state_sum", "off_done", "yb_done", "decay_done",
                 "state_done")
        (cols_landed, turned, rows_done, xw_done, state_sum, off_done, yb_done, decay_done, state_done) = [
            sem("sb_" + x) for x in names]
        landed = [sem(f"sb_landed{s}") for s in range(2)]
        stored = [sem(f"sb_stored{s}") for s in range(2)]
        yb_stored = [sem(f"sb_yb_stored{s}") for s in range(2)]
        src = dram["xbc"].rearrange("m p (c t) -> c p m t", t=P)
        ROWS = WIDTH + GROUPS * D_STATE
        block = ctx.enter_context(nc.Block())

        def steps(eng, body):
            for n in range(CTX_TILES):
                body(n, CTX_TILES - 1 - n, n % 2, False)
            with eng.Fori(0, LAT_TILES - 1, 2) as i:
                for u in range(2):
                    body(CTX_TILES + i + u, i * -1 + (TILES - 1 - u), u, True)

        @block.sync
        def _(sync):
            sync.dma_start(cols[:].rearrange("p a c h -> p (a c h)"), dram["dtcols"]).then_inc(cols_landed, 16)

            def body(n, c, s, latent):
                if latent:
                    sync.wait_ge(state_sum, n - 1)
                sync.dma_start(xbc[:, s], src[c]).then_inc(landed[s], 16)

            steps(sync, body)

        @block.scalar
        def _(act):
            def body(n, c, s, latent):
                act.wait_ge(turned, n + 1)
                act.wait_ge(stored[s], 16 * (n - s))
                if latent:
                    act.wait_ge(xw_done, n - 1)
                    act.wait_ge(state_sum, n - 1)
                act.activation(rows[:, s], ps_turn[:, 0:ROWS], ACT.Copy).then_inc(rows_done, 1)
                act.wait_ge(rows_done, n + 1)
                act.dma_start(dram["x"][c], rows[:, s, 0:WIDTH]).then_inc(stored[s], 16)
                act.dma_start(dram["b"][c], rows[:, s, WIDTH:ROWS]).then_inc(stored[s], 16)
                if latent:
                    act.wait_ge(yb_done, 2 * (n - CTX_TILES) + 2)
                    act.dma_start(dram["yb"][c - CTX_TILES], yb[:, s]).then_inc(yb_stored[s], 16)

            steps(act, body)
            for s in range(2):
                act.wait_ge(stored[s], 16 * TILES)
                act.wait_ge(yb_stored[s], 16 * LAT_TILES // 2)

        @block.tensor
        def _(pe):
            def body(n, c, s, latent):
                pe.wait_ge(landed[s], 8 * (n - s) + 16)
                pe.wait_ge(rows_done, n)
                for m in range(X_T + GROUPS):
                    last = pe.transpose(ps_turn[:, m * P:(m + 1) * P], xbc[:, s, m], keep["ident"][:])
                last.then_inc(turned, 1)
                if latent:
                    pe.wait_ge(state_done, n)
                    pe.wait_ge(yb_done, 2 * (n - CTX_TILES))
                    for g in range(GROUPS):
                        last = pe.matmul(ps_off[:, g * GW:(g + 1) * GW], xbc[:, s, X_T + GROUPS + g],
                                         state[:, g * GW:(g + 1) * GW], start=True, stop=True)
                    last.then_inc(off_done, 1)
                pe.wait_ge(xw_done, n + 1)
                pe.wait_ge(state_done, n)
                for g in range(GROUPS):
                    last = pe.matmul(ps_state[:, g * GW:(g + 1) * GW],
                                     rows[:, s, WIDTH + g * D_STATE:WIDTH + (g + 1) * D_STATE],
                                     xw[:, s, g * GW:(g + 1) * GW], start=True, stop=True)
                last.then_inc(state_sum, 1)

            steps(pe, body)

        @block.vector
        def _(dve):
            dve.wait_ge(cols_landed, 16)

            def body(n, c, s, latent):
                dve.wait_ge(rows_done, n + 1)
                if latent:
                    dve.wait_ge(state_sum, n - 1)
                dve.tensor_tensor(by_head(xw[:, s]), by_head(rows[:, s, 0:WIDTH]), spread(f.weight, c, 1),
                                  ALU.mult).then_inc(xw_done, 1)
                if isinstance(n, int) and n == 0:
                    dve.wait_ge(state_sum, 1)
                    dve.tensor_copy(state[:], ps_state[:]).then_inc(state_done, 1)
                    return
                dve.wait_ge(state_done, n)
                dve.tensor_tensor(by_head(decayed[:]), by_head(state[:]), spread(f.e_total, c, 1),
                                  ALU.mult).then_inc(decay_done, 1)
                if latent:
                    dve.wait_ge(off_done, n - CTX_TILES + 1)
                    dve.wait_ge(yb_stored[s], 8 * (n - s) - 8 * CTX_TILES)
                    for g in range(GROUPS):
                        cut = slice(g * GW, (g + 1) * GW)
                        dve.tensor_tensor(by_head(yb[:, s, cut]), by_head(ps_off[:, cut]),
                                          spread(f.e_cs, c, 1, g), ALU.mult).then_inc(yb_done, 1)
                dve.wait_ge(decay_done, n)
                dve.wait_ge(state_sum, n + 1)
                dve.tensor_tensor(state[:], decayed[:], ps_state[:], ALU.add).then_inc(state_done, 1)

            steps(dve, body)


def stage_ssd_forward(nc, sem, io, keep, dram, cols):
    f = Factors(cols)
    GW = HEADS_PER_GROUP * HEAD_DIM
    X_T = WIDTH // P
    HL = SSD_HEADS * P
    with ExitStack() as ctx:
        def sb(name, shape, dt=F32):
            return ctx.enter_context(nc.sbuf_tensor("sf_" + name, shape, dt))

        bc = sb("bc", [P, 2, 2 * GROUPS, P])
        rows = sb("rows", [P, 2, WIDTH + GROUPS * D_STATE])
        sums_f, sums_b = sb("sums_f", [P, 2, SSD_HEADS, P]), sb("sums_b", [P, 2, SSD_HEADS, P])
        yb, z = sb("yb", [P, 2, WIDTH]), sb("z", [P, 2, WIDTH])
        cb = sb("cb", [P, 2, GROUPS, P])
        w = sb("w", [P, 2, SSD_HEADS, P])
        xw, y, junk = sb("xw", [P, WIDTH]), sb("y", [P, WIDTH]), sb("junk", [P, WIDTH])
        skip_x = sb("skip_x", [P, 2, WIDTH])
        state, decayed = sb("state", [P, WIDTH]), sb("decayed", [P, WIDTH])
        d_skip = sb("d_skip", [P, SSD_HEADS])
        masks = sb("masks", [P, 2, P])
        t_hi, t_lo = sb("t_hi", [P, WIDTH], F32R), sb("t_lo", [P, WIDTH], F32R)
        ps_cb = ctx.enter_context(nc.psum_tensor("sf_ps_cb", [P, 512], F32))
        ps_turn = ctx.enter_context(nc.psum_tensor("sf_ps_turn", [P, 512], F32))
        ps_y = ctx.enter_context(nc.psum_tensor("sf_ps_y", [P, 2 * 512], F32))
        ps_off = ctx.enter_context(nc.psum_tensor("sf_ps_off", [P, 2 * 512], F32))
        ps_state = ctx.enter_context(nc.psum_tensor("sf_ps_state", [P, 2 * 512], F32))
        names = ("consts", "cb_done", "cb_masked", "diff_f", "diff_b", "least", "w_exp", "w_b", "w_sum", "w_done",
                 "xw_done", "state_sum", "state_done", "decay_done", "y_diag", "y_off", "y_a", "y_b", "y_c", "y_gated",
                 "skip_a", "skip_done", "squared", "turned", "hi_done", "lo_done",
                 "stored_hi", "stored_lo")
        sems = {x: sem("sf_" + x) for x in names}
        landed = [sem(f"sf_landed{s}") for s in range(2)]
        diag_landed = [sem(f"sf_diag_landed{s}") for s in range(2)]
        S = sems
        ROWS = WIDTH + GROUPS * D_STATE
        bc_src = dram["xbc"][X_T:XBC_TILES].rearrange("m p (c t) -> c p m t", t=P)
        cs_src = dram["cs"].rearrange("(d h) (c t) -> c d h t", d=2, t=P)
        out_dst = dram["ys"].rearrange("s m p (c t) -> s c p m t", t=P)
        block = ctx.enter_context(nc.Block())

        def steps(eng, context, first, both):
            for c in range(CTX_TILES):
                context(c, c, c % 2)
            first()
            with eng.Fori(0, LAT_TILES - 3, 2) as i:
                for u in range(2):
                    both(i + u, u, True)
            for c in (LAT_TILES - 2, LAT_TILES - 1):
                both(c, c % 2, c + 1 < LAT_TILES)

        def nothing(*_):
            pass

        @block.sync
        def _(sync):
            sync.dma_start(d_skip[:], io["d_skip"].broadcast_to([P, SSD_HEADS])).then_inc(S["consts"], 16)
            sync.dma_start(masks[:], io["masks"]).then_inc(S["consts"], 16)

            def context(c, n, s):
                sync.dma_start(rows[:, s, 0:WIDTH], dram["x"][c]).then_inc(landed[s], 16)
                sync.dma_start(rows[:, s, WIDTH:ROWS], dram["b"][c]).then_inc(landed[s], 16)

            def first(c, s):
                known = isinstance(c, int)
                if not known or c >= 2:
                    sync.wait_ge(S["w_done"], c - 1)
                    sync.wait_ge(S["y_off"], c - 1)
                sync.dma_start(bc[:, s], bc_src[c + CTX_TILES]).then_inc(diag_landed[s], 16)
                for d, dst in ((0, sums_f), (1, sums_b)):
                    sync.dma_start(dst[:, s], cs_src[c + CTX_TILES, d].unsqueeze(0).broadcast_to(
                        [P, SSD_HEADS, P])).then_inc(diag_landed[s], 16)
                sync.wait_ge(S["state_sum"], c + 1)
                if not known or c >= 2:
                    sync.wait_ge(S["y_diag"], c - 1)
                    sync.wait_ge(S["skip_done"], c - 1)
                    sync.wait_ge(S["xw_done"], c + CTX_TILES - 1)
                    sync.wait_ge(S["y_gated"], c - 1)
                sync.dma_start(rows[:, s, 0:WIDTH], dram["x"][c + CTX_TILES]).then_inc(landed[s], 16)
                sync.dma_start(rows[:, s, WIDTH:ROWS], dram["b"][c + CTX_TILES]).then_inc(landed[s], 16)
                sync.dma_start(yb[:, s], dram["yb"][c]).then_inc(landed[s], 16)
                sync.dma_start(z[:, s], dram["z"][c]).then_inc(landed[s], 16)

            def both(c, s, more):
                if more:
                    first(c + 1, 1 - s)

            steps(sync, context, lambda: first(0, 0), both)

        def rows_here(eng, c, s):
            eng.wait_ge(landed[s], 32 + 32 * (c - s) + 64)

        @block.gpsimd
        def _(pool):
            pool.wait_ge(S["consts"], 32)

            def weigh(n, s, chunk):
                if not isinstance(n, int) or n:
                    pool.wait_ge(S["state_sum"], n)
                pool.tensor_tensor(by_head(xw[:]), by_head(rows[:, s, 0:WIDTH]), spread(f.weight, chunk, 0),
                                   ALU.mult).then_inc(S["xw_done"], 1)

            def decay(n, chunk):
                pool.wait_ge(S["state_done"], n)
                pool.tensor_tensor(by_head(decayed[:]), by_head(state[:]), spread(f.e_total, chunk, 0),
                                   ALU.mult).then_inc(S["decay_done"], 1)

            def context(c, n, s):
                pool.wait_ge(landed[s], 32)
                weigh(n, s, c)
                if n:
                    decay(n, c)

            def differences(c, s):
                for d, x, name in ((0, sums_f, "diff_f"), (1, sums_b, "diff_b")):
                    pool.wait_ge(diag_landed[s], 24 * (c - s) + 48)
                    col = f.cs[:, c + CTX_TILES, d * SSD_HEADS:(d + 1) * SSD_HEADS]
                    pool.tensor_tensor(x[:, s], x[:, s], bcast(col, [(1, SSD_HEADS), (0, P)]),
                                       ALU.subtract).then_inc(S[name], 1)

            def skip(c, s):
                if not isinstance(c, int) or c >= 2:
                    pool.wait_ge(S["y_c"], c - 1)
                pool.tensor_tensor(by_head(skip_x[:, s]), by_head(rows[:, s, 0:WIDTH]),
                                   bcast(d_skip[:], [(1, SSD_HEADS), (0, HEAD_DIM)]), ALU.mult).then_inc(S["skip_a"], 1)
                pool.wait_ge(S["skip_a"], c + 1)
                pool.tensor_tensor(skip_x[:, s], skip_x[:, s], yb[:, s], ALU.add).then_inc(S["skip_done"], 1)

            def first():
                differences(0, 0)
                rows_here(pool, 0, 0)
                weigh(CTX_TILES, 0, CTX_TILES)
                skip(0, 0)

            def both(c, s, more):
                decay(c + CTX_TILES, c + CTX_TILES)
                if more:
                    differences(c + 1, 1 - s)
                    rows_here(pool, c + 1, 1 - s)
                    weigh(c + CTX_TILES + 1, 1 - s, c + CTX_TILES + 1)
                    skip(c + 1, 1 - s)

            steps(pool, context, first, both)

        @block.tensor
        def _(pe):
            def add_state(n, s):
                pe.wait_ge(S["xw_done"], n + 1)
                pe.wait_ge(S["state_done"], n)
                for g in range(GROUPS):
                    last = pe.matmul(ps_state[:, g * GW:(g + 1) * GW],
                                     rows[:, s, WIDTH + g * D_STATE:WIDTH + (g + 1) * D_STATE],
                                     xw[:, g * GW:(g + 1) * GW], start=True, stop=True)
                last.then_inc(S["state_sum"], 1)

            def first(c, s):
                pe.wait_ge(diag_landed[s], 24 * (c - s) + 48)
                pe.wait_ge(S["cb_masked"], 2 * c)
                for g in range(GROUPS):
                    last = pe.matmul(ps_cb[:, g * P:(g + 1) * P], bc[:, s, g], bc[:, s, GROUPS + g], start=True,
                                     stop=True)
                last.then_inc(S["cb_done"], 1)

            def second(c, s):
                pe.wait_ge(S["state_done"], c + CTX_TILES)
                pe.wait_ge(S["y_a"], 2 * c)
                for g in range(GROUPS):
                    last = pe.matmul(ps_off[:, g * GW:(g + 1) * GW], bc[:, s, GROUPS + g],
                                     state[:, g * GW:(g + 1) * GW], start=True, stop=True)
                last.then_inc(S["y_off"], 1)
                add_state(c + CTX_TILES, s)
                pe.wait_ge(S["w_done"], c + 1)
                pe.wait_ge(S["y_b"], c)
                for g in range(GROUPS):
                    for h in range(HEADS_PER_GROUP - 1, -1, -1):
                        head = g * HEADS_PER_GROUP + h
                        lo = (head - (h > 0)) * HEAD_DIM
                        last = pe.matmul(ps_y[:, lo:(head + 1) * HEAD_DIM], w[:, s, head],
                                         rows[:, s, lo:(head + 1) * HEAD_DIM], start=True, stop=True)
                last.then_inc(S["y_diag"], 1)
                pe.wait_ge(S["y_gated"], c + 1)
                for part in range(2):
                    pe.wait_ge(S["lo_done"], 2 * c + part)
                    for m in range(4):
                        at = (4 * part + m) * P
                        last = pe.transpose(ps_turn[:, m * P:(m + 1) * P], y[:, at:at + P], keep["ident"][:])
                    last.then_inc(S["turned"], 1)

            def both(c, s, more):
                if more:
                    first(c + 1, 1 - s)
                second(c, s)

            steps(pe, lambda c, n, s: add_state(n, s), lambda: first(0, 0), both)

        @block.scalar
        def _(act):
            def first(c, s):
                act.wait_ge(S["cb_masked"], 2 * c + 2)
                if not isinstance(c, int) or c >= 2:
                    act.wait_ge(S["y_diag"], c - 1)
                for h in range(SSD_HEADS):
                    act.activation(w[:, s, h], cb[:, 1, h // HEADS_PER_GROUP], ACT.Copy,
                                   scale=f.dt[:, c + CTX_TILES, SSD_HEADS + h:SSD_HEADS + h + 1]).then_inc(
                                       S["w_b"], 1)
                act.wait_ge(S["least"], c + 1)
                act.activation(sums_f[:, s], sums_f[:, s], ACT.Exp).then_inc(S["w_exp"], 1)

            def second(c, s):
                act.wait_ge(S["y_gated"], c + 1)
                act.wait_ge(S["squared"], c)
                act.activation(junk[:], y[:], ACT.Square,
                               accum_out=keep["ss_y"][:, bass.ds(c, 1)]).then_inc(S["squared"], 1)
                for part in range(2):
                    act.wait_ge(S["turned"], 2 * c + part + 1)
                    act.wait_ge(S["stored_hi"], 16 * c)
                    act.activation(t_hi[:, part * 512:(part + 1) * 512], ps_turn[:], ACT.Copy).then_inc(
                        S["hi_done"], 1)
                for part, done, stored, src in ((0, "hi_done", "stored_hi", t_hi), (1, "lo_done", "stored_lo", t_lo)):
                    act.wait_ge(S[done], 2 * c + 2)
                    act.dma_start(out_dst[part, c], src[:].bitcast(F32).rearrange("p (m t) -> p m t", t=P)).then_inc(
                        S[stored], 16)

            def both(c, s, more):
                if more:
                    first(c + 1, 1 - s)
                second(c, s)

            steps(act, nothing, lambda: first(0, 0), both)
            act.wait_ge(S["stored_hi"], 16 * LAT_TILES)
            act.wait_ge(S["stored_lo"], 16 * LAT_TILES)

        @block.vector
        def _(dve):
            dve.wait_ge(S["consts"], 32)

            def advance(n):
                dve.wait_ge(S["state_sum"], n + 1)
                if isinstance(n, int) and n == 0:
                    dve.tensor_copy(state[:], ps_state[:]).then_inc(S["state_done"], 1)
                    return
                dve.wait_ge(S["decay_done"], n)
                dve.tensor_tensor(state[:], decayed[:], ps_state[:], ALU.add).then_inc(S["state_done"], 1)

            def mask(c):
                dve.wait_ge(S["cb_done"], c + 1)
                dve.wait_ge(S["w_done"], c)
                for d in range(2):
                    dve.tensor_tensor(cb[:, d], ps_cb[:, 0:GROUPS * P].rearrange("p (g t) -> p g t", t=P),
                                      bcast(masks[:, d], [(0, GROUPS), (1, P)]), ALU.mult).then_inc(S["cb_masked"], 1)

            def weights(c, s):
                dve.wait_ge(S["cb_masked"], 2 * c + 2)
                for h in range(SSD_HEADS):
                    dve.wait_ge(S["w_b"], SSD_HEADS * c + h + 1)
                    dve.scalar_tensor_tensor(w[:, s, h], cb[:, 0, h // HEADS_PER_GROUP],
                                             f.dt[:, c + CTX_TILES, h:h + 1], w[:, s, h], ALU.mult,
                                             ALU.add).then_inc(S["w_sum"], 1)
                dve.wait_ge(S["diff_f"], c + 1)
                dve.wait_ge(S["diff_b"], c + 1)
                dve.tensor_tensor(sums_f[:, s], sums_f[:, s], sums_b[:, s], ALU.min).then_inc(S["least"], 1)

            def finish_w(c, s):
                dve.wait_ge(S["w_exp"], c + 1)
                dve.wait_ge(S["w_sum"], SSD_HEADS * (c + 1))
                dve.tensor_tensor(w[:, s], w[:, s], sums_f[:, s], ALU.mult).then_inc(S["w_done"], 1)

            def first():
                mask(0)
                weights(0, 0)
                finish_w(0, 0)

            def both(c, s, more):
                n = c + CTX_TILES
                if more:
                    mask(c + 1)
                dve.wait_ge(S["y_off"], c + 1)
                dve.wait_ge(S["squared"], c)
                dve.wait_ge(S["turned"], 2 * c)
                for g in range(GROUPS):
                    cut = slice(g * GW, (g + 1) * GW)
                    dve.tensor_tensor(by_head(y[:, cut]), by_head(ps_off[:, cut]), spread(f.e_cs, n, 0, g),
                                      ALU.mult).then_inc(S["y_a"], 1)
                advance(n)
                if more:
                    weights(c + 1, 1 - s)
                dve.wait_ge(S["y_diag"], c + 1)
                dve.wait_ge(S["y_a"], 2 * c + 2)
                dve.tensor_tensor(y[:], y[:], ps_y[:], ALU.add).then_inc(S["y_b"], 1)
                dve.wait_ge(S["skip_done"], c + 1)
                dve.wait_ge(S["y_b"], c + 1)
                dve.tensor_tensor(y[:], y[:], skip_x[:, s], ALU.add).then_inc(S["y_c"], 1)
                dve.wait_ge(S["y_c"], c + 1)
                dve.wait_ge(landed[s], 32 + 32 * (c - s) + 64)
                dve.tensor_tensor(y[:], y[:], z[:, s], ALU.mult).then_inc(S["y_gated"], 1)
                if more:
                    finish_w(c + 1, 1 - s)
                for part in range(2):
                    dve.wait_ge(S["hi_done"], 2 * c + part + 1)
                    dve.wait_ge(S["stored_lo"], 16 * c)
                    cut = slice(part * 512, (part + 1) * 512)
                    dve.tensor_tensor(t_lo[:, cut], ps_turn[:], t_hi[:, cut].bitcast(F32),
                                      ALU.subtract).then_inc(S["lo_done"], 1)

            steps(dve, lambda c, n, s: advance(n), first, both)


def stage_attention(nc, sem, io, keep, dram):
    HEADS_Q = Q_PER_KV * P
    GROUPS_ALL = LAT_TILES * N_KV
    CHUNKS = [(0, 1024), (1024, 1024), (2048, TOK - 2048)]
    N_CH = Q_PER_KV * len(CHUNKS)
    POOL_TILES = 12
    SHIFT_ROW, ODD = HEAD_DIM, HEAD_DIM
    FOLD_AT, SHIFT_AT = 1, 13
    with ExitStack() as ctx:
        def sb(name, shape, dt=F32):
            return ctx.enter_context(nc.sbuf_tensor("at_" + name, shape, dt))

        k_hi = sb("k_hi", [P, N_KV, TOK], F32R)
        k_lo = sb("k_lo", [P, N_KV, TOK], F32R)
        v = sb("v", [P, TILES, N_KV * HEAD_DIM])
        q = sb("q", [P, N_KV, Q_PER_KV, P], F32R)
        q_shift = sb("q_shift", [P, N_KV, Q_PER_KV, P], F32R)
        gate = sb("gate", [P, 2, 2, P])
        prob = sb("prob", [P, 2, TILES, HEADS_Q])
        top, neg_top = sb("top", [P, Q_PER_KV, len(CHUNKS)]), sb("neg_top", [P, Q_PER_KV])
        diag = sb("diag", [P, Q_PER_KV, P], F32R)
        sum_pool, sum_dve = sb("sum_pool", [P, 2 * HEADS_Q]), sb("sum_dve", [P, 2 * HEADS_Q])
        sum_all = sb("sum_all", [P, HEADS_Q])
        folded_pool, halves = sb("folded_pool", [P, HEADS_Q]), sb("halves", [P, HEADS_Q])
        fold, ones, ones_r = sb("fold", [P, HEAD_DIM]), sb("ones", [P, P]), sb("ones_r", [P, P], F32R)
        from_fold = sb("from_fold", [P, HEADS_Q])
        gated, recip = sb("gated", [P, 2 * P]), sb("recip", [P, 2 * P])
        o_hi, o_lo = sb("o_hi", [P, 2, 2 * P], F32R), sb("o_lo", [P, 2, 2 * P], F32R)
        ps_max = ctx.enter_context(nc.psum_tensor("at_ps_max", [P, 2 * 1024], F32))
        ps_s = ctx.enter_context(nc.psum_tensor("at_ps_s", [P, 2 * HEADS_Q], F32))
        ps_o = ctx.enter_context(nc.psum_tensor("at_ps_o", [P, HEADS_Q], F32))
        ps_x = ctx.enter_context(nc.psum_tensor("at_ps_x", [P, HEADS_Q], F32))
        names = ("kv_landed", "blank", "row_of_ones", "consts", "max_scored", "chunk_top", "top_done", "diag_done", "spread_done",
                 "shift_done", "scored", "exp_done", "pv_done", "halves_done", "pool_added", "pool_sum", "dve_added",
                 "sum_done", "folded", "read_fold", "recip_done", "gated_done", "o32_done", "hi_done", "lo_done")
        (kv_landed, blank, row_of_ones, consts, max_scored, chunk_top, top_done, diag_done, spread_done, shift_done, scored,
         exp_done, pv_done, halves_done, pool_added, pool_sum, dve_added, sum_done, folded,
         read_fold, recip_done, gated_done, o32_done, hi_done, lo_done) = [sem("at_" + x) for x in names]
        q_landed = [sem(f"at_q_landed{s}") for s in range(N_KV)]
        gate_landed = [sem(f"at_gate_landed{s}") for s in range(2)]
        stored = [sem(f"at_stored{s}") for s in range(2)]
        q_src = dram["q"].rearrange("s (g r) d (n t) -> s n g d r t", r=Q_PER_KV, t=P)
        gate_src = dram["gate"].rearrange("(g j) p (n t) -> n g p j t", j=2, t=P)
        o_dst = dram["ya"].rearrange("s (g j) p (n t) -> s n g p j t", j=2, t=P)
        block = ctx.enter_context(nc.Block())

        class Step:

            def __init__(self, n, g, counter=None):
                self.n, self.g, self.m, self.counter = n, g, n * N_KV + g, counter
                known = isinstance(n, int)
                self.maxima = not known or self.m + 2 < GROUPS_ALL
                self.shift = not known or -1 <= self.m and self.m + 1 < GROUPS_ALL
                self.scores = not known or 0 <= self.m < GROUPS_ALL
                self.pv = not known or 1 <= self.m <= GROUPS_ALL
                self.fold = not known or 2 <= self.m <= GROUPS_ALL + 1
                self.s = g % 2

            def at(self, d):
                return self.n + (self.g + d) // N_KV, (self.g + d) % N_KV

            def of(self, x, d):
                ahead, g = divmod(self.g + d, N_KV)
                return x[self.n + ahead, g] if self.counter is None else x[1 + ahead:][self.counter, g]

            def later(self, m):
                return not isinstance(self.n, int) or self.m >= m

        def steps(eng, body):
            for g in range(-2, N_KV):
                body(Step(0, g))
            with eng.Fori(0, LAT_TILES - 2) as before:
                for g in range(N_KV):
                    body(Step(before + 1, g, before))
            for g in range(N_KV + 2):
                body(Step(LAT_TILES - 1, g))

        @block.sync
        def _(sync):
            src = [dram["k"][a].rearrange("g d t -> d g t") for a in range(2)]
            sync.wait_ge(blank, 2)
            sync.dma_start(k_hi[0:HEAD_DIM].bitcast(F32), src[0]).then_inc(kv_landed, 16)
            sync.dma_start(k_hi[HEAD_DIM:P].bitcast(F32), src[0]).then_inc(kv_landed, 16)
            sync.dma_start(k_lo[0:HEAD_DIM].bitcast(F32), src[1]).then_inc(kv_landed, 16)
            sync.dma_start(v[:], dram["v"].rearrange("t p c -> p t c")).then_inc(kv_landed, 16)

            def load_q(st, d):
                g = (st.g + d) % N_KV
                for dst, part in ((q[0:HEAD_DIM], 0), (q[HEAD_DIM:P], 1), (q_shift[0:HEAD_DIM], 0)):
                    sync.dma_start(dst[:, g].bitcast(F32), st.of(q_src[part], d)).then_inc(q_landed[g], 16)

            load_q(Step(0, -2), 2)

            def body(st):
                if not isinstance(st.n, int) or st.m + 3 < GROUPS_ALL:
                    if st.later(1):
                        sync.wait_ge(scored, TILES * st.m)
                    load_q(st, 3)
                if st.pv:
                    if st.later(3):
                        sync.wait_ge(gated_done, st.m - 2)
                    sync.dma_start(gate[:, 1 - st.s], st.of(gate_src, -1)).then_inc(
                        gate_landed[1 - st.s], 16)
                if st.fold:
                    for part, done, src in ((0, hi_done, o_hi), (1, lo_done, o_lo)):
                        sync.wait_ge(done, st.m - 1)
                        sync.dma_start(st.of(o_dst[part], -2), src[:, st.s].bitcast(F32).rearrange(
                            "p (j t) -> p j t", t=P)).then_inc(stored[st.s], 16)

            steps(sync, body)
            for s in range(2):
                sync.wait_ge(stored[s], 16 * GROUPS_ALL)

        @block.gpsimd
        def _(pool):
            pool.memset(k_lo[HEAD_DIM:P].bitcast(F32), 0.0).then_inc(blank, 1)
            pool.memset(q_shift[HEAD_DIM:P].bitcast(F32), 0.0).then_inc(blank, 1)
            pool.wait_ge(blank, 2)
            pool.memset(k_lo[SHIFT_ROW:SHIFT_ROW + 1].bitcast(F32), 1.0).then_inc(row_of_ones, 1)

            def divide_and_gate(st):
                m = st.m - 2
                pool.wait_ge(read_fold, m + 1)
                pool.wait_ge(gate_landed[st.s], 16 * (st.n * 2 + st.g // 2))
                if st.later(3):
                    pool.wait_ge(lo_done, m)
                pool.tensor_tensor(gated[:], from_fold[:, 0:2 * P], gate[:, st.s].rearrange("p j t -> p (j t)"),
                                   ALU.mult).then_inc(gated_done, 1)
                pool.wait_ge(recip_done, m + 1)
                pool.wait_ge(gated_done, m + 1)
                pool.tensor_tensor(gated[:], gated[:], recip[:], ALU.mult).then_inc(o32_done, 1)

            def body(st):
                if st.fold and not st.scores:
                    divide_and_gate(st)
                if not st.scores:
                    return
                p = prob[:, st.s].rearrange("p t c -> p (t c)")
                W, adds = 2 * HEADS_Q, POOL_TILES // 2 - 1
                for a in range(adds):
                    pool.wait_ge(exp_done, TILES * st.m + 2 * a + 4)
                    if a or st.later(1):
                        pool.wait_ge(pool_added, adds * st.m + a)
                    if a == 0 and st.later(1):
                        pool.wait_ge(pool_sum, st.m)
                    left = p[:, 0:W] if a == 0 else sum_pool[:]
                    pool.tensor_tensor(sum_pool[:], left, p[:, (a + 1) * W:(a + 2) * W], ALU.add).then_inc(
                        pool_added, 1)
                    if a == 0 and st.fold:
                        divide_and_gate(st)
                pool.wait_ge(pool_added, adds * (st.m + 1))
                if st.later(1):
                    pool.wait_ge(sum_done, st.m)
                pool.tensor_tensor(folded_pool[:], sum_pool[:, 0:HEADS_Q], sum_pool[:, HEADS_Q:W],
                                   ALU.add).then_inc(pool_sum, 1)

            steps(pool, body)

        @block.tensor
        def _(pe):
            pe.wait_ge(kv_landed, 4 * 16)
            pe.wait_ge(row_of_ones, 1)
            pe.wait_ge(consts, 3)

            def score(st, u):
                if u == 0:
                    pe.wait_ge(shift_done, st.m + 1)
                if st.later(1) or u >= 2:
                    pe.wait_ge(exp_done, TILES * st.m + u - 1)
                bank = ps_s[:, (u % 2) * HEADS_Q:(u % 2 + 1) * HEADS_Q]
                for k, x, first in ((k_hi, q, True), (k_lo, q_shift, False)):
                    last = pe.matmul(bank, k[:, st.g, u * P:(u + 1) * P], x[:, st.g].rearrange("p r t -> p (r t)"),
                                     start=first, stop=not first)
                last.then_inc(scored, 1)

            def score_for_max(st, c):
                g = (st.g + 2) % N_KV
                key, width = CHUNKS[c % len(CHUNKS)]
                if c == 0:
                    pe.wait_ge(q_landed[g], 48 * (st.at(2)[0] + 1))
                if st.later(-1) or c >= 2:
                    pe.wait_ge(chunk_top, N_CH * (st.m + 2) + c - 1)
                for at in range(0, width, 512):
                    w = min(512, width - at)
                    to = (c % 2) * 1024 + at
                    last = pe.matmul(ps_max[:, to:to + w], q[:, g, c // len(CHUNKS)],
                                     k_hi[:, g, key + at:key + at + w], start=True, stop=True)
                last.then_inc(max_scored, 1)

            def spread_shift(st):
                pe.wait_ge(diag_done, st.m + 2)
                if st.fold:
                    pe.wait_ge(read_fold, st.m - 1)
                pe.matmul(ps_x[:], ones_r[:], diag[:].rearrange("p r t -> p (r t)"), start=True,
                          stop=True).then_inc(spread_done, 1)

            def add_values(st, u):
                g, s = (st.g - 1) % N_KV, 1 - st.s
                if u == 1:
                    pe.wait_ge(exp_done, TILES * st.m)
                    if st.fold:
                        pe.wait_ge(halves_done, st.m - 1)
                for odd in range(2):
                    last = pe.matmul(ps_o[odd * ODD:odd * ODD + HEAD_DIM, :],
                                     v[:, u - 1 + odd, g * HEAD_DIM:(g + 1) * HEAD_DIM], prob[:, s, u - 1 + odd],
                                     start=(u == 1), stop=(u == TILES - 1))
                if u == TILES - 1:
                    last.then_inc(pv_done, 1)

            def fold_group(st):
                pe.wait_ge(halves_done, st.m - 1)
                pe.wait_ge(sum_done, st.m - 1)
                if st.scores:
                    pe.wait_ge(shift_done, st.m + 1)
                else:
                    pe.wait_ge(read_fold, st.m - 2)
                for what, rhs in ((fold[:], halves), (ones[:, 0:HEAD_DIM], sum_all)):
                    for h in range(Q_PER_KV):
                        rows = slice((h % 2) * ODD, (h % 2) * ODD + HEAD_DIM)
                        at = (rhs is sum_all) * 2 * P + (h // 2) * P
                        last = pe.matmul(ps_x[rows, at:at + P], what, rhs[:, h * P:(h + 1) * P],
                                         start=True, stop=True)
                last.then_inc(folded, 1)

            def body(st):
                for u in range(TILES):
                    if st.scores:
                        score(st, u)
                    if st.maxima and u % 3 != 2:
                        score_for_max(st, 2 * (u // 3) + u % 3)
                    if st.pv and u % 2:
                        add_values(st, u)
                    if st.fold and u == FOLD_AT:
                        fold_group(st)
                    if st.shift and u == SHIFT_AT:
                        spread_shift(st)

            steps(pe, body)

        @block.scalar
        def _(act):
            def body(st):
                if st.fold:
                    act.wait_ge(pv_done, st.m - 1)
                    if st.later(3):
                        act.wait_ge(folded, st.m - 2)
                    act.activation(halves[:], ps_o[:], ACT.Copy).then_inc(halves_done, 1)
                    if st.scores:
                        act.wait_ge(sum_done, st.m - 1)
                for u in range(TILES):
                    if st.scores:
                        act.wait_ge(scored, TILES * st.m + u + 1)
                        act.activation(prob[:, st.s, u], ps_s[:, (u % 2) * HEADS_Q:(u % 2 + 1) * HEADS_Q],
                                       ACT.Exp).then_inc(exp_done, 1)
                    if st.fold and u == FOLD_AT + 1:
                        act.wait_ge(folded, st.m - 1)
                        if st.later(3):
                            act.wait_ge(o32_done, st.m - 2)
                            act.wait_ge(recip_done, st.m - 2)
                        act.activation(from_fold[:], ps_x[:], ACT.Copy).then_inc(read_fold, 1)
                    if st.shift and u == SHIFT_AT + 1:
                        row = slice(SHIFT_ROW, SHIFT_ROW + 1)
                        act.wait_ge(spread_done, st.m + 2)
                        act.activation(q_shift[row, (st.g + 1) % N_KV].rearrange("p r t -> p (r t)"), ps_x[row],
                                       ACT.Copy).then_inc(shift_done, 1)

            steps(act, body)

        @block.vector
        def _(dve):
            dve.tensor_tensor(fold[:], keep["ident"][:, 0:HEAD_DIM], keep["ident"][:, HEAD_DIM:P],
                              ALU.add).then_inc(consts, 1)
            dve.memset(ones[:], 1.0).then_inc(consts, 1)
            dve.wait_ge(consts, 2)
            dve.tensor_copy(ones_r[:], ones[:]).then_inc(consts, 1)

            def chunk_max(st, c):
                r, x = c // len(CHUNKS), c % len(CHUNKS)
                dve.wait_ge(max_scored, N_CH * (st.m + 2) + c + 1)
                if c == 0 and st.later(-1):
                    dve.wait_ge(top_done, st.m + 2)
                to = (c % 2) * 1024
                dve.tensor_reduce(top[:, r, x:x + 1], ps_max[:, to:to + CHUNKS[x][1]], AX.X, ALU.max).then_inc(
                    chunk_top, 1)

            def query_maxima(st):
                dve.wait_ge(chunk_top, N_CH * (st.m + 2))
                if st.later(0):
                    dve.wait_ge(diag_done, st.m + 1)
                dve.tensor_reduce(neg_top[:], top[:], AX.X, ALU.max, negate=True).then_inc(top_done, 1)

            def shift_diagonals(st):
                dve.wait_ge(top_done, st.m + 2)
                if st.later(0):
                    dve.wait_ge(spread_done, st.m + 1)
                dve.tensor_tensor(diag[:], bcast(keep["ident"][:], [(0, Q_PER_KV), (1, P)]),
                                  bcast(neg_top[:], [(1, Q_PER_KV), (0, P)]), ALU.mult).then_inc(diag_done, 1)

            def first_sum(st):
                W, t0 = 2 * HEADS_Q, POOL_TILES
                dve.wait_ge(exp_done, TILES * st.m + t0 + 4)
                if st.later(1):
                    dve.wait_ge(sum_done, st.m)
                p = prob[:, st.s].rearrange("p t c -> p (t c)")[:, t0 * HEADS_Q:]
                dve.tensor_tensor(sum_dve[:], p[:, 0:W], p[:, W:2 * W], ALU.add).then_inc(dve_added, 1)

            def late_sum(st, part):
                W, t0 = 2 * HEADS_Q, POOL_TILES + 4
                p = prob[:, 1 - st.s].rearrange("p t c -> p (t c)")[:, t0 * HEADS_Q:]
                dve.wait_ge(dve_added, 3 * st.m - 2 + part)
                if part == 0:
                    dve.wait_ge(exp_done, TILES * st.m)
                    dve.tensor_tensor(sum_dve[:], sum_dve[:], p[:, 0:W], ALU.add).then_inc(dve_added, 1)
                elif part == 1:
                    dve.wait_ge(pool_sum, st.m)
                    dve.tensor_tensor(sum_dve[:, 0:HEADS_Q], sum_dve[:, 0:HEADS_Q], folded_pool[:],
                                      ALU.add).then_inc(dve_added, 1)
                else:
                    if st.later(2):
                        dve.wait_ge(folded, st.m - 1)
                    dve.tensor_tensor(sum_all[:], sum_dve[:, 0:HEADS_Q], sum_dve[:, HEADS_Q:W], ALU.add).then_inc(
                        sum_done, 1)

            def split_output(st, part):
                m = st.m - 2
                if part == 0:
                    dve.wait_ge(read_fold, m + 1)
                    if st.later(3):
                        dve.wait_ge(o32_done, m)
                    dve.reciprocal(recip[:], from_fold[:, 2 * P:4 * P]).then_inc(recip_done, 1)
                elif part == 1:
                    dve.wait_ge(o32_done, m + 1)
                    if st.later(4):
                        dve.wait_ge(stored[st.s], 16 * (st.m - st.s) - 32)
                    dve.tensor_copy(o_hi[:, st.s], gated[:]).then_inc(hi_done, 1)
                else:
                    dve.wait_ge(hi_done, m + 1)
                    dve.tensor_tensor(o_lo[:, st.s], gated[:], o_hi[:, st.s].bitcast(F32), ALU.subtract).then_inc(
                        lo_done, 1)

            def body(st):
                if st.shift:
                    query_maxima(st)
                for c in range(N_CH):
                    if st.maxima:
                        chunk_max(st, c)
                    if st.shift and c == 0:
                        shift_diagonals(st)
                    if st.pv and 1 <= c <= 3:
                        late_sum(st, c - 1)
                    if st.fold and c in (5, 8, 9):
                        split_output(st, (5, 8, 9).index(c))
                if st.scores:
                    first_sum(st)

            steps(dve, body)


def stage_out(nc, sem, io, keep, dram, out):
    K2, HALF = 2 * WIDTH // P, 512
    with ExitStack() as ctx:
        def sb(name, shape, dt=F32):
            return ctx.enter_context(nc.sbuf_tensor("ou_" + name, shape, dt))

        w_raw = sb("w_raw", [P, 2, D_MODEL])
        w_hi, w_lo = sb("w_hi", [P, K2, D_MODEL], F32R), sb("w_lo", [P, K2, D_MODEL], F32R)
        gate, final = sb("gate", [P, D_MODEL]), sb("final", [P, D_MODEL])
        yt = sb("yt", [P, 2, 2, K2, P], F32R)
        x, junk = sb("x", [P, 2, D_MODEL]), sb("junk", [P, D_MODEL])
        part, part2 = sb("part", [P, D_MODEL]), sb("part2", [P, D_MODEL])
        rms_y, rstd_y = sb("rms_y", [P, LAT_TILES]), sb("rstd_y", [P, LAT_TILES])
        ss, rms, rstd = sb("ss", [P, 1]), sb("rms", [P, 1]), sb("rstd", [P, 1])
        ps = [[ctx.enter_context(nc.psum_tensor(f"ou_ps{s}{h}", [P, 2 * HALF], F32)) for h in range(2)]
              for s in range(2)]
        names = ("consts", "w_scaled", "w_hi_done", "w_split", "y_rms", "y_rstd", "attn_done", "ssd_done", "part_done",
                 "mixed", "added", "squared", "rms_done", "rstd_done", "normed")
        (consts, w_scaled, w_hi_done, w_split, y_rms, y_rstd, attn_done, ssd_done, part_done, mixed, added, squared,
         rms_done, rstd_done, normed) = [sem("ou_" + a) for a in names]
        w_landed = [sem(f"ou_w_landed{s}") for s in range(2)]
        landed = [sem(f"ou_landed{s}") for s in range(2)]
        stored = [sem(f"ou_stored{s}") for s in range(2)]
        w_src = io["w_out"].rearrange("o (k p) c -> (o k) p c", p=P)
        srcs = [dram[a].rearrange("s m p (n t) -> n s p m t", t=P) for a in ("ya", "ys")]
        x_src = io["x"].rearrange("o (n p) d -> (o n) p d", p=P)
        out_dst = out.rearrange("o (n p) d -> (o n) p d", p=P)
        block = ctx.enter_context(nc.Block())

        def tiles(eng, body):
            with eng.Fori(0, LAT_TILES - 1, 2) as i:
                for u in range(2):
                    body(i + u, u)

        @block.sync
        def _(sync):
            sync.dma_start(gate[:], keep["gate_dram"].unsqueeze(0).broadcast_to([P, D_MODEL])).then_inc(consts, 16)
            sync.dma_start(final[:], io["final_g"].unsqueeze(0).broadcast_to([P, D_MODEL])).then_inc(consts, 16)
            for k in range(K2):
                if k >= 2:
                    sync.wait_ge(w_split, k - 1)
                sync.dma_start(w_raw[:, k % 2], w_src[k]).then_inc(w_landed[k % 2], 16)

        @block.gpsimd
        def _(pool):
            def load(n, s):
                pool.wait_ge(ssd_done, n + 1)
                pool.wait_ge(stored[s], 8 * (n - s))
                for half, src in enumerate(srcs):
                    for a in range(2):
                        pool.dma_start(yt[:, s, a, half * KD:(half + 1) * KD].bitcast(F32), src[n, a]).then_inc(
                            landed[s], 16)
                pool.dma_start(x[:, s], x_src[n]).then_inc(landed[s], 16)

            tiles(pool, load)

        @block.tensor
        def _(pe):
            pe.sem_inc(ssd_done, 2)

            def body(n, s):
                pe.wait_ge(landed[s], 40 * (n - s) + 80)
                pe.wait_ge(mixed, n + 1)
                for half in range(2):
                    for k in range(half * KD, (half + 1) * KD):
                        pe.wait_ge(w_split, k + 1)
                        for a, w in ((0, w_hi), (0, w_lo), (1, w_hi)):
                            for c in range(2):
                                last = pe.matmul(ps[s][half][:, c * HALF:(c + 1) * HALF], yt[:, s, a, k],
                                                 w[:, k, c * HALF:(c + 1) * HALF],
                                                 start=(k % KD == 0 and a == 0 and w is w_hi),
                                                 stop=(k % KD == KD - 1 and a == 1))
                    last.then_inc((attn_done, ssd_done)[half], 1)

            tiles(pe, body)

        @block.scalar
        def _(act):
            act.activation(rms_y[:], keep["ss_y"][:], ACT.Sqrt, scale=1.0 / WIDTH, bias=keep["eps"][:]).then_inc(
                y_rms, 1)

            def body(n, s):
                act.wait_ge(attn_done, n + 1)
                act.wait_ge(mixed, n + 2)
                act.activation(part[:], ps[s][0][:], ACT.Copy).then_inc(part_done, 1)
                act.wait_ge(added, n + 3)
                act.wait_ge(squared, n)
                act.activation(junk[:], x[:, s], ACT.Square, accum_out=ss[:]).then_inc(squared, 1)
                act.wait_ge(squared, n + 1)
                act.wait_ge(rstd_done, n)
                act.activation(rms[:], ss[:], ACT.Sqrt, scale=1.0 / D_MODEL, bias=keep["eps"][:]).then_inc(
                    rms_done, 1)
                act.wait_ge(normed, n + 1)
                act.dma_start(out_dst[n], x[:, s]).then_inc(stored[s], 16)

            tiles(act, body)
            for s in range(2):
                act.wait_ge(stored[s], 16 * LAT_TILES // 2)

        @block.vector
        def _(dve):
            dve.sem_inc(mixed, 2)
            dve.sem_inc(added, 2)
            dve.wait_ge(consts, 32)
            for k in range(K2):
                dve.wait_ge(w_landed[k % 2], 16 * (k // 2 + 1))
                raw = w_raw[:, k % 2]
                if k < KD:
                    dve.tensor_tensor(raw, raw, gate[:], ALU.mult).then_inc(w_scaled, 1)
                else:
                    row = ROW_SSDG + k - KD
                    dve.scalar_tensor_tensor(raw, raw, keep["cols"][:, row:row + 1], gate[:], ALU.mult,
                                             ALU.mult).then_inc(w_scaled, 1)
                dve.wait_ge(w_scaled, k + 1)
                split(dve, raw, w_hi[:, k], w_lo[:, k], w_hi_done, k + 1, w_split)
            dve.wait_ge(y_rms, 1)
            dve.reciprocal(rstd_y[:], rms_y[:]).then_inc(y_rstd, 1)
            dve.wait_ge(y_rstd, 1)

            def body(n, s):
                dve.wait_ge(part_done, n + 1)
                dve.wait_ge(ssd_done, n + 3)
                dve.wait_ge(added, n + 2)
                dve.scalar_tensor_tensor(part2[:], ps[s][1][:], rstd_y[:, bass.ds(n, 1)], part[:], ALU.mult,
                                         ALU.add).then_inc(mixed, 1)
                dve.wait_ge(mixed, n + 3)
                dve.wait_ge(landed[s], 40 * (n - s) + 80)
                dve.tensor_tensor(x[:, s], x[:, s], part2[:], ALU.add).then_inc(added, 1)
                dve.wait_ge(rms_done, n + 1)
                dve.reciprocal(rstd[:], rms[:]).then_inc(rstd_done, 1)
                dve.wait_ge(rstd_done, n + 1)
                dve.scalar_tensor_tensor(x[:, s], x[:, s], rstd[:], final[:], ALU.mult, ALU.mult).then_inc(normed, 1)

            tiles(dve, body)


def build(nc, io, out):
    with ExitStack() as ctx:
        made = []

        def sem(name):
            made.append(nc.alloc_semaphore(name=name))
            return made[-1]

        def reuse_semaphores():
            nc.clear_and_free_semaphores(made)
            made.clear()
            nc.all_engine_barrier()

        def sb(name, shape, dt=F32):
            return ctx.enter_context(nc.sbuf_tensor(name, shape, dt))

        def scratch(name, shape):
            return nc.dram_tensor(name, shape, F32).ap()

        NH = 2 * SSD_HEADS
        dram = {
            "xbc": scratch("xbc_t", [XBC_TILES, P, TOK]), "gate": scratch("gate_t", [WIDTH // P, P, SEQ]),
            "z": scratch("z_rows", [LAT_TILES, P, WIDTH]), "v": scratch("v_rows", [TILES, P, N_KV * HEAD_DIM]),
            "k": scratch("k_t", [2, N_KV, HEAD_DIM, TOK]), "q": scratch("q_t", [2, N_Q, HEAD_DIM, SEQ]),
            "cs": scratch("cs_rows", [NH, TOK]), "dtcols": scratch("dt_factors", [P, 5 * TILES * NH]),
            "x": scratch("x_rows", [TILES, P, WIDTH]), "b": scratch("b_rows", [TILES, P, GROUPS * D_STATE]),
            "yb": scratch("yb_rows", [LAT_TILES, P, WIDTH]),
            "ys": scratch("ys_t", [2, WIDTH // P, P, SEQ]), "ya": scratch("ya_t", [2, WIDTH // P, P, SEQ]),
        }
        keep = {"ident": sb("ident", [P, P]), "cols": sb("cols", [P, P]), "shift": sb("shift", [P, 2, KD]),
                "scale": sb("scale", [P, 2, KD]), "eps": sb("eps", [P, 1]), "one": sb("one", [P, 1]),
                "pick": sb("pick", [P, 2, P]), "ss_y": sb("ss_y", [P, LAT_TILES]),
                "gate_dram": scratch("gate_vec", [D_MODEL])}
        stage_modulation(nc, sem, io, keep)
        with ExitStack() as hs:
            h_hi = hs.enter_context(nc.sbuf_tensor("h_hi", [P, KD, TOK], F32R))
            h_lo = hs.enter_context(nc.sbuf_tensor("h_lo", [P, KD, TOK], F32R))
            stage_hidden(nc, sem, io, keep, h_hi, h_lo)
            stage_dt(nc, sem, io, keep, h_hi, h_lo, dram)
            stage_channels(nc, sem, io, keep, h_hi, h_lo, dram)
            w_in = io["w_in"].rearrange("o (k p) c -> p (o k) c", p=P)
            lat, every = list(range(CTX_TILES, TILES)), list(range(TILES))
            n_blocks = WIDTH // COLS_W
            w_q = w_in[:, :, OFF_Q:OFF_Q + WIDTH + COLS_W].rearrange("p k (b c) -> p b k c", c=COLS_W)
            w_z = w_in[:, :, OFF_Z - COLS_W:OFF_Z + WIDTH].rearrange("p k (b c) -> p b k c", c=COLS_W)
            k_dst = dram["k"].rearrange("s (j g) d t -> s (g d) j t", g=2)
            q_dst = dram["q"].rearrange("s (b j g) d (n t) -> s b n (g d) j t", j=HPB // 2, g=2, t=P)
            z_dst = dram["z"].rearrange("n p (b c) -> n b p c", c=COLS_W)
            stage_heads(nc, sem, io, keep, h_hi, h_lo, "k_", lambda b: w_in[:, :, 0:COLS_W], 1, every,
                        "k_norm_g", 1.0, lambda s, b, i: k_dst[s, :, :, i * P:(i + 1) * P])
            stage_plain(nc, sem, h_hi, h_lo, "v_", lambda b: w_in[:, :, COLS_W:2 * COLS_W], 1, every,
                        ACT.Copy, lambda b, i: dram["v"][i])
            stage_heads(nc, sem, io, keep, h_hi, h_lo, "q_", lambda b: w_q[:, b], n_blocks, lat,
                        "q_norm_g", HEAD_DIM ** -0.5, lambda s, b, i: q_dst[s, b, i])
            stage_plain(nc, sem, h_hi, h_lo, "z_", lambda b: w_z[:, b * -1 + n_blocks], n_blocks, lat,
                        ACT.Silu, lambda b, i: z_dst[i, b * -1 + (n_blocks - 1)])
        reuse_semaphores()
        with ExitStack() as ss:
            cols = ss.enter_context(nc.sbuf_tensor("ssd_cols", [P, 5, TILES, NH], F32))
            stage_ssd_backward(nc, sem, io, keep, dram, cols)
            stage_ssd_forward(nc, sem, io, keep, dram, cols)
        reuse_semaphores()
        stage_attention(nc, sem, io, keep, dram)
        stage_out(nc, sem, io, keep, dram, out)


def constants():
    ident = np.eye(P, dtype=np.float32)
    s, l = np.arange(P)[:, None], np.arange(P)[None]
    pick = np.zeros((2, P, P), np.float32)
    pick[0, P - 1], pick[1, 0] = 1, 1
    masks = np.stack([s <= l, s >= l]).astype(np.float32)
    nf = HEAD_DIM // 4
    t = np.arange(SEQ)
    freq = (10000.0 ** (-np.arange(nf, dtype=np.float32) / np.float32(nf))).astype(np.float32)
    pos = np.stack([t // GRID_W, t % GRID_W], 1).astype(np.float32)
    ang = pos[:, :, None] * freq
    rope = np.zeros((2, TOK, 2, 2, nf), np.float32)
    rope[0] = 1
    rope[0, CTX:] = np.cos(ang)[:, :, None]
    rope[1, CTX:] = np.sin(ang)[:, :, None] * np.array([-1, 1], np.float32)[None, None, :, None]
    rope = rope.reshape(2, TILES, P, HEAD_DIM).transpose(2, 0, 1, 3)
    return {"ident": ident, "pick": pick.transpose(1, 0, 2), "masks": masks.transpose(1, 0, 2), "rope": rope}


_INPUTS = ["x", "c", "ctx", "c_ctx", "ada_w", "ada_b", "norm_g", "w_in", "conv_w", "conv_b", "dt_bias", "a_log",
           "d_skip", "q_norm_g", "k_norm_g", "ssd_norm_g", "w_out", "final_g"]


def kernel(**inputs):
    import numpy as _np
    import concourse.bacc as _bacc
    from concourse import mybir as _mybir
    from concourse.bass_utils import run_bass_kernel_spmd as _run

    nc = _bacc.Bacc("TRN2", target_bir_lowering=False, num_devices=1)
    given = {name: inputs[name] for name in _INPUTS}
    given.update(constants())
    arrays, io = {}, {}
    for name, value in given.items():
        a = _np.ascontiguousarray(value)
        arrays[f"in_{name}_dram"] = a
        io[name] = nc.dram_tensor(f"in_{name}_dram", a.shape, _mybir.dt.from_np(a.dtype), kind="ExternalInput").ap()
    out = nc.dram_tensor("out_0_dram", (1, SEQ, D_MODEL), F32, kind="ExternalOutput").ap()
    build(nc, io, out)
    r = _run(nc, [arrays], core_ids=[0])
    return r.results[0]["out_0_dram"]
```

```python
from contextlib import ExitStack

import numpy as np

import concourse.bass as bass
from concourse import mybir

P = 128
D_MODEL = 1024
SEQ = 2048
CTX = 256
TOK = CTX + SEQ
GRID_W = 64
HEAD_DIM = 64
N_Q = 16
N_KV = 4
Q_PER_KV = N_Q // N_KV
SSD_HEADS = 16
GROUPS = 2
HEADS_PER_GROUP = SSD_HEADS // GROUPS
D_STATE = 128
D_CONV = 5
EPS = 1e-6
WIDTH = 1024
KD = D_MODEL // P
CTX_TILES = CTX // P
LAT_TILES = SEQ // P
TILES = TOK // P
XBC_TILES = (WIDTH + 2 * GROUPS * D_STATE) // P
OFF_XBC = 2 * N_KV * HEAD_DIM
OFF_Q = OFF_XBC + XBC_TILES * P + 2 * SSD_HEADS
OFF_G = OFF_Q + WIDTH
OFF_Z = OFF_G + WIDTH
PAD = D_CONV // 2
COLS_W = 256
HPB = COLS_W // HEAD_DIM
ADA_W = 512
ADA_CHUNKS = 3 * D_MODEL // ADA_W
BLOCKS = [(0, CTX)] + [(CTX + 512 * i, 512) for i in range(SEQ // 512)]

F32 = mybir.dt.float32
F32R = mybir.dt.float32r
ALU = mybir.AluOpType
ACT = mybir.ActivationFunctionType
AX = mybir.AxisListType

ROW_C, ROW_CCTX, ROW_NORM, ROW_CONVW = 0, KD, 2 * KD, 3 * KD
ROW_CONVB = ROW_CONVW + D_CONV * XBC_TILES
ROW_ADAB = ROW_CONVB + XBC_TILES
ROW_SSDG = ROW_ADAB + 3 * KD


def bcast(ap, dims):
    return bass.AP(tensor=ap.tensor, offset=ap.offset, ap=[list(ap.ap[0])] + [list(d) for d in dims])


def split(dve, w_raw, w_hi, w_lo, hi_done, count, lo_done):
    dve.tensor_copy(w_hi, w_raw).then_inc(hi_done, 1)
    dve.wait_ge(hi_done, count)
    dve.tensor_tensor(w_lo, w_raw, w_hi.bitcast(F32), ALU.subtract).then_inc(lo_done, 1)


def stage_hidden(nc, sem, io, keep, ada, h_hi, h_lo):
    with ExitStack() as ctx:
        def sb(name, shape, dt=F32):
            return ctx.enter_context(nc.sbuf_tensor(name, shape, dt))

        CW, GT, CHUNKS = ADA_W, 4, ADA_CHUNKS
        PER = CW // P
        rows = sb("rows", [P, P])
        silu_c = sb("silu_c", [P, 2, KD])
        ODD = P // 2
        mod_row = sb("mod_row", [ODD + 2, 2, CW])
        add_pairs = sb("add_pairs", [ODD + 2, 2])
        mod = sb("mod", [P, 3 * KD, 2])
        xin = sb("xin", [P, 2, GT, D_MODEL])
        junk = sb("junk", [P, D_MODEL])
        ss = sb("ss", [P, 2, GT])
        rms, rstd = sb("rms", [P, 2, GT]), sb("rstd", [P, 2, GT])
        h32 = sb("h32", [P, 2, 512])
        ps_x = [ctx.enter_context(nc.psum_tensor(f"ps_x{b}", [P, 512], F32)) for b in range(4)]
        ps_row = [ctx.enter_context(nc.psum_tensor(f"ps_row{b}", [P, CW], F32)) for b in range(2)]
        ps_cols = ctx.enter_context(nc.psum_tensor("ps_cols", [P, 512], F32))
        ps_mod = ctx.enter_context(nc.psum_tensor("ps_mod", [P, 512], F32))
        mod_psum = ps_mod[:, 0:2 * 3 * KD].rearrange("p (m j) -> p m j", j=2)
        names = ("rows_landed", "ident_landed", "cols_turned", "cols_ready", "c_ready", "row_done", "row_copied",
                 "mod_turned", "mod_ready", "eps_ready", "pairs_ready", "vecs_ready", "gate_stored",
                 "x_squared", "x_rms", "x_rstd",
                 "x_normed", "x_turned", "h_full", "h_hi_done", "h_lo_done")
        (rows_landed, ident_landed, cols_turned, cols_ready, c_ready, row_done, row_copied, mod_turned, mod_ready,
         eps_ready, pairs_ready, vecs_ready, gate_stored, x_squared, x_rms, x_rstd, x_normed, x_turned, h_full, h_hi_done,
         h_lo_done) = [sem(x) for x in names]
        ada_landed = [sem(f"ada_landed{n}") for n in range(CHUNKS)]
        x_landed = [sem(f"x_landed{s}") for s in range(2)]
        ada_w = io["ada_w"].rearrange("o (k p) (m c) -> p (o k) m c", p=P, c=CW)
        x_lat = io["x"].rearrange("o (g t p) d -> p (o g) t d", p=P, t=GT)
        x_ctx = io["ctx"].rearrange("o (t p) d -> p (o t) d", p=P)
        groups = [(CTX_TILES, 0, 1)] + [(GT, CTX + 512 * g, 0) for g in range(SEQ // 512)]
        before = [sum(x[0] for x in groups[:g]) for g in range(len(groups) + 1)]
        NEXT_AT = 4
        block = ctx.enter_context(nc.Block())

        @block.sync
        def _(sync):
            def load_x(g):
                if g >= 2:
                    sync.wait_ge(x_turned, KD * (g - 1))
                src = x_ctx if g == 0 else x_lat[:, g - 1]
                sync.dma_start(xin[:, g % 2, 0:groups[g][0]], src).then_inc(x_landed[g % 2], 16)

            sync.dma_start(keep["ident"][:], io["ident"]).then_inc(ident_landed, 16)
            sync.dma_start(keep["pick"][:], io["pick"]).then_inc(ident_landed, 16)
            for row, name, view in ((ROW_C, "c", "o (r p) -> (o r) p"), (ROW_CCTX, "c_ctx", "(r p) -> r p"),
                                    (ROW_NORM, "norm_g", "o (r p) -> (o r) p"),
                                    (ROW_CONVW, "conv_w", "o k (r p) -> (o k r) p"),
                                    (ROW_CONVB, "conv_b", "o (r p) -> (o r) p"),
                                    (ROW_ADAB, "ada_b", "o (r p) -> (o r) p"),
                                    (ROW_SSDG, "ssd_norm_g", "o (r p) -> (o r) p")):
                src = io[name].rearrange(view, p=P)
                sync.dma_start(rows[row:row + src.shape[0], :], src).then_inc(rows_landed, 16)
            load_x(0)
            for n in range(CHUNKS):
                sync.dma_start(ada[:, n], ada_w[:, :, n]).then_inc(ada_landed[n], 16)
            for g in range(1, len(groups)):
                load_x(g)
            sync.wait_ge(mod_ready, 1)
            sync.dma_start(keep["gate_dram"].rearrange("(k p) -> p k", p=P),
                           mod[:, 2 * KD:3 * KD, 0], allow_slow_non_contiguous=True).then_inc(gate_stored, 16)
            sync.wait_ge(gate_stored, 16)

        @block.tensor
        def _(pe):
            pe.wait_ge(rows_landed, 7 * 16)
            pe.wait_ge(ident_landed, 32)
            pe.wait_ge(pairs_ready, 1)
            pe.transpose(ps_cols[:, 0:P], rows[:], keep["ident"][:]).then_inc(cols_turned, 1)
            pe.wait_ge(c_ready, 1)

            def turn_row(n):
                pe.wait_ge(row_copied, 2 * n + 2)
                for j in range(PER):
                    last = pe.matmul(mod_psum[:, n * PER + j, :], mod_row[:, n % 2, j * P:(j + 1) * P], add_pairs[:],
                                     start=True, stop=True)
                last.then_inc(mod_turned, 1)

            for n in range(CHUNKS):
                pe.wait_ge(ada_landed[n], 16)
                if n >= 2:
                    pe.wait_ge(row_copied, 2 * n - 2)
                for k in range(KD):
                    row = (k % 2) * ODD
                    last = pe.matmul(ps_row[n % 2][row:row + 2, :], silu_c[:, :, k], ada[:, n, k], start=(k < 2),
                                     stop=(k >= KD - 2))
                last.then_inc(row_done, 1)
                if n:
                    turn_row(n - 1)
            turn_row(CHUNKS - 1)

            for g, (tiles, tok, which) in enumerate(groups):
                pe.wait_ge(x_normed, before[g + 1])
                for k in range(KD):
                    n = g * KD + k
                    if n >= 4:
                        pe.wait_ge(h_full, n - 3)
                    for t in range(tiles):
                        last = pe.transpose(ps_x[n % 4][:, t * P:(t + 1) * P], xin[:, g % 2, t, k * P:(k + 1) * P],
                                            keep["ident"][:])
                    last.then_inc(x_turned, 1)

        @block.scalar
        def _(act):
            act.wait_ge(cols_ready, 1)
            act.activation(silu_c[:].rearrange("p j k -> p (j k)"), keep["cols"][:, 0:2 * KD],
                           ACT.Silu).then_inc(c_ready, 1)

            def norms(g):
                tiles = groups[g][0]
                act.wait_ge(x_landed[g % 2], 16 * (g // 2 + 1))
                for t in range(tiles):
                    if g or t:
                        act.wait_ge(x_squared, before[g] + t)
                    if g >= 2 and t == 0:
                        act.wait_ge(x_rstd, g - 1)
                    act.activation(junk[:], xin[:, g % 2, t], ACT.Square,
                                   accum_out=ss[:, g % 2, t:t + 1]).then_inc(x_squared, 1)
                act.wait_ge(x_squared, before[g + 1])
                act.activation(rms[:, g % 2, 0:tiles], ss[:, g % 2, 0:tiles], ACT.Sqrt, scale=1.0 / D_MODEL,
                               bias=keep["eps"][:]).then_inc(x_rms, 1)

            act.wait_ge(eps_ready, 3)
            norms(0)
            for n in range(CHUNKS):
                act.wait_ge(row_done, n + 1)
                if n >= 2:
                    act.wait_ge(mod_turned, n - 1)
                for row in (0, ODD):
                    act.activation(mod_row[row:row + 2, n % 2], ps_row[n % 2][row:row + 2, :], ACT.Copy).then_inc(
                        row_copied, 1)
            act.wait_ge(vecs_ready, 4)
            for g, (tiles, tok, which) in enumerate(groups):
                for k in range(KD):
                    n = g * KD + k
                    act.wait_ge(x_turned, n + 1)
                    if n >= 2:
                        act.wait_ge(h_lo_done, n - 1)
                    act.activation(h32[:, n % 2, 0:tiles * P], ps_x[n % 4][:, 0:tiles * P], ACT.Identity,
                                   bias=keep["shift"][:, which, k:k + 1],
                                   scale=keep["scale"][:, which, k:k + 1]).then_inc(h_full, 1)
                    if k == NEXT_AT and g + 1 < len(groups):
                        norms(g + 1)

        @block.vector
        def _(dve):
            dve.memset(keep["eps"][:], EPS).then_inc(eps_ready, 1)
            dve.memset(keep["one"][:], 1.0).then_inc(eps_ready, 1)
            dve.memset(mod_row[:], 0.0).then_inc(eps_ready, 1)
            dve.wait_ge(ident_landed, 32)
            ident = keep["ident"][0:ODD + 2]
            dve.tensor_tensor(add_pairs[:], ident[:, 0:2], ident[:, ODD:ODD + 2], ALU.add).then_inc(pairs_ready, 1)
            dve.wait_ge(cols_turned, 1)
            dve.tensor_copy(keep["cols"][:], ps_cols[:, 0:P]).then_inc(cols_ready, 1)
            dve.wait_ge(cols_ready, 1)

            def normalise(g):
                dve.wait_ge(x_rms, g + 1)
                if g >= 2:
                    dve.wait_ge(x_normed, before[g - 1])
                dve.reciprocal(rstd[:, g % 2, 0:groups[g][0]], rms[:, g % 2, 0:groups[g][0]]).then_inc(x_rstd, 1)
                dve.wait_ge(x_rstd, g + 1)
                for t in range(groups[g][0]):
                    dve.tensor_scalar(xin[:, g % 2, t], xin[:, g % 2, t], rstd[:, g % 2, t:t + 1], None,
                                      ALU.mult).then_inc(x_normed, 1)

            normalise(0)
            dve.wait_ge(mod_turned, CHUNKS)
            bias = keep["cols"][:, ROW_ADAB:ROW_ADAB + 3 * KD]
            dve.tensor_tensor(mod[:], mod_psum, bcast(bias, [(1, 3 * KD), (0, 2)]), ALU.add).then_inc(mod_ready, 1)
            dve.wait_ge(mod_ready, 1)
            for j in range(2):
                dve.tensor_copy(keep["shift"][:, j], mod[:, 0:KD, j]).then_inc(vecs_ready, 1)
                dve.scalar_tensor_tensor(keep["scale"][:, j], mod[:, KD:2 * KD, j], 1.0,
                                         keep["cols"][:, ROW_NORM:ROW_NORM + KD], ALU.add,
                                         ALU.mult).then_inc(vecs_ready, 1)

            for g, (tiles, tok, which) in enumerate(groups):
                for k in range(KD):
                    n = g * KD + k
                    dve.wait_ge(h_full, n + 1)
                    split(dve, h32[:, n % 2, 0:tiles * P], h_hi[:, k, tok:tok + tiles * P],
                          h_lo[:, k, tok:tok + tiles * P], h_hi_done, n + 1, h_lo_done)
                    if k == NEXT_AT and g + 1 < len(groups):
                        normalise(g + 1)


RING = 2


class Weights:

    def __init__(self, sem, sb):
        self.raw = sb("w_raw", [P, KD, COLS_W])
        self.hi, self.lo = sb("w_hi", [P, RING, KD, COLS_W], F32R), sb("w_lo", [P, RING, KD, COLS_W], F32R)
        self.landed, self.hi_done, self.split_done = sem("w_landed"), sem("w_hi_done"), sem("w_split")
        self.slabs, self.used = sem("w_slabs"), sem("w_used")


class TokenMajor:

    def __init__(self, nc, sem, ctx, tag, weights, base, src, count, tiles, following):
        self.src, self.count, self.tiles, self.n_tiles, self.base = src, count, tiles, len(tiles), base
        self.weights, self.following, self.next = weights, following, count + (count > 1)
        self.acc = [ctx.enter_context(nc.psum_tensor(f"{tag}_acc{b}", [P, 512], F32)) for b in range(4)]
        self.acc_done, self.acc_free = sem(tag + "acc_done"), sem(tag + "acc_free")

    def slot(self, u):
        return (self.base + u) % RING

    def blocks(self, eng, body):
        if self.count == 1:
            body(0, self.slot(0))
            return
        with eng.Fori(0, self.count - 1, 2) as i:
            for u in range(2):
                body(i + u, self.slot(u))

    def load(self, sync, b, src=None):
        w = self.weights
        sync.wait_ge(w.split_done, self.base + b)
        sync.dma_start(w.raw[:], self.src(b) if src is None else src).then_inc(w.landed, 16)

    def load_following(self, sync):
        if self.following is not None:
            self.load(sync, self.next, self.following)

    def high_half(self, dve, b, slot):
        w = self.weights
        dve.wait_ge(w.landed, (self.base + b + 1) * 16)
        dve.wait_ge(w.used, self.base + b + 1)
        dve.tensor_copy(w.hi[:, slot], w.raw[:]).then_inc(w.hi_done, 1)

    def split(self, dve, b, slot):
        w = self.weights
        self.high_half(dve, b, slot)
        dve.wait_ge(w.hi_done, self.base + b + 1)
        dve.tensor_tensor(w.lo[:, slot], w.raw[:], w.hi[:, slot].bitcast(F32), ALU.subtract).then_inc(w.split_done, 1)

    def low_half(self, pool, b, slot, k):
        w = self.weights
        if k == 0:
            pool.wait_ge(w.hi_done, self.base + b + 1)
        pool.tensor_tensor(w.lo[:, slot, k], w.raw[:, k], w.hi[:, slot, k].bitcast(F32),
                           ALU.subtract).then_inc(w.split_done if k == KD - 1 else w.slabs, 1)

    def products(self, pe, h_hi, h_lo, b, slot, i):
        n, bank, w = b * self.n_tiles + i, self.acc[i % 4][:, 0:COLS_W], self.weights
        tok = slice(self.tiles[i] * P, (self.tiles[i] + 1) * P)
        if i == 0:
            pe.wait_ge(w.split_done, self.base + b + 1)
        pe.wait_ge(self.acc_free, n + 1)
        for k in range(KD):
            pe.matmul(bank, h_hi[:, k, tok], w.hi[:, slot, k], start=(k == 0), stop=False)
            pe.matmul(bank, h_hi[:, k, tok], w.lo[:, slot, k], start=False, stop=False)
            last = pe.matmul(bank, h_lo[:, k, tok], w.hi[:, slot, k], start=False, stop=(k == KD - 1))
        last.then_inc(self.acc_done, 1)

    def used(self, pe):
        pe.drain().then_inc(self.weights.used, 1)


def stage_plain(nc, sem, h_hi, h_lo, tag, weights, base, src, count, tiles, following, func, dst):
    with ExitStack() as ctx:
        tm = TokenMajor(nc, sem, ctx, tag, weights, base, src, count, tiles, following)
        out = ctx.enter_context(nc.sbuf_tensor(f"{tag}_out", [P, RING, COLS_W], F32))
        stored = [sem(f"{tag}stored{s}") for s in range(RING)]
        block = ctx.enter_context(nc.Block())
        nt = len(tiles)

        @block.sync
        def _(sync):
            def body(b, slot):
                if count > 1:
                    tm.load(sync, b + 1)
                else:
                    tm.load_following(sync)
                for i in range(nt):
                    sync.wait_ge(tm.acc_free, b * nt + i + 5)
                    sync.dma_start(dst(b, i), out[:, i % RING]).then_inc(stored[i % RING], 16)

            tm.blocks(sync, body)
            for s in range(RING):
                sync.wait_ge(stored[s], 16 * count * nt // RING)

        @block.tensor
        def _(pe):
            def body(b, slot):
                for i in range(nt):
                    tm.products(pe, h_hi, h_lo, b, slot, i)
                tm.used(pe)

            tm.blocks(pe, body)

        @block.scalar
        def _(act):
            act.sem_inc(tm.acc_free, 4)

            def body(b, slot):
                for i in range(nt):
                    n, s = b * nt + i, i % RING
                    act.wait_ge(tm.acc_done, n + 1)
                    act.wait_ge(stored[s], 16 * (b * (nt // RING) + i // RING))
                    act.activation(out[:, s], tm.acc[i % 4][:, 0:COLS_W], func).then_inc(tm.acc_free, 1)

            tm.blocks(act, body)

        @block.vector
        def _(dve):
            if count > 1:
                tm.blocks(dve, lambda b, slot: tm.split(dve, b + 1, 1 - slot))
            elif following is not None:
                tm.split(dve, 1, tm.slot(1))


def stage_heads(nc, sem, io, keep, h_hi, h_lo, tag, weights, base, src, count, tiles, following, gain, gain_scale,
                dst):
    with ExitStack() as ctx:
        def sb(name, shape, dt=F32):
            return ctx.enter_context(nc.sbuf_tensor(f"{tag}_{name}", shape, dt))

        tm = TokenMajor(nc, sem, ctx, tag, weights, base, src, count, tiles, following)
        turn = [ctx.enter_context(nc.psum_tensor(f"{tag}_turn{b}", [P, 512], F32)) for b in range(RING)]
        rope = sb("rope", [P, 2, TILES, HEAD_DIM])
        gains = sb("gains", [P, 2, HEAD_DIM])
        sq, raw = sb("sq", [P, RING, COLS_W]), sb("raw", [P, RING, COLS_W])
        r1, r2 = sb("r1", [P, RING, COLS_W]), sb("r2", [P, RING, COLS_W])
        t_hi, t_lo = sb("t_hi", [P, RING, COLS_W], F32R), sb("t_lo", [P, RING, COLS_W], F32R)
        hss, hrms, hrstd = sb("hss", [P, RING, HPB]), sb("hrms", [P, RING, HPB]), sb("hrstd", [P, RING, HPB])
        names = ("sq_done", "hss_done", "rms_done", "rstd_done", "n_done", "r1_done", "r2_done", "rot_done",
                 "turned", "hi_done", "lo_free", "raw_free", "sq_free", "tables_landed", "tables_scaled")
        (sq_done, hss_done, rms_done, rstd_done, n_done, r1_done, r2_done, rot_done, turned, hi_done, lo_free,
         raw_free, sq_free, tables_landed, tables_scaled) = [sem(f"{tag}{x}") for x in names]
        hi_stored, lo_stored = [sem(f"{tag}hi_st{s}") for s in range(RING)], [sem(f"{tag}lo_st{s}") for s in range(RING)]
        nt = len(tiles)
        LOW_AT = 4
        QUARTER = HEAD_DIM // 4

        def heads(x):
            return x.rearrange("p (h d) -> p h d", d=HEAD_DIM)

        def quarters(x, half):
            return x.rearrange("p (a f d) -> p a f d", f=2, d=QUARTER)[:, :, half]

        block = ctx.enter_context(nc.Block())

        @block.sync
        def _(sync):
            if base == 0:
                tm.load(sync, 0)
            sync.dma_start(rope[:], io["rope"]).then_inc(tables_landed, 16)
            sync.dma_start(gains[:, 0], io[gain].broadcast_to([P, HEAD_DIM])).then_inc(tables_landed, 16)
            swap = io[gain].rearrange("o (a f d) -> o a f d", f=2, d=QUARTER)
            for half in range(2):
                sync.dma_start(quarters(gains[:, 1], half),
                               swap[:, :, 1 - half].broadcast_to([P, 2, QUARTER])).then_inc(tables_landed, 16)

            def body(b, slot):
                if count > 1:
                    tm.load(sync, b + 1)
                else:
                    tm.load_following(sync)
                for i in range(nt):
                    n = b * nt + i
                    sync.wait_ge(hi_done, n + 1)
                    sync.dma_start(dst(0, b, i), t_hi[:, i % RING].bitcast(F32).rearrange(
                        "p (j t) -> p j t", t=P)).then_inc(hi_stored[i % RING], 16)
                    sync.wait_ge(lo_free, n + 1 + RING)
                    sync.dma_start(dst(1, b, i), t_lo[:, i % RING].bitcast(F32).rearrange(
                        "p (j t) -> p j t", t=P)).then_inc(lo_stored[i % RING], 16)

            tm.blocks(sync, body)
            if count > 1:
                tm.load_following(sync)
            for s in range(RING):
                sync.wait_ge(hi_stored[s], 16 * count * nt // RING)
                sync.wait_ge(lo_stored[s], 16 * count * nt // RING)

        @block.tensor
        def _(pe):
            pe.sem_inc(turned, RING)

            def turn_tile(b, i):
                n, s = b * nt + i, i % RING
                pe.wait_ge(rot_done, n + 1)
                pe.wait_ge(lo_free, n + 1)
                for j in range(COLS_W // P):
                    last = pe.transpose(turn[s][:, j * P:(j + 1) * P], r1[:, s, j * P:(j + 1) * P], keep["ident"][:])
                last.then_inc(turned, 1)

            for i in range(2):
                tm.products(pe, h_hi, h_lo, 0, tm.slot(0), i)

            def body(b, slot):
                for i in range(2, nt):
                    tm.products(pe, h_hi, h_lo, b, slot, i)
                    turn_tile(b, i - 2)
                tm.used(pe)
                for i in range(2):
                    if count > 1:
                        tm.products(pe, h_hi, h_lo, b + 1, 1 - slot, i)
                    turn_tile(b, nt - 2 + i)

            tm.blocks(pe, body)
            if count > 1:
                tm.used(pe)

        @block.scalar
        def _(act):
            act.sem_inc(tm.acc_free, 4)

            def take(b, i):
                n, s = b * nt + i, i % RING
                act.wait_ge(tm.acc_done, n + 1)
                act.wait_ge(sq_free, n + 1)
                act.activation(sq[:, s], tm.acc[i % 4][:, 0:COLS_W], ACT.Square).then_inc(sq_done, 1)
                act.wait_ge(raw_free, n + 1)
                act.activation(raw[:, s], tm.acc[i % 4][:, 0:COLS_W], ACT.Copy).then_inc(tm.acc_free, 1)

            def rms(b, i):
                n, s = b * nt + i, i % RING
                act.wait_ge(hss_done, n + 1)
                act.activation(hrms[:, s], hss[:, s], ACT.Sqrt, scale=1.0 / HEAD_DIM, bias=keep["eps"][:]).then_inc(
                    rms_done, 1)

            def hi(b, i):
                n, s = b * nt + i, i % RING
                act.wait_ge(turned, n + 1 + RING)
                act.wait_ge(hi_stored[s], 16 * (b * (nt // RING) + i // RING))
                act.activation(t_hi[:, s], turn[s][:, 0:COLS_W], ACT.Copy).then_inc(hi_done, 1)

            def body(b, slot):
                for i in range(nt + 3):
                    if i < nt:
                        take(b, i)
                    if 1 <= i <= nt:
                        rms(b, i - 1)
                    if i >= 3:
                        hi(b, i - 3)

            tm.blocks(act, body)

        @block.gpsimd
        def _(pool):
            pool.wait_ge(tables_scaled, 3)

            def body(b, slot):
                for i in range(nt):
                    if count > 1 and i >= LOW_AT and i < LOW_AT + KD:
                        tm.low_half(pool, b + 1, 1 - slot, i - LOW_AT)
                    n, s = b * nt + i, i % RING
                    pool.wait_ge(n_done, n + 1)
                    pool.wait_ge(turned, n + 1)
                    pool.tensor_tensor(heads(r1[:, s]), heads(raw[:, s]),
                                       bcast(rope[:, 0, tiles[i]], [(0, HPB), (1, HEAD_DIM)]),
                                       ALU.mult).then_inc(r1_done, 1)

            tm.blocks(pool, body)
            if count > 1 and following is not None:
                for k in range(KD):
                    tm.low_half(pool, tm.next, tm.slot(tm.next), k)

        @block.vector
        def _(dve):
            if base == 0:
                dve.sem_inc(weights.used, RING)
            dve.sem_inc(sq_free, RING)
            dve.sem_inc(raw_free, RING)
            dve.sem_inc(lo_free, RING)
            if base == 0:
                tm.split(dve, 0, tm.slot(0))
            dve.wait_ge(tables_landed, 64)
            dve.tensor_scalar(gains[:], gains[:], gain_scale, None, ALU.mult).then_inc(tables_scaled, 1)
            dve.wait_ge(tables_scaled, 1)
            for which in range(2):
                dve.tensor_tensor(rope[:, which], rope[:, which],
                                  bcast(gains[:, which], [(0, TILES), (1, HEAD_DIM)]), ALU.mult).then_inc(
                                      tables_scaled, 1)
            dve.wait_ge(tables_scaled, 3)

            def total(b, i):
                n, s = b * nt + i, i % RING
                dve.wait_ge(sq_done, n + 1)
                dve.tensor_reduce(hss[:, s], heads(sq[:, s]), AX.X, ALU.add).then_inc(hss_done, 1)
                dve.wait_ge(hss_done, n + 1)
                dve.sem_inc(sq_free, 1)

            def rotate(b, i):
                n, s = b * nt + i, i % RING
                dve.wait_ge(rms_done, n + 1)
                dve.reciprocal(hrstd[:, s], hrms[:, s]).then_inc(rstd_done, 1)
                dve.wait_ge(rstd_done, n + 1)
                dve.wait_ge(tm.acc_free, n + 5)
                dve.tensor_tensor(heads(raw[:, s]), heads(raw[:, s]), bcast(hrstd[:, s], [(1, HPB), (0, HEAD_DIM)]),
                                  ALU.mult).then_inc(n_done, 1)
                dve.wait_ge(n_done, n + 1)
                dve.wait_ge(rot_done, n)
                for half in range(2):
                    t = rope[:, 1, tiles[i]].rearrange("p (a f d) -> p a f d", f=2, d=QUARTER)[:, :, half]
                    dve.tensor_tensor(
                        quarters(r2[:, s], half).rearrange("p (h a) d -> p h a d", a=2),
                        quarters(raw[:, s], 1 - half).rearrange("p (h a) d -> p h a d", a=2),
                        bcast(t, [(0, HPB), (2 * QUARTER, 2), (1, QUARTER)]), ALU.mult).then_inc(r2_done, 1)
                dve.wait_ge(r2_done, 2 * n + 2)
                dve.wait_ge(r1_done, n + 1)
                dve.sem_inc(raw_free, 1)
                dve.tensor_tensor(r1[:, s], r1[:, s], r2[:, s], ALU.add).then_inc(rot_done, 1)

            def lo(b, i):
                n, s = b * nt + i, i % RING
                dve.wait_ge(hi_done, n + 1)
                dve.wait_ge(lo_stored[s], 16 * (b * (nt // RING) + i // RING))
                dve.tensor_tensor(t_lo[:, s], turn[s][:, 0:COLS_W], t_hi[:, s].bitcast(F32),
                                  ALU.subtract).then_inc(lo_free, 1)

            def body(b, slot):
                for i in range(nt + 3):
                    if i < nt:
                        total(b, i)
                    if 1 <= i <= nt:
                        rotate(b, i - 1)
                    if i == LOW_AT and count > 1:
                        tm.high_half(dve, b + 1, 1 - slot)
                    elif i == LOW_AT and following is not None:
                        tm.split(dve, 1, tm.slot(1))
                    if i >= 3:
                        lo(b, i - 3)

            tm.blocks(dve, body)
            if count > 1 and following is not None:
                tm.high_half(dve, tm.next, tm.slot(tm.next))



def channel_products(pe, h_hi, h_lo, w_hi, w_lo, bank, tok, width):
    for k in range(KD):
        pe.matmul(bank, w_hi[:, k], h_hi[:, k, tok:tok + width], start=(k == 0), stop=False)
        pe.matmul(bank, w_hi[:, k], h_lo[:, k, tok:tok + width], start=False, stop=False)
        last = pe.matmul(bank, w_lo[:, k], h_hi[:, k, tok:tok + width], start=False, stop=(k == KD - 1))
    return last


def stage_channels(nc, sem, io, keep, h_hi, h_lo, dram):
    with ExitStack() as ctx:
        def sb(name, shape, dt=F32):
            return ctx.enter_context(nc.sbuf_tensor("cm_" + name, shape, dt))

        GATE_TILES = WIDTH // P
        CONV = TOK + PAD
        NB = len(BLOCKS)
        w_raw = sb("w_raw", [P, KD, P])
        w_hi, w_lo = sb("w_hi", [P, RING, KD, P], F32R), sb("w_lo", [P, RING, KD, P], F32R)
        line = sb("line", [P, RING, TOK + 3 * PAD])
        y = sb("y", [P, RING, CONV])
        acc = [ctx.enter_context(nc.psum_tensor(f"cm_acc{b}", [P, 512], F32)) for b in range(NB)]
        (w_landed, w_hi_done, w_split, w_used, acc_done, acc_free, line_zero, line_free, tap_done, y_done) = [
            sem("cm_" + x) for x in ("w_landed", "w_hi_done", "w_split", "w_used", "acc_done", "acc_free",
                                     "line_zero", "line_free", "tap_done", "y_done")]
        stored = [sem(f"cm_stored{s}") for s in range(RING)]
        w_in = io["w_in"].rearrange("o (k p) c -> p (o k) c", p=P)
        w_xbc = w_in[:, :, OFF_XBC:OFF_XBC + XBC_TILES * P].rearrange("p k (m c) -> p m k c", c=P)
        w_gate = w_in[:, :, OFF_G:OFF_G + WIDTH].rearrange("p k (m c) -> p m k c", c=P)
        block = ctx.enter_context(nc.Block())

        def loop(eng, count, body):
            with eng.Fori(0, count - 1, 2) as i:
                for u in range(2):
                    body(i + u, u)

        @block.sync
        def _(sync):
            def load(src, m):
                sync.wait_ge(w_split, m)
                sync.dma_start(w_raw[:], src).then_inc(w_landed, 16)

            loop(sync, XBC_TILES, lambda m, s: load(w_xbc[:, m], m))
            loop(sync, GATE_TILES, lambda m, s: load(w_gate[:, m], m + XBC_TILES))

        @block.tensor
        def _(pe):
            def xbc(m, s):
                pe.wait_ge(w_split, m + 1)
                for i, (tok, width) in enumerate(BLOCKS):
                    pe.wait_ge(acc_free, m * NB + i + 1)
                    channel_products(pe, h_hi, h_lo, w_hi[:, s], w_lo[:, s], acc[i][:, 0:width], tok,
                                     width).then_inc(acc_done, 1)
                pe.drain().then_inc(w_used, 1)

            def gate(m, s):
                pe.wait_ge(w_split, m + XBC_TILES + 1)
                for i in range(1, NB):
                    pe.wait_ge(acc_free, XBC_TILES * NB + m * (NB - 1) + i + 1)
                    channel_products(pe, h_hi, h_lo, w_hi[:, s], w_lo[:, s], acc[i][:], BLOCKS[i][0],
                                     512).then_inc(acc_done, 1)
                pe.drain().then_inc(w_used, 1)

            loop(pe, XBC_TILES, xbc)
            loop(pe, GATE_TILES, gate)

        @block.scalar
        def _(act):
            act.sem_inc(acc_free, NB)

            def xbc(m, s):
                act.wait_ge(line_zero, 1)
                act.wait_ge(line_free, m + 1)
                for i, (tok, width) in enumerate(BLOCKS):
                    act.wait_ge(acc_done, m * NB + i + 1)
                    at = PAD + tok + (PAD if i else 0)
                    act.activation(line[:, s, at:at + width], acc[i][:, 0:width], ACT.Copy).then_inc(acc_free, 1)
                act.wait_ge(tap_done, D_CONV * (m + 1))
                act.activation(y[:, s], y[:, s], ACT.Silu).then_inc(y_done, 1)
                act.wait_ge(y_done, m + 1)
                act.dma_start(dram["xbc"][m, :, 0:CTX], y[:, s, 0:CTX]).then_inc(stored[s], 16)
                act.dma_start(dram["xbc"][m, :, CTX:TOK], y[:, s, CTX + PAD:CONV]).then_inc(stored[s], 16)

            def gate(m, s):
                act.wait_ge(stored[s], 16 * (XBC_TILES + m // 2) if isinstance(m, int) else gate_stored(m, s))
                for i in range(1, NB):
                    act.wait_ge(acc_done, XBC_TILES * NB + m * (NB - 1) + i)
                    act.activation(y[:, s, (i - 1) * 512:i * 512], acc[i][:], ACT.Silu).then_inc(acc_free, 1)
                act.wait_ge(acc_free, NB + XBC_TILES * NB + (m + 1) * (NB - 1))
                act.dma_start(dram["gate"][m], y[:, s, 0:SEQ]).then_inc(stored[s], 16)

            def gate_stored(m, s):
                return 16 * XBC_TILES + 8 * (m - s)

            loop(act, XBC_TILES, xbc)
            loop(act, GATE_TILES, gate)
            for s in range(RING):
                act.wait_ge(stored[s], 16 * XBC_TILES + 8 * GATE_TILES)

        @block.vector
        def _(dve):
            def part(m, s):
                dve.wait_ge(w_landed, 16 * (m + 1))
                dve.wait_ge(w_used, m + 1)
                split(dve, w_raw[:], w_hi[:, s], w_lo[:, s], w_hi_done, m + 1, w_split)

            dve.sem_inc(w_used, RING)
            dve.sem_inc(line_free, RING)
            part(0, 0)
            dve.memset(line[:], 0.0).then_inc(line_zero, 1)
            dve.wait_ge(line_zero, 1)

            def conv(m, s):
                part(m + 1, 1 - s)
                dve.wait_ge(acc_free, NB + NB * (m + 1))
                dve.wait_ge(stored[s], 16 * (m - s))
                for k in range(D_CONV):
                    tap = keep["cols"][:, bass.ds(ROW_CONVW + k * XBC_TILES + m, 1)]
                    if k == 0:
                        dve.tensor_scalar(y[:, s], line[:, s, 0:CONV], tap,
                                          keep["cols"][:, bass.ds(ROW_CONVB + m, 1)], ALU.mult,
                                          ALU.add).then_inc(tap_done, 1)
                    else:
                        dve.wait_ge(tap_done, D_CONV * m + k)
                        dve.scalar_tensor_tensor(y[:, s], line[:, s, k:k + CONV], tap, y[:, s], ALU.mult,
                                                 ALU.add).then_inc(tap_done, 1)
                dve.wait_ge(tap_done, D_CONV * (m + 1))
                dve.sem_inc(line_free, 1)

            loop(dve, XBC_TILES, conv)
            with dve.Fori(0, GATE_TILES - 3, 2) as i:
                for u in range(2):
                    part(XBC_TILES + 1 + i + u, 1 - u)
            part(XBC_TILES + GATE_TILES - 1, 1)


def stage_dt(nc, sem, io, keep, h_hi, h_lo, dram):
    NH = 2 * SSD_HEADS
    with ExitStack() as ctx:
        def sb(name, shape, dt=F32):
            return ctx.enter_context(nc.sbuf_tensor("dt_" + name, shape, dt))

        w_raw, w_hi, w_lo = sb("w_raw", [P, KD, P]), sb("w_hi", [P, KD, P], F32R), sb("w_lo", [P, KD, P], F32R)
        head = sb("head", [NH, 4])
        raw, soft = sb("raw", [NH, TOK]), sb("soft", [NH, TOK])
        sums = sb("sums", [NH, 2, TOK])
        ones = sb("ones", [NH, P])
        cols = sb("cols", [P, 5, TILES, NH])
        total = cols[:, 3]
        ps = [ctx.enter_context(nc.psum_tensor(f"dt_ps{b}", [P, 512], F32)) for b in range(8)]
        names = ("w_landed", "head_landed", "w_hi_done", "w_split", "head_ready", "acc_done", "raw_done", "steps",
                 "dt_done", "a_done", "ones_done", "scanned", "turned", "cols_done", "total_done", "factors", "stored",
                 "total_copied", "weight_log", "weighted")
        (w_landed, head_landed, w_hi_done, w_split, head_ready, acc_done, raw_done, steps, dt_done, a_done, ones_done,
         scanned, turned, cols_done, total_done, factors, stored, total_copied, weight_log, weighted) = [
             sem("dt_" + x) for x in names]
        HALF = TILES // 2
        w_in = io["w_in"].rearrange("o (k p) c -> p (o k) c", p=P)
        off = OFF_XBC + XBC_TILES * P
        block = ctx.enter_context(nc.Block())

        @block.sync
        def _(sync):
            sync.dma_start(w_raw[:], w_in[:, :, off:off + P]).then_inc(w_landed, 16)
            sync.dma_start(head[:, 0:1], io["dt_bias"].rearrange("o d h -> (d h) o")).then_inc(head_landed, 16)
            sync.dma_start(head[:, 1:2], io["a_log"].rearrange("o d h -> (d h) o")).then_inc(head_landed, 16)
            sync.wait_ge(scanned, 2 * TILES)
            for d in range(2):
                rows = slice(d * SSD_HEADS, (d + 1) * SSD_HEADS)
                sync.dma_start(dram["cs"][rows], sums[rows, d]).then_inc(stored, 16)
            sync.wait_ge(weighted, 1)
            sync.dma_start(dram["dtcols"], cols[:].rearrange("p a c h -> p (a c h)")).then_inc(stored, 16)
            sync.wait_ge(stored, 48)

        @block.tensor
        def _(pe):
            pe.wait_ge(w_split, 1)
            for i, (tok, width) in enumerate(BLOCKS):
                channel_products(pe, h_hi, h_lo, w_hi, w_lo, ps[i][:, 0:width], tok, width).then_inc(acc_done, 1)
            pe.wait_ge(raw_done, len(BLOCKS))
            pe.wait_ge(scanned, 2 * TILES)
            pe.wait_ge(dt_done, 1)
            for what in range(3):
                for c in range(TILES):
                    src = soft if what == 0 else sums[:, what - 1]
                    at = (c % HALF) * NH
                    last = pe.transpose(ps[2 * what + c // HALF][:, at:at + NH],
                                        (src[:, c * P:(c + 1) * P]), keep["ident"][0:NH, 0:NH])
                last.then_inc(turned, 1)
            pe.wait_ge(cols_done, 6)
            for d in range(2):
                pe.matmul(ps[6 + d][:, 0:TILES * SSD_HEADS], keep["pick"][:, d],
                          cols[:, 1, :, d * SSD_HEADS:(d + 1) * SSD_HEADS], start=True, stop=True).then_inc(
                              total_done, 1)

        @block.scalar
        def _(act):
            act.wait_ge(head_landed, 32)
            act.activation(head[:, 2:3], head[:, 1:2], ACT.Exp).then_inc(head_ready, 1)
            for i, (tok, width) in enumerate(BLOCKS):
                act.wait_ge(acc_done, i + 1)
                act.activation(raw[:, tok:tok + width], ps[i][0:NH, 0:width], ACT.Identity,
                               bias=head[:, 0:1]).then_inc(raw_done, 1)
            act.wait_ge(raw_done, len(BLOCKS))
            act.activation(soft[:], raw[:], ACT.Abs).then_inc(steps, 1)
            act.wait_ge(steps, 1)
            act.activation(soft[:], soft[:], ACT.Exp, scale=-1.0).then_inc(steps, 1)
            act.wait_ge(steps, 2)
            act.activation(soft[:], soft[:], ACT.Ln, bias=keep["one"][0:NH]).then_inc(steps, 1)
            act.wait_ge(cols_done, 6)
            act.activation(cols[:, 2], cols[:, 1], ACT.Exp).then_inc(factors, 1)
            act.wait_ge(weight_log, 1)
            act.activation(cols[:, 3], cols[:, 3], ACT.Exp).then_inc(factors, 1)
            act.activation(cols[:, 4], cols[:, 4], ACT.Exp).then_inc(factors, 1)

        @block.vector
        def _(dve):
            dve.wait_ge(w_landed, 16)
            split(dve, w_raw[:], w_hi[:], w_lo[:], w_hi_done, 1, w_split)
            dve.memset(ones[:], 1.0).then_inc(ones_done, 1)
            dve.wait_ge(head_ready, 1)
            dve.wait_ge(steps, 3)
            dve.scalar_tensor_tensor(soft[:], raw[:], 0.0, soft[:], ALU.max, ALU.add).then_inc(dt_done, 1)
            dve.wait_ge(dt_done, 1)
            dve.tensor_scalar(raw[:], soft[:], head[:, 2:3], -1.0, ALU.mult, ALU.mult).then_inc(a_done, 1)
            dve.wait_ge(a_done, 1)
            dve.wait_ge(ones_done, 1)
            for c in range(TILES):
                for d in range(2):
                    def way(x):
                        return x[:, ::-1] if d else x
                    dve.tensor_tensor_scan(way(sums[:, d, c * P:(c + 1) * P]), way(ones[:]),
                                           way(raw[:, c * P:(c + 1) * P]), 0.0, ALU.mult, ALU.add).then_inc(scanned, 1)
            heads = [slice(0, NH), slice(0, SSD_HEADS), slice(SSD_HEADS, NH)]
            for what in range(3):
                dve.wait_ge(turned, what + 1)
                for half in range(2):
                    src = ps[2 * what + half][:, 0:HALF * NH].rearrange("p (c h) -> p c h", h=NH)
                    dve.tensor_copy(cols[:, min(what, 1), half * HALF:(half + 1) * HALF, heads[what]],
                                    src[:, :, heads[what]]).then_inc(cols_done, 1)
            for d in range(2):
                dve.wait_ge(total_done, 2)
                dve.tensor_copy(total[:, :, heads[1 + d]],
                                ps[6 + d][:, 0:TILES * SSD_HEADS].rearrange("p (c h) -> p c h", h=SSD_HEADS)).then_inc(
                                    total_copied, 1)
            dve.wait_ge(total_copied, 2)
            dve.tensor_tensor(cols[:, 4], total, cols[:, 1], ALU.subtract).then_inc(weight_log, 1)
            dve.wait_ge(factors, 3)
            dve.tensor_tensor(cols[:, 4], cols[:, 4], cols[:, 0], ALU.mult).then_inc(weighted, 1)




class Factors:

    def __init__(self, cols):
        self.dt, self.cs, self.e_cs, self.e_total, self.weight = [cols[:, a] for a in range(5)]


def spread(x, at, d, g=None):
    heads = SSD_HEADS if g is None else HEADS_PER_GROUP
    h0 = d * SSD_HEADS + (0 if g is None else g * HEADS_PER_GROUP)
    return bcast(x[:, at, h0:h0 + heads], [(1, heads), (0, HEAD_DIM)])


def by_head(x):
    return x.rearrange("p (h d) -> p h d", d=HEAD_DIM)


def stage_ssd_backward(nc, sem, io, keep, dram, cols):
    f = Factors(cols)
    GW = HEADS_PER_GROUP * HEAD_DIM
    X_T = WIDTH // P
    with ExitStack() as ctx:
        def sb(name, shape, dt=F32):
            return ctx.enter_context(nc.sbuf_tensor("sb_" + name, shape, dt))

        xbc = sb("xbc", [P, 2, XBC_TILES, P])
        rows = sb("rows", [P, 2, WIDTH + GROUPS * D_STATE])
        xw = sb("xw", [P, 2, WIDTH])
        yb = sb("yb", [P, 2, WIDTH])
        state, decayed = sb("state", [P, WIDTH]), sb("decayed", [P, WIDTH])
        ps_turn = ctx.enter_context(nc.psum_tensor("sb_ps_turn", [P, 3 * 512], F32))
        ps_state = ctx.enter_context(nc.psum_tensor("sb_ps_state", [P, 2 * 512], F32))
        ps_off = ctx.enter_context(nc.psum_tensor("sb_ps_off", [P, 2 * 512], F32))
        names = ("cols_landed", "turned", "rows_done", "xw_done", "state_sum", "off_done", "yb_done", "decay_done",
                 "state_done")
        (cols_landed, turned, rows_done, xw_done, state_sum, off_done, yb_done, decay_done, state_done) = [
            sem("sb_" + x) for x in names]
        landed = [sem(f"sb_landed{s}") for s in range(2)]
        stored = [sem(f"sb_stored{s}") for s in range(2)]
        yb_stored = [sem(f"sb_yb_stored{s}") for s in range(2)]
        src = dram["xbc"].rearrange("m p (c t) -> c p m t", t=P)
        ROWS = WIDTH + GROUPS * D_STATE
        block = ctx.enter_context(nc.Block())

        def steps(eng, body):
            for n in range(CTX_TILES):
                body(n, CTX_TILES - 1 - n, n % 2, False)
            with eng.Fori(0, LAT_TILES - 1, 2) as i:
                for u in range(2):
                    body(CTX_TILES + i + u, i * -1 + (TILES - 1 - u), u, True)

        @block.sync
        def _(sync):
            sync.dma_start(cols[:].rearrange("p a c h -> p (a c h)"), dram["dtcols"]).then_inc(cols_landed, 16)

            def body(n, c, s, latent):
                if latent:
                    sync.wait_ge(state_sum, n - 1)
                sync.dma_start(xbc[:, s], src[c]).then_inc(landed[s], 16)

            steps(sync, body)

        @block.scalar
        def _(act):
            def body(n, c, s, latent):
                act.wait_ge(turned, n + 1)
                act.wait_ge(stored[s], 16 * (n - s))
                if latent:
                    act.wait_ge(xw_done, n - 1)
                    act.wait_ge(state_sum, n - 1)
                act.activation(rows[:, s], ps_turn[:, 0:ROWS], ACT.Copy).then_inc(rows_done, 1)
                act.wait_ge(rows_done, n + 1)
                act.dma_start(dram["x"][c], rows[:, s, 0:WIDTH]).then_inc(stored[s], 16)
                act.dma_start(dram["b"][c], rows[:, s, WIDTH:ROWS]).then_inc(stored[s], 16)
                if latent:
                    act.wait_ge(yb_done, 2 * (n - CTX_TILES) + 2)
                    act.dma_start(dram["yb"][c - CTX_TILES], yb[:, s]).then_inc(yb_stored[s], 16)

            steps(act, body)
            for s in range(2):
                act.wait_ge(stored[s], 16 * TILES)
                act.wait_ge(yb_stored[s], 16 * LAT_TILES // 2)

        @block.tensor
        def _(pe):
            def body(n, c, s, latent):
                pe.wait_ge(landed[s], 8 * (n - s) + 16)
                pe.wait_ge(rows_done, n)
                for m in range(X_T + GROUPS):
                    last = pe.transpose(ps_turn[:, m * P:(m + 1) * P], xbc[:, s, m], keep["ident"][:])
                last.then_inc(turned, 1)
                if latent:
                    pe.wait_ge(state_done, n)
                    pe.wait_ge(yb_done, 2 * (n - CTX_TILES))
                    for g in range(GROUPS):
                        last = pe.matmul(ps_off[:, g * GW:(g + 1) * GW], xbc[:, s, X_T + GROUPS + g],
                                         state[:, g * GW:(g + 1) * GW], start=True, stop=True)
                    last.then_inc(off_done, 1)
                pe.wait_ge(xw_done, n + 1)
                pe.wait_ge(state_done, n)
                for g in range(GROUPS):
                    last = pe.matmul(ps_state[:, g * GW:(g + 1) * GW],
                                     rows[:, s, WIDTH + g * D_STATE:WIDTH + (g + 1) * D_STATE],
                                     xw[:, s, g * GW:(g + 1) * GW], start=True, stop=True)
                last.then_inc(state_sum, 1)

            steps(pe, body)

        @block.vector
        def _(dve):
            dve.wait_ge(cols_landed, 16)

            def body(n, c, s, latent):
                dve.wait_ge(rows_done, n + 1)
                if latent:
                    dve.wait_ge(state_sum, n - 1)
                dve.tensor_tensor(by_head(xw[:, s]), by_head(rows[:, s, 0:WIDTH]), spread(f.weight, c, 1),
                                  ALU.mult).then_inc(xw_done, 1)
                if isinstance(n, int) and n == 0:
                    dve.wait_ge(state_sum, 1)
                    dve.tensor_copy(state[:], ps_state[:]).then_inc(state_done, 1)
                    return
                dve.wait_ge(state_done, n)
                dve.tensor_tensor(by_head(decayed[:]), by_head(state[:]), spread(f.e_total, c, 1),
                                  ALU.mult).then_inc(decay_done, 1)
                if latent:
                    dve.wait_ge(off_done, n - CTX_TILES + 1)
                    dve.wait_ge(yb_stored[s], 8 * (n - s) - 8 * CTX_TILES)
                    for g in range(GROUPS):
                        cut = slice(g * GW, (g + 1) * GW)
                        dve.tensor_tensor(by_head(yb[:, s, cut]), by_head(ps_off[:, cut]),
                                          spread(f.e_cs, c, 1, g), ALU.mult).then_inc(yb_done, 1)
                dve.wait_ge(decay_done, n)
                dve.wait_ge(state_sum, n + 1)
                dve.tensor_tensor(state[:], decayed[:], ps_state[:], ALU.add).then_inc(state_done, 1)

            steps(dve, body)


def stage_ssd_forward(nc, sem, io, keep, dram, cols):
    f = Factors(cols)
    GW = HEADS_PER_GROUP * HEAD_DIM
    X_T = WIDTH // P
    HL = SSD_HEADS * P
    with ExitStack() as ctx:
        def sb(name, shape, dt=F32):
            return ctx.enter_context(nc.sbuf_tensor("sf_" + name, shape, dt))

        bc = sb("bc", [P, 2, 2 * GROUPS, P])
        rows = sb("rows", [P, 2, WIDTH + GROUPS * D_STATE])
        sums_f, sums_b = sb("sums_f", [P, 2, SSD_HEADS, P]), sb("sums_b", [P, 2, SSD_HEADS, P])
        yb, z = sb("yb", [P, 2, WIDTH]), sb("z", [P, 2, WIDTH])
        cb = sb("cb", [P, 2, GROUPS, P])
        w = sb("w", [P, 2, SSD_HEADS, P])
        xw, y, junk = sb("xw", [P, WIDTH]), sb("y", [P, WIDTH]), sb("junk", [P, WIDTH])
        skip_x = sb("skip_x", [P, 2, WIDTH])
        state, decayed = sb("state", [P, WIDTH]), sb("decayed", [P, WIDTH])
        d_skip = sb("d_skip", [P, SSD_HEADS])
        masks = sb("masks", [P, 2, P])
        t_hi, t_lo = sb("t_hi", [P, WIDTH], F32R), sb("t_lo", [P, WIDTH], F32R)
        ps_cb = ctx.enter_context(nc.psum_tensor("sf_ps_cb", [P, 512], F32))
        ps_turn = ctx.enter_context(nc.psum_tensor("sf_ps_turn", [P, 512], F32))
        ps_y = ctx.enter_context(nc.psum_tensor("sf_ps_y", [P, 2 * 512], F32))
        ps_off = ctx.enter_context(nc.psum_tensor("sf_ps_off", [P, 2 * 512], F32))
        ps_state = ctx.enter_context(nc.psum_tensor("sf_ps_state", [P, 2 * 512], F32))
        turn_bank = (ps_turn[:], ps_y[:, 0:512])
        names = ("consts", "cb_done", "cb_masked", "diff_f", "diff_b", "least", "w_exp", "w_b", "w_sum", "w_done",
                 "xw_done", "state_sum", "state_done", "decay_done", "y_diag", "y_off", "y_a", "y_b", "y_c", "y_gated",
                 "skip_a", "skip_done", "squared", "turned", "hi_done", "lo_done",
                 "stored_hi", "stored_lo")
        sems = {x: sem("sf_" + x) for x in names}
        landed = [sem(f"sf_landed{s}") for s in range(2)]
        diag_landed = [sem(f"sf_diag_landed{s}") for s in range(2)]
        S = sems
        ROWS = WIDTH + GROUPS * D_STATE
        bc_src = dram["xbc"][X_T:XBC_TILES].rearrange("m p (c t) -> c p m t", t=P)
        cs_src = dram["cs"].rearrange("(d h) (c t) -> c d h t", d=2, t=P)
        out_dst = dram["ys"].rearrange("s m p (c t) -> s c p m t", t=P)
        block = ctx.enter_context(nc.Block())

        def steps(eng, context, first, both):
            for c in range(CTX_TILES):
                context(c, c, c % 2)
            first()
            with eng.Fori(0, LAT_TILES - 3, 2) as i:
                for u in range(2):
                    both(i + u, u, True)
            for c in (LAT_TILES - 2, LAT_TILES - 1):
                both(c, c % 2, c + 1 < LAT_TILES)

        def nothing(*_):
            pass

        @block.sync
        def _(sync):
            sync.dma_start(d_skip[:], io["d_skip"].broadcast_to([P, SSD_HEADS])).then_inc(S["consts"], 16)
            sync.dma_start(masks[:], io["masks"]).then_inc(S["consts"], 16)

            def context(c, n, s):
                sync.dma_start(rows[:, s, 0:WIDTH], dram["x"][c]).then_inc(landed[s], 16)
                sync.dma_start(rows[:, s, WIDTH:ROWS], dram["b"][c]).then_inc(landed[s], 16)

            def first(c, s):
                known = isinstance(c, int)
                if not known or c >= 2:
                    sync.wait_ge(S["w_done"], c - 1)
                    sync.wait_ge(S["y_off"], c - 1)
                sync.dma_start(bc[:, s], bc_src[c + CTX_TILES]).then_inc(diag_landed[s], 16)
                for d, dst in ((0, sums_f), (1, sums_b)):
                    sync.dma_start(dst[:, s], cs_src[c + CTX_TILES, d].unsqueeze(0).broadcast_to(
                        [P, SSD_HEADS, P])).then_inc(diag_landed[s], 16)
                sync.wait_ge(S["state_sum"], c + 1)
                if not known or c >= 2:
                    sync.wait_ge(S["y_diag"], c - 1)
                    sync.wait_ge(S["skip_done"], c - 1)
                    sync.wait_ge(S["xw_done"], c + CTX_TILES - 1)
                    sync.wait_ge(S["y_gated"], c - 1)
                sync.dma_start(rows[:, s, 0:WIDTH], dram["x"][c + CTX_TILES]).then_inc(landed[s], 16)
                sync.dma_start(rows[:, s, WIDTH:ROWS], dram["b"][c + CTX_TILES]).then_inc(landed[s], 16)
                sync.dma_start(yb[:, s], dram["yb"][c]).then_inc(landed[s], 16)
                sync.dma_start(z[:, s], dram["z"][c]).then_inc(landed[s], 16)

            def both(c, s, more):
                if more:
                    first(c + 1, 1 - s)

            steps(sync, context, lambda: first(0, 0), both)

        def rows_here(eng, c, s):
            eng.wait_ge(landed[s], 32 + 32 * (c - s) + 64)

        @block.gpsimd
        def _(pool):
            pool.wait_ge(S["consts"], 32)

            def weigh(n, s, chunk):
                if not isinstance(n, int) or n:
                    pool.wait_ge(S["state_sum"], n)
                pool.tensor_tensor(by_head(xw[:]), by_head(rows[:, s, 0:WIDTH]), spread(f.weight, chunk, 0),
                                   ALU.mult).then_inc(S["xw_done"], 1)

            def decay(n, chunk):
                pool.wait_ge(S["state_done"], n)
                pool.tensor_tensor(by_head(decayed[:]), by_head(state[:]), spread(f.e_total, chunk, 0),
                                   ALU.mult).then_inc(S["decay_done"], 1)

            def context(c, n, s):
                pool.wait_ge(landed[s], 32)
                weigh(n, s, c)
                if n:
                    decay(n, c)

            def differences(c, s):
                for d, x, name in ((0, sums_f, "diff_f"), (1, sums_b, "diff_b")):
                    pool.wait_ge(diag_landed[s], 24 * (c - s) + 48)
                    col = f.cs[:, c + CTX_TILES, d * SSD_HEADS:(d + 1) * SSD_HEADS]
                    pool.tensor_tensor(x[:, s], x[:, s], bcast(col, [(1, SSD_HEADS), (0, P)]),
                                       ALU.subtract).then_inc(S[name], 1)

            def skip(c, s):
                if not isinstance(c, int) or c >= 2:
                    pool.wait_ge(S["y_c"], c - 1)
                pool.tensor_tensor(by_head(skip_x[:, s]), by_head(rows[:, s, 0:WIDTH]),
                                   bcast(d_skip[:], [(1, SSD_HEADS), (0, HEAD_DIM)]), ALU.mult).then_inc(S["skip_a"], 1)
                pool.wait_ge(S["skip_a"], c + 1)
                pool.tensor_tensor(skip_x[:, s], skip_x[:, s], yb[:, s], ALU.add).then_inc(S["skip_done"], 1)

            def first():
                differences(0, 0)
                rows_here(pool, 0, 0)
                weigh(CTX_TILES, 0, CTX_TILES)
                skip(0, 0)

            def both(c, s, more):
                decay(c + CTX_TILES, c + CTX_TILES)
                if more:
                    differences(c + 1, 1 - s)
                    rows_here(pool, c + 1, 1 - s)
                    weigh(c + CTX_TILES + 1, 1 - s, c + CTX_TILES + 1)
                    skip(c + 1, 1 - s)

            steps(pool, context, first, both)

        @block.tensor
        def _(pe):
            def add_state(n, s):
                pe.wait_ge(S["xw_done"], n + 1)
                pe.wait_ge(S["state_done"], n)
                for g in range(GROUPS):
                    last = pe.matmul(ps_state[:, g * GW:(g + 1) * GW],
                                     rows[:, s, WIDTH + g * D_STATE:WIDTH + (g + 1) * D_STATE],
                                     xw[:, g * GW:(g + 1) * GW], start=True, stop=True)
                last.then_inc(S["state_sum"], 1)

            def first(c, s):
                pe.wait_ge(diag_landed[s], 24 * (c - s) + 48)
                pe.wait_ge(S["cb_masked"], 2 * c)
                for g in range(GROUPS):
                    last = pe.matmul(ps_cb[:, g * P:(g + 1) * P], bc[:, s, g], bc[:, s, GROUPS + g], start=True,
                                     stop=True)
                last.then_inc(S["cb_done"], 1)

            def from_state(c, s):
                pe.wait_ge(S["state_done"], c + CTX_TILES)
                pe.wait_ge(S["y_a"], 2 * c)
                for g in range(GROUPS):
                    last = pe.matmul(ps_off[:, g * GW:(g + 1) * GW], bc[:, s, GROUPS + g],
                                     state[:, g * GW:(g + 1) * GW], start=True, stop=True)
                last.then_inc(S["y_off"], 1)

            def begin():
                first(0, 0)
                from_state(0, 0)

            def both(c, s, more):
                add_state(c + CTX_TILES, s)
                if more:
                    first(c + 1, 1 - s)
                pe.wait_ge(S["w_done"], c + 1)
                pe.wait_ge(S["y_b"], c)
                pe.wait_ge(S["lo_done"], 2 * c)
                for g in range(GROUPS):
                    for h in range(HEADS_PER_GROUP - 1, -1, -1):
                        head = g * HEADS_PER_GROUP + h
                        lo = (head - (h > 0)) * HEAD_DIM
                        last = pe.matmul(ps_y[:, lo:(head + 1) * HEAD_DIM], w[:, s, head],
                                         rows[:, s, lo:(head + 1) * HEAD_DIM], start=True, stop=True)
                last.then_inc(S["y_diag"], 1)
                if more:
                    from_state(c + 1, 1 - s)
                pe.wait_ge(S["y_gated"], c + 1)
                for part in range(2):
                    for m in range(4):
                        at = (4 * part + m) * P
                        last = pe.transpose(turn_bank[part][:, m * P:(m + 1) * P], y[:, at:at + P], keep["ident"][:])
                    last.then_inc(S["turned"], 1)

            steps(pe, lambda c, n, s: add_state(n, s), begin, both)

        @block.scalar
        def _(act):
            def first(c, s):
                act.wait_ge(S["cb_masked"], 2 * c + 2)
                if not isinstance(c, int) or c >= 2:
                    act.wait_ge(S["y_diag"], c - 1)
                for h in range(SSD_HEADS):
                    act.activation(w[:, s, h], cb[:, 1, h // HEADS_PER_GROUP], ACT.Copy,
                                   scale=f.dt[:, c + CTX_TILES, SSD_HEADS + h:SSD_HEADS + h + 1]).then_inc(
                                       S["w_b"], 1)
                act.wait_ge(S["least"], c + 1)
                act.activation(sums_f[:, s], sums_f[:, s], ACT.Exp).then_inc(S["w_exp"], 1)

            def second(c, s):
                act.wait_ge(S["y_gated"], c + 1)
                act.wait_ge(S["squared"], c)
                act.activation(junk[:], y[:], ACT.Square,
                               accum_out=keep["ss_y"][:, bass.ds(c, 1)]).then_inc(S["squared"], 1)
                for part in range(2):
                    act.wait_ge(S["turned"], 2 * c + part + 1)
                    act.wait_ge(S["stored_hi"], 16 * c)
                    act.activation(t_hi[:, part * 512:(part + 1) * 512], turn_bank[part], ACT.Copy).then_inc(
                        S["hi_done"], 1)
                for part, done, stored, src in ((0, "hi_done", "stored_hi", t_hi), (1, "lo_done", "stored_lo", t_lo)):
                    act.wait_ge(S[done], 2 * c + 2)
                    act.dma_start(out_dst[part, c], src[:].bitcast(F32).rearrange("p (m t) -> p m t", t=P)).then_inc(
                        S[stored], 16)

            def both(c, s, more):
                if more:
                    first(c + 1, 1 - s)
                second(c, s)

            steps(act, nothing, lambda: first(0, 0), both)
            act.wait_ge(S["stored_hi"], 16 * LAT_TILES)
            act.wait_ge(S["stored_lo"], 16 * LAT_TILES)

        @block.vector
        def _(dve):
            dve.wait_ge(S["consts"], 32)

            def advance(n):
                dve.wait_ge(S["state_sum"], n + 1)
                if isinstance(n, int) and n == 0:
                    dve.tensor_copy(state[:], ps_state[:]).then_inc(S["state_done"], 1)
                    return
                dve.wait_ge(S["decay_done"], n)
                dve.tensor_tensor(state[:], decayed[:], ps_state[:], ALU.add).then_inc(S["state_done"], 1)

            def mask(c):
                dve.wait_ge(S["cb_done"], c + 1)
                dve.wait_ge(S["w_done"], c)
                for d in range(2):
                    dve.tensor_tensor(cb[:, d], ps_cb[:, 0:GROUPS * P].rearrange("p (g t) -> p g t", t=P),
                                      bcast(masks[:, d], [(0, GROUPS), (1, P)]), ALU.mult).then_inc(S["cb_masked"], 1)

            def weights(c, s):
                dve.wait_ge(S["cb_masked"], 2 * c + 2)
                for h in range(SSD_HEADS):
                    dve.wait_ge(S["w_b"], SSD_HEADS * c + h + 1)
                    dve.scalar_tensor_tensor(w[:, s, h], cb[:, 0, h // HEADS_PER_GROUP],
                                             f.dt[:, c + CTX_TILES, h:h + 1], w[:, s, h], ALU.mult,
                                             ALU.add).then_inc(S["w_sum"], 1)
                dve.wait_ge(S["diff_f"], c + 1)
                dve.wait_ge(S["diff_b"], c + 1)
                dve.tensor_tensor(sums_f[:, s], sums_f[:, s], sums_b[:, s], ALU.min).then_inc(S["least"], 1)

            def finish_w(c, s):
                dve.wait_ge(S["w_exp"], c + 1)
                dve.wait_ge(S["w_sum"], SSD_HEADS * (c + 1))
                dve.tensor_tensor(w[:, s], w[:, s], sums_f[:, s], ALU.mult).then_inc(S["w_done"], 1)

            def first():
                mask(0)
                weights(0, 0)
                finish_w(0, 0)

            def both(c, s, more):
                n = c + CTX_TILES
                dve.wait_ge(S["y_off"], c + 1)
                dve.wait_ge(S["squared"], c)
                dve.wait_ge(S["turned"], 2 * c)
                for g in range(GROUPS):
                    cut = slice(g * GW, (g + 1) * GW)
                    dve.tensor_tensor(by_head(y[:, cut]), by_head(ps_off[:, cut]), spread(f.e_cs, n, 0, g),
                                      ALU.mult).then_inc(S["y_a"], 1)
                advance(n)
                if more:
                    mask(c + 1)
                    weights(c + 1, 1 - s)
                dve.wait_ge(S["y_diag"], c + 1)
                dve.wait_ge(S["y_a"], 2 * c + 2)
                dve.tensor_tensor(y[:], y[:], ps_y[:], ALU.add).then_inc(S["y_b"], 1)
                dve.wait_ge(S["skip_done"], c + 1)
                dve.wait_ge(S["y_b"], c + 1)
                dve.tensor_tensor(y[:], y[:], skip_x[:, s], ALU.add).then_inc(S["y_c"], 1)
                dve.wait_ge(S["y_c"], c + 1)
                dve.wait_ge(landed[s], 32 + 32 * (c - s) + 64)
                dve.tensor_tensor(y[:], y[:], z[:, s], ALU.mult).then_inc(S["y_gated"], 1)
                if more:
                    finish_w(c + 1, 1 - s)
                for part in range(2):
                    dve.wait_ge(S["hi_done"], 2 * c + part + 1)
                    dve.wait_ge(S["stored_lo"], 16 * c)
                    cut = slice(part * 512, (part + 1) * 512)
                    dve.tensor_tensor(t_lo[:, cut], turn_bank[part], t_hi[:, cut].bitcast(F32),
                                      ALU.subtract).then_inc(S["lo_done"], 1)

            steps(dve, lambda c, n, s: advance(n), first, both)


def stage_attention(nc, sem, io, keep, dram):
    HEADS_Q = Q_PER_KV * P
    GROUPS_ALL = LAT_TILES * N_KV
    CHUNKS = [(0, 1024), (1024, 1024), (2048, TOK - 2048)]
    N_CH = Q_PER_KV * len(CHUNKS)
    POOL_TILES = 12
    SHIFT_ROW, ODD = HEAD_DIM, HEAD_DIM
    FOLD_AT, SHIFT_AT = 1, 13
    with ExitStack() as ctx:
        def sb(name, shape, dt=F32):
            return ctx.enter_context(nc.sbuf_tensor("at_" + name, shape, dt))

        k_hi = sb("k_hi", [P, N_KV, TOK], F32R)
        k_lo = sb("k_lo", [P, N_KV, TOK], F32R)
        v = sb("v", [P, TILES, N_KV * HEAD_DIM])
        q = sb("q", [P, N_KV, Q_PER_KV, P], F32R)
        q_shift = sb("q_shift", [P, N_KV, Q_PER_KV, P], F32R)
        gate = sb("gate", [P, 2, 2, P])
        prob = sb("prob", [P, 2, TILES, HEADS_Q])
        top, neg_top = sb("top", [P, Q_PER_KV, len(CHUNKS)]), sb("neg_top", [P, Q_PER_KV])
        diag = sb("diag", [P, Q_PER_KV, P], F32R)
        sum_pool, sum_dve = sb("sum_pool", [P, 2 * HEADS_Q]), sb("sum_dve", [P, 2 * HEADS_Q])
        sum_all = sb("sum_all", [P, HEADS_Q])
        folded_pool, halves = sb("folded_pool", [P, HEADS_Q]), sb("halves", [P, HEADS_Q])
        fold, ones, ones_r = sb("fold", [P, HEAD_DIM]), sb("ones", [P, P]), sb("ones_r", [P, P], F32R)
        from_fold = sb("from_fold", [P, HEADS_Q])
        gated, recip = sb("gated", [P, 2 * P]), sb("recip", [P, 2 * P])
        o_hi, o_lo = sb("o_hi", [P, 2, 2 * P], F32R), sb("o_lo", [P, 2, 2 * P], F32R)
        ps_max = ctx.enter_context(nc.psum_tensor("at_ps_max", [P, 2 * 1024], F32))
        ps_s = ctx.enter_context(nc.psum_tensor("at_ps_s", [P, 2 * HEADS_Q], F32))
        ps_o = ctx.enter_context(nc.psum_tensor("at_ps_o", [P, HEADS_Q], F32))
        ps_x = ctx.enter_context(nc.psum_tensor("at_ps_x", [P, HEADS_Q], F32))
        names = ("v_landed", "ones_row", "shift_blank", "consts", "max_scored", "chunk_top", "top_done", "diag_done",
                 "spread_done",
                 "shift_done", "scored", "exp_done", "pv_done", "halves_done", "pool_added", "pool_sum", "dve_added",
                 "sum_done", "folded", "read_fold", "recip_done", "gated_done", "o32_done", "hi_done", "lo_done")
        (v_landed, ones_row, shift_blank, consts, max_scored, chunk_top, top_done, diag_done, spread_done,
         shift_done, scored,
         exp_done, pv_done, halves_done, pool_added, pool_sum, dve_added, sum_done, folded,
         read_fold, recip_done, gated_done, o32_done, hi_done, lo_done) = [sem("at_" + x) for x in names]
        q_landed = [sem(f"at_q_landed{s}") for s in range(N_KV)]
        k_landed = [sem(f"at_k_landed{g}") for g in range(N_KV)]
        gate_landed = [sem(f"at_gate_landed{s}") for s in range(2)]
        stored = [sem(f"at_stored{s}") for s in range(2)]
        q_src = dram["q"].rearrange("s (g r) d (n t) -> s n g d r t", r=Q_PER_KV, t=P)
        gate_src = dram["gate"].rearrange("(g j) p (n t) -> n g p j t", j=2, t=P)
        o_dst = dram["ya"].rearrange("s (g j) p (n t) -> s n g p j t", j=2, t=P)
        block = ctx.enter_context(nc.Block())

        class Step:

            def __init__(self, n, g, counter=None):
                self.n, self.g, self.m, self.counter = n, g, n * N_KV + g, counter
                known = isinstance(n, int)
                self.maxima = not known or self.m + 2 < GROUPS_ALL
                self.shift = not known or -1 <= self.m and self.m + 1 < GROUPS_ALL
                self.scores = not known or 0 <= self.m < GROUPS_ALL
                self.pv = not known or 1 <= self.m <= GROUPS_ALL
                self.fold = not known or 2 <= self.m <= GROUPS_ALL + 1
                self.s = g % 2

            def at(self, d):
                return self.n + (self.g + d) // N_KV, (self.g + d) % N_KV

            def of(self, x, d):
                ahead, g = divmod(self.g + d, N_KV)
                return x[self.n + ahead, g] if self.counter is None else x[1 + ahead:][self.counter, g]

            def later(self, m):
                return not isinstance(self.n, int) or self.m >= m

        def steps(eng, body):
            for g in range(-2, N_KV):
                body(Step(0, g))
            with eng.Fori(0, LAT_TILES - 2) as before:
                for g in range(N_KV):
                    body(Step(before + 1, g, before))
            for g in range(N_KV + 2):
                body(Step(LAT_TILES - 1, g))

        @block.sync
        def _(sync):
            def load_q(st, d):
                g = (st.g + d) % N_KV
                for dst, part in ((q[0:HEAD_DIM], 0), (q[HEAD_DIM:P], 1), (q_shift[0:HEAD_DIM], 0)):
                    sync.dma_start(dst[:, g].bitcast(F32), st.of(q_src[part], d)).then_inc(q_landed[g], 16)

            def load_k(g):
                for dst, part in ((k_hi[0:HEAD_DIM], 0), (k_hi[HEAD_DIM:P], 0), (k_lo[0:HEAD_DIM], 1)):
                    sync.dma_start(dst[:, g].bitcast(F32), dram["k"][part, g]).then_inc(k_landed[g], 16)

            load_q(Step(0, -2), 2)
            load_k(0)

            def body(st):
                if isinstance(st.n, int) and st.m + 3 < N_KV:
                    load_k(st.m + 3)
                if isinstance(st.n, int) and st.m == -1:
                    sync.dma_start(v[:], dram["v"].rearrange("t p c -> p t c")).then_inc(v_landed, 16)
                if not isinstance(st.n, int) or st.m + 3 < GROUPS_ALL:
                    if st.later(1):
                        sync.wait_ge(scored, TILES * st.m)
                    load_q(st, 3)
                if st.pv:
                    if st.later(3):
                        sync.wait_ge(gated_done, st.m - 2)
                    sync.dma_start(gate[:, 1 - st.s], st.of(gate_src, -1)).then_inc(
                        gate_landed[1 - st.s], 16)
                if st.fold:
                    for part, done, src in ((0, hi_done, o_hi), (1, lo_done, o_lo)):
                        sync.wait_ge(done, st.m - 1)
                        sync.dma_start(st.of(o_dst[part], -2), src[:, st.s].bitcast(F32).rearrange(
                            "p (j t) -> p j t", t=P)).then_inc(stored[st.s], 16)

            steps(sync, body)
            for s in range(2):
                sync.wait_ge(stored[s], 16 * GROUPS_ALL)

        @block.gpsimd
        def _(pool):
            pool.memset(q_shift[HEAD_DIM:P].bitcast(F32), 0.0).then_inc(shift_blank, 1)
            pool.wait_ge(shift_blank, 1)
            for g in range(N_KV):
                if g:
                    pool.wait_ge(ones_row, 2 * g)
                pool.memset(k_lo[HEAD_DIM:P, g].bitcast(F32), 0.0).then_inc(ones_row, 1)
                pool.wait_ge(ones_row, 2 * g + 1)
                pool.memset(k_lo[SHIFT_ROW:SHIFT_ROW + 1, g].bitcast(F32), 1.0).then_inc(ones_row, 1)
            pool.wait_ge(ones_row, 2 * N_KV)

            def divide_and_gate(st):
                m = st.m - 2
                pool.wait_ge(read_fold, m + 1)
                pool.wait_ge(gate_landed[st.s], 16 * (st.n * 2 + st.g // 2))
                if st.later(3):
                    pool.wait_ge(lo_done, m)
                pool.tensor_tensor(gated[:], from_fold[:, 0:2 * P], gate[:, st.s].rearrange("p j t -> p (j t)"),
                                   ALU.mult).then_inc(gated_done, 1)
                pool.wait_ge(recip_done, m + 1)
                pool.wait_ge(gated_done, m + 1)
                pool.tensor_tensor(gated[:], gated[:], recip[:], ALU.mult).then_inc(o32_done, 1)

            def body(st):
                if st.fold and not st.scores:
                    divide_and_gate(st)
                if not st.scores:
                    return
                p = prob[:, st.s].rearrange("p t c -> p (t c)")
                W, adds = 2 * HEADS_Q, POOL_TILES // 2 - 1
                for a in range(adds):
                    pool.wait_ge(exp_done, TILES * st.m + 2 * a + 4)
                    if a or st.later(1):
                        pool.wait_ge(pool_added, adds * st.m + a)
                    if a == 0 and st.later(1):
                        pool.wait_ge(pool_sum, st.m)
                    left = p[:, 0:W] if a == 0 else sum_pool[:]
                    pool.tensor_tensor(sum_pool[:], left, p[:, (a + 1) * W:(a + 2) * W], ALU.add).then_inc(
                        pool_added, 1)
                    if a == 0 and st.fold:
                        divide_and_gate(st)
                pool.wait_ge(pool_added, adds * (st.m + 1))
                if st.later(1):
                    pool.wait_ge(sum_done, st.m)
                pool.tensor_tensor(folded_pool[:], sum_pool[:, 0:HEADS_Q], sum_pool[:, HEADS_Q:W],
                                   ALU.add).then_inc(pool_sum, 1)

            steps(pool, body)

        @block.tensor
        def _(pe):
            pe.wait_ge(shift_blank, 1)
            pe.wait_ge(consts, 3)

            def score(st, u):
                if u == 0:
                    if isinstance(st.n, int) and st.m < N_KV:
                        pe.wait_ge(ones_row, 2 * (st.m + 1))
                    pe.wait_ge(shift_done, st.m + 1)
                if st.later(1) or u >= 2:
                    pe.wait_ge(exp_done, TILES * st.m + u - 1)
                bank = ps_s[:, (u % 2) * HEADS_Q:(u % 2 + 1) * HEADS_Q]
                for k, x, first in ((k_hi, q, True), (k_lo, q_shift, False)):
                    last = pe.matmul(bank, k[:, st.g, u * P:(u + 1) * P], x[:, st.g].rearrange("p r t -> p (r t)"),
                                     start=first, stop=not first)
                last.then_inc(scored, 1)

            def score_for_max(st, c):
                g = (st.g + 2) % N_KV
                key, width = CHUNKS[c % len(CHUNKS)]
                if c == 0:
                    if isinstance(st.n, int) and st.m + 2 < N_KV:
                        pe.wait_ge(k_landed[g], 3 * 16)
                    pe.wait_ge(q_landed[g], 48 * (st.at(2)[0] + 1))
                if st.later(-1) or c >= 2:
                    pe.wait_ge(chunk_top, N_CH * (st.m + 2) + c - 1)
                for at in range(0, width, 512):
                    w = min(512, width - at)
                    to = (c % 2) * 1024 + at
                    last = pe.matmul(ps_max[:, to:to + w], q[:, g, c // len(CHUNKS)],
                                     k_hi[:, g, key + at:key + at + w], start=True, stop=True)
                last.then_inc(max_scored, 1)

            def spread_shift(st):
                pe.wait_ge(diag_done, st.m + 2)
                if st.fold:
                    pe.wait_ge(read_fold, st.m - 1)
                pe.matmul(ps_x[:], ones_r[:], diag[:].rearrange("p r t -> p (r t)"), start=True,
                          stop=True).then_inc(spread_done, 1)

            def add_values(st, u):
                g, s = (st.g - 1) % N_KV, 1 - st.s
                if u == 1:
                    if isinstance(st.n, int) and st.m == 1:
                        pe.wait_ge(v_landed, 16)
                    pe.wait_ge(exp_done, TILES * st.m)
                    if st.fold:
                        pe.wait_ge(halves_done, st.m - 1)
                for odd in range(2):
                    last = pe.matmul(ps_o[odd * ODD:odd * ODD + HEAD_DIM, :],
                                     v[:, u - 1 + odd, g * HEAD_DIM:(g + 1) * HEAD_DIM], prob[:, s, u - 1 + odd],
                                     start=(u == 1), stop=(u == TILES - 1))
                if u == TILES - 1:
                    last.then_inc(pv_done, 1)

            def fold_group(st):
                pe.wait_ge(halves_done, st.m - 1)
                pe.wait_ge(sum_done, st.m - 1)
                if st.scores:
                    pe.wait_ge(shift_done, st.m + 1)
                else:
                    pe.wait_ge(read_fold, st.m - 2)
                for what, rhs in ((fold[:], halves), (ones[:, 0:HEAD_DIM], sum_all)):
                    for h in range(Q_PER_KV):
                        rows = slice((h % 2) * ODD, (h % 2) * ODD + HEAD_DIM)
                        at = (rhs is sum_all) * 2 * P + (h // 2) * P
                        last = pe.matmul(ps_x[rows, at:at + P], what, rhs[:, h * P:(h + 1) * P],
                                         start=True, stop=True)
                last.then_inc(folded, 1)

            def body(st):
                for u in range(TILES):
                    if st.scores:
                        score(st, u)
                    if st.maxima and u % 3 != 2:
                        score_for_max(st, 2 * (u // 3) + u % 3)
                    if st.pv and u % 2:
                        add_values(st, u)
                    if st.fold and u == FOLD_AT:
                        fold_group(st)
                    if st.shift and u == SHIFT_AT:
                        spread_shift(st)

            steps(pe, body)

        @block.scalar
        def _(act):
            def body(st):
                if st.fold:
                    act.wait_ge(pv_done, st.m - 1)
                    if st.later(3):
                        act.wait_ge(folded, st.m - 2)
                    act.activation(halves[:], ps_o[:], ACT.Copy).then_inc(halves_done, 1)
                    if st.scores:
                        act.wait_ge(sum_done, st.m - 1)
                for u in range(TILES):
                    if st.scores:
                        act.wait_ge(scored, TILES * st.m + u + 1)
                        act.activation(prob[:, st.s, u], ps_s[:, (u % 2) * HEADS_Q:(u % 2 + 1) * HEADS_Q],
                                       ACT.Exp).then_inc(exp_done, 1)
                    if st.fold and u == FOLD_AT + 1:
                        act.wait_ge(folded, st.m - 1)
                        if st.later(3):
                            act.wait_ge(o32_done, st.m - 2)
                            act.wait_ge(recip_done, st.m - 2)
                        act.activation(from_fold[:], ps_x[:], ACT.Copy).then_inc(read_fold, 1)
                    if st.shift and u == SHIFT_AT + 1:
                        row = slice(SHIFT_ROW, SHIFT_ROW + 1)
                        act.wait_ge(spread_done, st.m + 2)
                        act.activation(q_shift[row, (st.g + 1) % N_KV].rearrange("p r t -> p (r t)"), ps_x[row],
                                       ACT.Copy).then_inc(shift_done, 1)

            steps(act, body)

        @block.vector
        def _(dve):
            dve.tensor_tensor(fold[:], keep["ident"][:, 0:HEAD_DIM], keep["ident"][:, HEAD_DIM:P],
                              ALU.add).then_inc(consts, 1)
            dve.memset(ones[:], 1.0).then_inc(consts, 1)
            dve.wait_ge(consts, 2)
            dve.tensor_copy(ones_r[:], ones[:]).then_inc(consts, 1)

            def chunk_max(st, c):
                r, x = c // len(CHUNKS), c % len(CHUNKS)
                dve.wait_ge(max_scored, N_CH * (st.m + 2) + c + 1)
                if c == 0 and st.later(-1):
                    dve.wait_ge(top_done, st.m + 2)
                to = (c % 2) * 1024
                dve.tensor_reduce(top[:, r, x:x + 1], ps_max[:, to:to + CHUNKS[x][1]], AX.X, ALU.max).then_inc(
                    chunk_top, 1)

            def query_maxima(st):
                dve.wait_ge(chunk_top, N_CH * (st.m + 2))
                if st.later(0):
                    dve.wait_ge(diag_done, st.m + 1)
                dve.tensor_reduce(neg_top[:], top[:], AX.X, ALU.max, negate=True).then_inc(top_done, 1)

            def shift_diagonals(st):
                dve.wait_ge(top_done, st.m + 2)
                if st.later(0):
                    dve.wait_ge(spread_done, st.m + 1)
                dve.tensor_tensor(diag[:], bcast(keep["ident"][:], [(0, Q_PER_KV), (1, P)]),
                                  bcast(neg_top[:], [(1, Q_PER_KV), (0, P)]), ALU.mult).then_inc(diag_done, 1)

            def first_sum(st):
                W, t0 = 2 * HEADS_Q, POOL_TILES
                dve.wait_ge(exp_done, TILES * st.m + t0 + 4)
                if st.later(1):
                    dve.wait_ge(sum_done, st.m)
                p = prob[:, st.s].rearrange("p t c -> p (t c)")[:, t0 * HEADS_Q:]
                dve.tensor_tensor(sum_dve[:], p[:, 0:W], p[:, W:2 * W], ALU.add).then_inc(dve_added, 1)

            def late_sum(st, part):
                W, t0 = 2 * HEADS_Q, POOL_TILES + 4
                p = prob[:, 1 - st.s].rearrange("p t c -> p (t c)")[:, t0 * HEADS_Q:]
                dve.wait_ge(dve_added, 3 * st.m - 2 + part)
                if part == 0:
                    dve.wait_ge(exp_done, TILES * st.m)
                    dve.tensor_tensor(sum_dve[:], sum_dve[:], p[:, 0:W], ALU.add).then_inc(dve_added, 1)
                elif part == 1:
                    dve.wait_ge(pool_sum, st.m)
                    dve.tensor_tensor(sum_dve[:, 0:HEADS_Q], sum_dve[:, 0:HEADS_Q], folded_pool[:],
                                      ALU.add).then_inc(dve_added, 1)
                else:
                    if st.later(2):
                        dve.wait_ge(folded, st.m - 1)
                    dve.tensor_tensor(sum_all[:], sum_dve[:, 0:HEADS_Q], sum_dve[:, HEADS_Q:W], ALU.add).then_inc(
                        sum_done, 1)

            def split_output(st, part):
                m = st.m - 2
                if part == 0:
                    dve.wait_ge(read_fold, m + 1)
                    if st.later(3):
                        dve.wait_ge(o32_done, m)
                    dve.reciprocal(recip[:], from_fold[:, 2 * P:4 * P]).then_inc(recip_done, 1)
                elif part == 1:
                    dve.wait_ge(o32_done, m + 1)
                    if st.later(4):
                        dve.wait_ge(stored[st.s], 16 * (st.m - st.s) - 32)
                    dve.tensor_copy(o_hi[:, st.s], gated[:]).then_inc(hi_done, 1)
                else:
                    dve.wait_ge(hi_done, m + 1)
                    dve.tensor_tensor(o_lo[:, st.s], gated[:], o_hi[:, st.s].bitcast(F32), ALU.subtract).then_inc(
                        lo_done, 1)

            def body(st):
                if st.shift:
                    query_maxima(st)
                for c in range(N_CH):
                    if st.maxima:
                        chunk_max(st, c)
                    if st.shift and c == 0:
                        shift_diagonals(st)
                    if st.pv and 1 <= c <= 3:
                        late_sum(st, c - 1)
                    if st.fold and c in (5, 8, 9):
                        split_output(st, (5, 8, 9).index(c))
                if st.scores:
                    first_sum(st)

            steps(dve, body)


def stage_out(nc, sem, io, keep, dram, out):
    K2, HALF = 2 * WIDTH // P, 512
    with ExitStack() as ctx:
        def sb(name, shape, dt=F32):
            return ctx.enter_context(nc.sbuf_tensor("ou_" + name, shape, dt))

        with nc.sbuf_tensor("ou_w_raw", [P, K2, D_MODEL], F32) as w_raw:
            pass
        w_lo = sb("w_lo", [P, K2, D_MODEL], F32R)
        w_hi = sb("w_hi", [P, K2, D_MODEL], F32R)
        SCALED = 3
        w_scaled_at = sb("w_scaled", [P, SCALED, D_MODEL])
        gate, final = sb("gate", [P, D_MODEL]), sb("final", [P, D_MODEL])
        yt = sb("yt", [P, 2, 2, K2, P], F32R)
        x, junk = sb("x", [P, 2, D_MODEL]), sb("junk", [P, D_MODEL])
        part, part2 = sb("part", [P, D_MODEL]), sb("part2", [P, D_MODEL])
        rms_y, rstd_y = sb("rms_y", [P, LAT_TILES]), sb("rstd_y", [P, LAT_TILES])
        ss, rms, rstd = sb("ss", [P, 1]), sb("rms", [P, 1]), sb("rstd", [P, 1])
        ps = [[ctx.enter_context(nc.psum_tensor(f"ou_ps{s}{h}", [P, 2 * HALF], F32)) for h in range(2)]
              for s in range(2)]
        names = ("consts", "w_scaled", "w_hi_done", "w_split_dve", "w_split_pool", "y_rms", "y_rstd", "attn_done",
                 "ssd_done", "part_done",
                 "mixed", "added", "squared", "rms_done", "rstd_done", "normed")
        (consts, w_scaled, w_hi_done, w_split_dve, w_split_pool, y_rms, y_rstd, attn_done, ssd_done, part_done,
         mixed, added, squared,
         rms_done, rstd_done, normed) = [sem("ou_" + a) for a in names]
        w_landed = [sem(f"ou_w_landed{s}") for s in range(K2)]
        landed = [sem(f"ou_landed{s}") for s in range(2)]
        stored = [sem(f"ou_stored{s}") for s in range(2)]
        w_src = io["w_out"].rearrange("o (k p) c -> (o k) p c", p=P)
        srcs = [dram[a].rearrange("s m p (n t) -> n s p m t", t=P) for a in ("ya", "ys")]
        x_src = io["x"].rearrange("o (n p) d -> (o n) p d", p=P)
        out_dst = out.rearrange("o (n p) d -> (o n) p d", p=P)
        block = ctx.enter_context(nc.Block())

        def tiles(eng, body):
            with eng.Fori(0, LAT_TILES - 1, 2) as i:
                for u in range(2):
                    body(i + u, u)

        def wait_split(eng, k):
            eng.wait_ge((w_split_dve, w_split_pool)[k % 2], k // 2 + 1)

        @block.sync
        def _(sync):
            def load(n, s):
                sync.wait_ge(stored[s], 8 * (n - s))
                for half, src in enumerate(srcs):
                    for a in range(2):
                        sync.dma_start(yt[:, s, a, half * KD:(half + 1) * KD].bitcast(F32), src[n, a]).then_inc(
                            landed[s], 16)
                sync.dma_start(x[:, s], x_src[n]).then_inc(landed[s], 16)

            sync.dma_start(gate[:], keep["gate_dram"].unsqueeze(0).broadcast_to([P, D_MODEL])).then_inc(consts, 16)
            for k in range(K2):
                sync.dma_start(w_raw[:, k], w_src[k]).then_inc(w_landed[k], 16)
                if k == 2:
                    load(0, 0)
            sync.dma_start(final[:], io["final_g"].unsqueeze(0).broadcast_to([P, D_MODEL])).then_inc(consts, 16)
            load(1, 1)
            with sync.Fori(2, LAT_TILES - 1, 2) as i:
                for u in range(2):
                    load(i + u, u)

        def low_half(eng, k, done):
            eng.wait_ge(w_hi_done, k + 1)
            eng.tensor_tensor(w_lo[:, k], w_scaled_at[:, k % SCALED], w_hi[:, k].bitcast(F32),
                              ALU.subtract).then_inc(done, 1)

        @block.gpsimd
        def _(pool):
            for k in range(1, K2, 2):
                low_half(pool, k, w_split_pool)

        @block.tensor
        def _(pe):
            pe.sem_inc(ssd_done, 2)

            def body(n, s):
                pe.wait_ge(landed[s], 40 * (n - s) + 80)
                pe.wait_ge(mixed, n + 1)
                for half in range(2):
                    for k in range(half * KD, (half + 1) * KD):
                        wait_split(pe, k)
                        for a, w in ((0, w_hi), (0, w_lo), (1, w_hi)):
                            for c in range(2):
                                last = pe.matmul(ps[s][half][:, c * HALF:(c + 1) * HALF], yt[:, s, a, k],
                                                 w[:, k, c * HALF:(c + 1) * HALF],
                                                 start=(k % KD == 0 and a == 0 and w is w_hi),
                                                 stop=(k % KD == KD - 1 and a == 1))
                    last.then_inc((attn_done, ssd_done)[half], 1)

            tiles(pe, body)

        @block.scalar
        def _(act):
            act.activation(rms_y[:], keep["ss_y"][:], ACT.Sqrt, scale=1.0 / WIDTH, bias=keep["eps"][:]).then_inc(
                y_rms, 1)
            for k in range(K2):
                act.wait_ge(w_scaled, k + 1)
                act.activation(w_hi[:, k], w_scaled_at[:, k % SCALED], ACT.Copy).then_inc(w_hi_done, 1)

            def body(n, s):
                act.wait_ge(attn_done, n + 1)
                act.wait_ge(mixed, n + 2)
                act.activation(part[:], ps[s][0][:], ACT.Copy).then_inc(part_done, 1)
                act.wait_ge(added, n + 3)
                act.wait_ge(squared, n)
                act.activation(junk[:], x[:, s], ACT.Square, accum_out=ss[:]).then_inc(squared, 1)
                act.wait_ge(squared, n + 1)
                act.wait_ge(rstd_done, n)
                act.activation(rms[:], ss[:], ACT.Sqrt, scale=1.0 / D_MODEL, bias=keep["eps"][:]).then_inc(
                    rms_done, 1)
                act.wait_ge(normed, n + 1)
                act.dma_start(out_dst[n], x[:, s]).then_inc(stored[s], 16)

            tiles(act, body)
            for s in range(2):
                act.wait_ge(stored[s], 16 * LAT_TILES // 2)

        @block.vector
        def _(dve):
            dve.sem_inc(mixed, 2)
            dve.sem_inc(added, 2)
            dve.wait_ge(consts, 16)
            for k in range(K2):
                dve.wait_ge(w_landed[k], 16)
                raw, scaled = w_raw[:, k], w_scaled_at[:, k % SCALED]
                if k >= SCALED:
                    wait_split(dve, k - SCALED)
                if k < KD:
                    dve.tensor_tensor(scaled, raw, gate[:], ALU.mult).then_inc(w_scaled, 1)
                else:
                    row = ROW_SSDG + k - KD
                    dve.scalar_tensor_tensor(scaled, raw, keep["cols"][:, row:row + 1], gate[:], ALU.mult,
                                             ALU.mult).then_inc(w_scaled, 1)
                if k % 2:
                    low_half(dve, k - 1, w_split_dve)
            dve.wait_ge(consts, 32)
            dve.wait_ge(y_rms, 1)
            dve.reciprocal(rstd_y[:], rms_y[:]).then_inc(y_rstd, 1)
            dve.wait_ge(y_rstd, 1)

            def body(n, s):
                dve.wait_ge(part_done, n + 1)
                dve.wait_ge(ssd_done, n + 3)
                dve.wait_ge(added, n + 2)
                dve.scalar_tensor_tensor(part2[:], ps[s][1][:], rstd_y[:, bass.ds(n, 1)], part[:], ALU.mult,
                                         ALU.add).then_inc(mixed, 1)
                dve.wait_ge(mixed, n + 3)
                dve.wait_ge(landed[s], 40 * (n - s) + 80)
                dve.tensor_tensor(x[:, s], x[:, s], part2[:], ALU.add).then_inc(added, 1)
                dve.wait_ge(rms_done, n + 1)
                dve.reciprocal(rstd[:], rms[:]).then_inc(rstd_done, 1)
                dve.wait_ge(rstd_done, n + 1)
                dve.scalar_tensor_tensor(x[:, s], x[:, s], rstd[:], final[:], ALU.mult, ALU.mult).then_inc(normed, 1)

            tiles(dve, body)


def build(nc, io, out):
    with ExitStack() as ctx:
        made = []

        def sem(name):
            made.append(nc.alloc_semaphore(name=name))
            return made[-1]

        def reuse_semaphores():
            nc.clear_and_free_semaphores(made)
            made.clear()
            nc.all_engine_barrier()

        def sb(name, shape, dt=F32):
            return ctx.enter_context(nc.sbuf_tensor(name, shape, dt))

        def scratch(name, shape):
            return nc.dram_tensor(name, shape, F32).ap()

        NH = 2 * SSD_HEADS
        dram = {
            "xbc": scratch("xbc_t", [XBC_TILES, P, TOK]), "gate": scratch("gate_t", [WIDTH // P, P, SEQ]),
            "z": scratch("z_rows", [LAT_TILES, P, WIDTH]), "v": scratch("v_rows", [TILES, P, N_KV * HEAD_DIM]),
            "k": scratch("k_t", [2, N_KV, HEAD_DIM, TOK]), "q": scratch("q_t", [2, N_Q, HEAD_DIM, SEQ]),
            "cs": scratch("cs_rows", [NH, TOK]), "dtcols": scratch("dt_factors", [P, 5 * TILES * NH]),
            "x": scratch("x_rows", [TILES, P, WIDTH]), "b": scratch("b_rows", [TILES, P, GROUPS * D_STATE]),
            "yb": scratch("yb_rows", [LAT_TILES, P, WIDTH]),
            "ys": scratch("ys_t", [2, WIDTH // P, P, SEQ]), "ya": scratch("ya_t", [2, WIDTH // P, P, SEQ]),
        }
        keep = {"ident": sb("ident", [P, P]), "cols": sb("cols", [P, P]), "shift": sb("shift", [P, 2, KD]),
                "scale": sb("scale", [P, 2, KD]), "eps": sb("eps", [P, 1]), "one": sb("one", [P, 1]),
                "pick": sb("pick", [P, 2, P]), "ss_y": sb("ss_y", [P, LAT_TILES]),
                "gate_dram": scratch("gate_vec", [D_MODEL])}
        with ExitStack() as hs:
            with nc.sbuf_tensor("ada", [P, ADA_CHUNKS, KD, ADA_W], F32) as ada:
                pass
            h_hi = hs.enter_context(nc.sbuf_tensor("h_hi", [P, KD, TOK], F32R))
            h_lo = hs.enter_context(nc.sbuf_tensor("h_lo", [P, KD, TOK], F32R))
            stage_hidden(nc, sem, io, keep, ada, h_hi, h_lo)
            stage_dt(nc, sem, io, keep, h_hi, h_lo, dram)
            stage_channels(nc, sem, io, keep, h_hi, h_lo, dram)
            w_in = io["w_in"].rearrange("o (k p) c -> p (o k) c", p=P)
            lat, every = list(range(CTX_TILES, TILES)), list(range(TILES))
            n_blocks = WIDTH // COLS_W
            w_q = w_in[:, :, OFF_Q:OFF_Q + WIDTH + COLS_W].rearrange("p k (b c) -> p b k c", c=COLS_W)
            w_z = w_in[:, :, OFF_Z - COLS_W:OFF_Z + WIDTH].rearrange("p k (b c) -> p b k c", c=COLS_W)
            k_dst = dram["k"].rearrange("s (j g) d t -> s (g d) j t", g=2)
            q_dst = dram["q"].rearrange("s (b j g) d (n t) -> s b n (g d) j t", j=HPB // 2, g=2, t=P)
            z_dst = dram["z"].rearrange("n p (b c) -> n b p c", c=COLS_W)
            weights = Weights(sem, lambda name, shape, dt=F32: hs.enter_context(nc.sbuf_tensor(name, shape, dt)))
            v_at, q_at = 1, 2
            z_at = q_at + n_blocks + 1
            stage_heads(nc, sem, io, keep, h_hi, h_lo, "k_", weights, 0, lambda b: w_in[:, :, 0:COLS_W], 1, every,
                        w_in[:, :, COLS_W:2 * COLS_W], "k_norm_g", 1.0,
                        lambda s, b, i: k_dst[s, :, :, i * P:(i + 1) * P])
            stage_plain(nc, sem, h_hi, h_lo, "v_", weights, v_at, None, 1, every, w_q[:, 0],
                        ACT.Copy, lambda b, i: dram["v"][i])
            stage_heads(nc, sem, io, keep, h_hi, h_lo, "q_", weights, q_at, lambda b: w_q[:, b], n_blocks, lat,
                        w_z[:, n_blocks], "q_norm_g", HEAD_DIM ** -0.5, lambda s, b, i: q_dst[s, b, i])
            stage_plain(nc, sem, h_hi, h_lo, "z_", weights, z_at, lambda b: w_z[:, b * -1 + n_blocks], n_blocks, lat,
                        None, ACT.Silu, lambda b, i: z_dst[i, b * -1 + (n_blocks - 1)])
        reuse_semaphores()
        with ExitStack() as ss:
            cols = ss.enter_context(nc.sbuf_tensor("ssd_cols", [P, 5, TILES, NH], F32))
            stage_ssd_backward(nc, sem, io, keep, dram, cols)
            stage_ssd_forward(nc, sem, io, keep, dram, cols)
        reuse_semaphores()
        stage_attention(nc, sem, io, keep, dram)
        stage_out(nc, sem, io, keep, dram, out)


def constants():
    ident = np.eye(P, dtype=np.float32)
    s, l = np.arange(P)[:, None], np.arange(P)[None]
    pick = np.zeros((2, P, P), np.float32)
    pick[0, P - 1], pick[1, 0] = 1, 1
    masks = np.stack([s <= l, s >= l]).astype(np.float32)
    nf = HEAD_DIM // 4
    t = np.arange(SEQ)
    freq = (10000.0 ** (-np.arange(nf, dtype=np.float32) / np.float32(nf))).astype(np.float32)
    pos = np.stack([t // GRID_W, t % GRID_W], 1).astype(np.float32)
    ang = pos[:, :, None] * freq
    rope = np.zeros((2, TOK, 2, 2, nf), np.float32)
    rope[0] = 1
    rope[0, CTX:] = np.cos(ang)[:, :, None]
    rope[1, CTX:] = np.sin(ang)[:, :, None] * np.array([-1, 1], np.float32)[None, None, :, None]
    rope = rope.reshape(2, TILES, P, HEAD_DIM).transpose(2, 0, 1, 3)
    return {"ident": ident, "pick": pick.transpose(1, 0, 2), "masks": masks.transpose(1, 0, 2), "rope": rope}


_INPUTS = ["x", "c", "ctx", "c_ctx", "ada_w", "ada_b", "norm_g", "w_in", "conv_w", "conv_b", "dt_bias", "a_log",
           "d_skip", "q_norm_g", "k_norm_g", "ssd_norm_g", "w_out", "final_g"]


def kernel(**inputs):
    import numpy as _np
    import concourse.bacc as _bacc
    from concourse import mybir as _mybir
    from concourse.bass_utils import run_bass_kernel_spmd as _run

    nc = _bacc.Bacc("TRN2", target_bir_lowering=False, num_devices=1)
    given = {name: inputs[name] for name in _INPUTS}
    given.update(constants())
    arrays, io = {}, {}
    for name, value in given.items():
        a = _np.ascontiguousarray(value)
        arrays[f"in_{name}_dram"] = a
        io[name] = nc.dram_tensor(f"in_{name}_dram", a.shape, _mybir.dt.from_np(a.dtype), kind="ExternalInput").ap()
    out = nc.dram_tensor("out_0_dram", (1, SEQ, D_MODEL), F32, kind="ExternalOutput").ap()
    build(nc, io, out)
    r = _run(nc, [arrays], core_ids=[0])
    return r.results[0]["out_0_dram"]
```
